# Optimizing a Trainium2 kernel written in Bass

```python
import math
import jax, jax.numpy as jnp
from jax import lax
import numpy as np

D_MODEL = 1024
BATCH = 1
SEQ = 512
DEPTH = 2

CHUNK = 64
Q_BLOCK = 128
N_A_LAYERS = DEPTH // 2
N_B_LAYERS = DEPTH - N_A_LAYERS
A_HEADS = 8
A_HEAD_DIM = D_MODEL // (2 * A_HEADS)
B_HEADS = 16
B_HEAD_DIM = D_MODEL // B_HEADS
LEFT_CHUNKS = 8
BAND_CHUNKS = LEFT_CHUNKS + 1
MAX_REL_DIST = 256
D_FF = -(-8 * D_MODEL // (3 * 256)) * 256
ROPE_THETA = 10000.0
LN_EPS = 1e-5
SUBLN_EPS = 1e-5
DEEPNORM_ALPHA = (2 * DEPTH) ** 0.25
DEEPNORM_BETA = (8 * DEPTH) ** -0.25


def layer_norm(x, g, b):
    xf = x.astype(jnp.float32)
    mu = jnp.mean(xf, axis=-1, keepdims=True)
    var = jnp.mean(jnp.square(xf - mu), axis=-1, keepdims=True)
    y = (xf - mu) * lax.rsqrt(var + LN_EPS) * g.astype(jnp.float32) + b.astype(jnp.float32)
    return y.astype(x.dtype)

def rms_norm(x, g):
    xf = x.astype(jnp.float32)
    y = xf * lax.rsqrt(jnp.mean(jnp.square(xf), axis=-1, keepdims=True) + SUBLN_EPS)
    return (y * g.astype(jnp.float32)).astype(x.dtype)

def rope_tables(seq, dim):
    inv = ROPE_THETA ** (-jnp.arange(0, dim, 2, dtype=jnp.float32) / dim)
    ang = jnp.arange(seq, dtype=jnp.float32)[:, None] * inv[None, :]
    return jnp.cos(ang), jnp.sin(ang)

def apply_rope(x, cos, sin):
    half = x.shape[-1] // 2
    x1, x2 = x[..., :half], x[..., half:]
    cos = cos.astype(x.dtype)
    sin = sin.astype(x.dtype)
    return jnp.concatenate([x1 * cos - x2 * sin, x1 * sin + x2 * cos], axis=-1)

def lambda_init_fn(layer_idx):
    return 0.8 - 0.6 * math.exp(-0.3 * layer_idx)

def diff_attention(x, w_qkv, lam_params, subln_g, w_o, lambda_init):
    b, s, _ = x.shape
    qkv = x @ w_qkv
    q, k, v = jnp.split(qkv, 3, axis=-1)
    q = q.reshape(b, s, A_HEADS, 2, A_HEAD_DIM)
    k = k.reshape(b, s, A_HEADS, 2, A_HEAD_DIM)
    v = v.reshape(b, s, A_HEADS, 2 * A_HEAD_DIM)
    cos, sin = rope_tables(s, A_HEAD_DIM)
    cos = cos[:, None, None, :]
    sin = sin[:, None, None, :]
    q = apply_rope(q, cos, sin) * (A_HEAD_DIM ** -0.5)
    k = apply_rope(k, cos, sin)
    lp = lam_params.astype(jnp.float32)
    lam = jnp.exp(jnp.sum(lp[0] * lp[1])) - jnp.exp(jnp.sum(lp[2] * lp[3])) + lambda_init
    chunk_id = jnp.arange(s) // CHUNK
    neg = jnp.finfo(jnp.float32).min
    outs = []
    for i in range(s // Q_BLOCK):
        q0 = i * Q_BLOCK
        kend = q0 + Q_BLOCK
        sc = jnp.einsum('bqhmd,bkhmd->bhmqk', q[:, q0:kend], k[:, :kend],
                        preferred_element_type=jnp.float32)
        allowed = chunk_id[None, :kend] <= chunk_id[q0:kend, None]
        p = jax.nn.softmax(jnp.where(allowed, sc, neg), axis=-1)
        a = p[:, :, 0] - lam * p[:, :, 1]
        outs.append(jnp.einsum('bhqk,bkhe->bqhe', a.astype(v.dtype), v[:, :kend]))
    o = jnp.concatenate(outs, axis=1)
    o = rms_norm(o, subln_g) * (1.0 - lambda_init)
    return o.reshape(b, s, D_MODEL) @ w_o

def shared_kv_band(x, kv_w):
    b, s, _ = x.shape
    nc = s // CHUNK
    kv = x @ kv_w
    k, v = jnp.split(kv, 2, axis=-1)
    k = k.reshape(b, nc, CHUNK, B_HEADS, B_HEAD_DIM)
    v = v.reshape(b, nc, CHUNK, B_HEADS, B_HEAD_DIM)
    pad = ((0, 0), (LEFT_CHUNKS, 0), (0, 0), (0, 0), (0, 0))
    kp = jnp.pad(k, pad)
    vp = jnp.pad(v, pad)
    k_band = jnp.concatenate([kp[:, j:j + nc] for j in range(BAND_CHUNKS)], axis=2)
    v_band = jnp.concatenate([vp[:, j:j + nc] for j in range(BAND_CHUNKS)], axis=2)
    band_chunk = jnp.arange(BAND_CHUNKS * CHUNK) // CHUNK
    band_valid = (jnp.arange(nc)[:, None] - LEFT_CHUNKS + band_chunk[None, :]) >= 0
    return k_band, v_band, band_valid

def chunk_attention(x, k_band, v_band, band_valid, w_q, rel_table, w_o):
    b, s, _ = x.shape
    nc = s // CHUNK
    q = (x @ w_q).reshape(b, nc, CHUNK, B_HEADS, B_HEAD_DIM) * (B_HEAD_DIM ** -0.5)
    rel = (jnp.arange(BAND_CHUNKS * CHUNK)[None, :] - LEFT_CHUNKS * CHUNK
           - jnp.arange(CHUNK)[:, None])
    idx = jnp.clip(rel, -MAX_REL_DIST, MAX_REL_DIST) + MAX_REL_DIST
    bias = rel_table[:, idx].astype(jnp.float32)
    sc = jnp.einsum('bnqhd,bnkhd->bhnqk', q, k_band,
                    preferred_element_type=jnp.float32) + bias[:, None]
    sc = jnp.where(band_valid[:, None, :], sc, jnp.finfo(jnp.float32).min)
    p = jax.nn.softmax(sc, axis=-1)
    o = jnp.einsum('bhnqk,bnkhd->bnqhd', p.astype(v_band.dtype), v_band)
    return o.reshape(b, s, D_MODEL) @ w_o

def swiglu(x, w_in, w_out):
    gate, up = jnp.split(x @ w_in, 2, axis=-1)
    return (jax.nn.silu(gate) * up) @ w_out

def first_inputs(seed: int = 0) -> dict:
    key = jax.random.key(seed)
    ks = jax.random.split(key, 14)
    f32 = jnp.float32
    d = D_MODEL
    nrm = lambda k, shape, sc: jax.random.normal(k, shape, f32) * sc
    return {
        "x": nrm(ks[0], (BATCH, SEQ, d), 1.0),
        "a_w_qkv": nrm(ks[1], (N_A_LAYERS, d, 3 * d), d ** -0.5),
        "a_lambda": nrm(ks[2], (N_A_LAYERS, 4, A_HEAD_DIM), 0.1),
        "a_subln_g": 1.0 + nrm(ks[3], (N_A_LAYERS, 2 * A_HEAD_DIM), 0.02),
        "a_w_o": nrm(ks[4], (N_A_LAYERS, d, d), d ** -0.5 * DEEPNORM_BETA),
        "kv_w": nrm(ks[5], (d, 2 * d), d ** -0.5),
        "b_w_q": nrm(ks[6], (N_B_LAYERS, d, d), d ** -0.5),
        "b_rel_bias": nrm(ks[7], (N_B_LAYERS, B_HEADS, 2 * MAX_REL_DIST + 1), 0.2),
        "b_w_o": nrm(ks[8], (N_B_LAYERS, d, d), d ** -0.5 * DEEPNORM_BETA),
        "ln_g": 1.0 + nrm(ks[9], (DEPTH, 2, d), 0.02),
        "ln_b": nrm(ks[10], (DEPTH, 2, d), 0.02),
        "ffn_w_in": nrm(ks[11], (DEPTH, d, 2 * D_FF), d ** -0.5),
        "ffn_w_out": nrm(ks[12], (DEPTH, D_FF, d), D_FF ** -0.5 * DEEPNORM_BETA),
    }

def first_block(x, a_w_qkv, a_lambda, a_subln_g, a_w_o, kv_w, b_w_q, b_rel_bias, b_w_o,
              ln_g, ln_b, ffn_w_in, ffn_w_out):
    k_band = v_band = band_valid = None
    for l in range(DEPTH):
        if l < N_A_LAYERS:
            mix = diff_attention(x, a_w_qkv[l], a_lambda[l], a_subln_g[l], a_w_o[l],
                                 lambda_init_fn(l))
        else:
            if l == N_A_LAYERS:
                k_band, v_band, band_valid = shared_kv_band(x, kv_w)
            j = l - N_A_LAYERS
            mix = chunk_attention(x, k_band, v_band, band_valid, b_w_q[j], b_rel_bias[j], b_w_o[j])
        x = layer_norm(DEEPNORM_ALPHA * x + mix, ln_g[l, 0], ln_b[l, 0])
        x = layer_norm(DEEPNORM_ALPHA * x + swiglu(x, ffn_w_in[l], ffn_w_out[l]), ln_g[l, 1], ln_b[l, 1])
    return x


N_META = 16
EPS = 1e-6

HG_HEADS = 4
HG_DIM = 128
HG_WIDTH = HG_HEADS * HG_DIM
RET_HEADS = 4
RET_DK = 32
RET_DV = 64
RET_QK_WIDTH = RET_HEADS * RET_DK
RET_V_WIDTH = RET_HEADS * RET_DV
ROPE_BASE = 10000.0
LRU_WIDTH = 256
LRU_BLOCKS = 4
LRU_BLOCK = LRU_WIDTH // LRU_BLOCKS
LRU_CONV = 4
LRU_C = 8.0
D_MIX = HG_WIDTH + RET_V_WIDTH + LRU_WIDTH
IN_SIZES = (HG_WIDTH, HG_WIDTH, HG_WIDTH, HG_WIDTH,
            RET_QK_WIDTH, RET_QK_WIDTH, RET_V_WIDTH, RET_V_WIDTH,
            LRU_WIDTH, LRU_WIDTH)
IN_COLS = sum(IN_SIZES)
IN_SPLITS = tuple(int(s) for s in np.cumsum(IN_SIZES)[:-1])
D_FF_2 = 2816
FFN_CONV = 3


def rmsnorm(x, g):
    xf = x.astype(jnp.float32)
    y = xf * lax.rsqrt(jnp.mean(xf * xf, axis=-1, keepdims=True) + EPS)
    return (y * g.astype(jnp.float32)).astype(x.dtype)

def head_groupnorm(o, g):
    of = o.astype(jnp.float32)
    mu = jnp.mean(of, axis=-1, keepdims=True)
    var = jnp.mean(jnp.square(of - mu), axis=-1, keepdims=True)
    return ((of - mu) * lax.rsqrt(var + EPS) * g.astype(jnp.float32)).astype(o.dtype)

def causal_dwconv(x, w, b):
    width, ch = w.shape
    y = lax.conv_general_dilated(
        x, w[:, None, :].astype(x.dtype), window_strides=(1,), padding=[(width - 1, 0)],
        dimension_numbers=('NWC', 'WIO', 'NWC'), feature_group_count=ch)
    return y + b.astype(x.dtype)

def split_heads(a, n):
    bsz, t, _ = a.shape
    return a.reshape(bsz, t, n, -1).transpose(0, 2, 1, 3)

def merge_heads(a):
    bsz, h, t, d = a.shape
    return a.transpose(0, 2, 1, 3).reshape(bsz, t, h * d)

def to_chunks(a, pad):
    bsz, h, _, d = a.shape
    a = jnp.pad(a, ((0, 0), (0, 0), (pad, 0), (0, 0)))
    return a.reshape(bsz, h, -1, CHUNK, d).transpose(2, 0, 1, 3, 4)

def from_chunks(o, pad):
    n, bsz, h, c, d = o.shape
    return o.transpose(1, 2, 0, 3, 4).reshape(bsz, h, n * c, d)[:, :, pad:]

def hgrn2_chunked(q, k, v, log_f):
    bsz, h, t, dk = q.shape
    dv = v.shape[-1]
    pad = (-t) % CHUNK
    qc, kc, vc, gc = (to_chunks(a, pad) for a in (q, k, v, log_f))
    causal = jnp.tril(jnp.ones((CHUNK, CHUNK), dtype=bool))[:, :, None]

    def step(state, inp):
        qi, ki, vi, gi = inp
        b = jnp.cumsum(gi.astype(jnp.float32), axis=-2)
        diff = b[:, :, :, None, :] - b[:, :, None, :, :]
        decay = jnp.exp(jnp.where(causal, diff, -jnp.inf))
        scores = jnp.einsum('bhtd,bhtsd,bhsd->bhts', qi, decay, ki)
        o = jnp.einsum('bhts,bhse->bhte', scores, vi) + \
            jnp.einsum('bhtd,bhde->bhte', qi * jnp.exp(b), state)
        b_last = b[:, :, -1:, :]
        state = jnp.exp(b_last[:, :, 0, :])[..., None] * state + \
            jnp.einsum('bhsd,bhse->bhde', ki * jnp.exp(b_last - b), vi)
        return state, o

    s0 = jnp.zeros((bsz, h, dk, dv), jnp.float32)
    _, o = lax.scan(step, s0, (qc, kc, vc, gc))
    return from_chunks(o, pad)

def retention_chunked(q, k, v, log_gamma):
    bsz, h, t, dk = q.shape
    dv = v.shape[-1]
    pad = (-t) % CHUNK
    qc, kc, vc = (to_chunks(a, pad).transpose(1, 2, 0, 3, 4) for a in (q, k, v))
    idx = jnp.arange(CHUNK, dtype=jnp.float32)
    lg = log_gamma[:, None]
    rel = idx[:, None] - idx[None, :]
    dmat = jnp.where(rel >= 0, jnp.exp(lg[:, :, None] * jnp.maximum(rel, 0.0)), 0.0)
    scores = jnp.einsum('bhntd,bhnsd->bhnts', qc, kc) * dmat[None, :, None]
    intra = jnp.einsum('bhnts,bhnse->bhnte', scores, vc)
    w_state = jnp.exp(lg * (CHUNK - 1 - idx))
    kv = jnp.einsum('bhnsd,bhnse->nbhde', kc * w_state[None, :, None, :, None], vc)
    chunk_decay = jnp.exp(log_gamma * CHUNK)[None, :, None, None]

    def step(state, kv_n):
        return chunk_decay * state + kv_n, state

    _, r_prev = lax.scan(step, jnp.zeros((bsz, h, dk, dv), jnp.float32), kv)
    w_q = jnp.exp(lg * (idx + 1.0))
    inter = jnp.einsum('bhntd,nbhde->bhnte', qc * w_q[None, :, None, :, None], r_prev)
    o = (intra + inter).transpose(2, 0, 1, 3, 4)
    return from_chunks(o, pad)

def rope(x, cos, sin):
    x1, x2 = jnp.split(x, 2, axis=-1)
    return jnp.concatenate([x1 * cos - x2 * sin, x1 * sin + x2 * cos], axis=-1)

def rg_lru(x, gate_a_w, gate_a_b, gate_i_w, gate_i_b, lam):
    bsz, t, w = x.shape
    xb = x.reshape(bsz, t, LRU_BLOCKS, LRU_BLOCK)
    r = jax.nn.sigmoid(jnp.einsum('btnd,nde->btne', xb, gate_a_w).reshape(bsz, t, w) + gate_a_b)
    i = jax.nn.sigmoid(jnp.einsum('btnd,nde->btne', xb, gate_i_w).reshape(bsz, t, w) + gate_i_b)
    log_a = -LRU_C * r.astype(jnp.float32) * jax.nn.softplus(-lam.astype(jnp.float32))
    a = jnp.exp(log_a)
    u = jnp.sqrt(-jnp.expm1(2.0 * log_a)) * (i * x)

    def combine(c1, c2):
        a1, b1 = c1
        a2, b2 = c2
        return a1 * a2, a2 * b1 + b2

    _, hseq = lax.associative_scan(combine, (a, u), axis=1)
    return hseq.astype(x.dtype)

def hybrid_mixer(h, w_in, lb, hg_norm_g, ret_norm_g, lru_conv_w, lru_conv_b,
                 gate_a_w, gate_a_b, gate_i_w, gate_i_b, lru_lambda, w_out, cos, sin):
    proj = jnp.einsum('btd,dc->btc', h, w_in)
    hq, hf, hi, hg, rq, rk, rv, rg, lx, ly = jnp.split(proj, IN_SPLITS, axis=-1)

    z = hf.astype(jnp.float32)
    log_f = jnp.logaddexp(jnp.log(lb), jnp.log1p(-lb) + jax.nn.log_sigmoid(z))
    k_hg = (1.0 - lb) * jax.nn.sigmoid(-z)
    q_hg = jax.nn.silu(hq) * HG_DIM ** -0.5
    o_hg = hgrn2_chunked(split_heads(q_hg, HG_HEADS), split_heads(k_hg, HG_HEADS),
                         split_heads(hi, HG_HEADS), split_heads(log_f, HG_HEADS))
    o_hg = merge_heads(rmsnorm(o_hg, hg_norm_g)) * jax.nn.silu(hg)

    log_gamma = jnp.log1p(-jnp.exp2(-5.0 - jnp.arange(RET_HEADS, dtype=jnp.float32)))
    q_r = rope(split_heads(rq, RET_HEADS), cos, sin)
    k_r = rope(split_heads(rk, RET_HEADS), cos, sin) * RET_DK ** -0.5
    o_ret = retention_chunked(q_r, k_r, split_heads(rv, RET_HEADS), log_gamma)
    o_ret = merge_heads(head_groupnorm(o_ret, ret_norm_g)) * jax.nn.silu(rg)

    xc = causal_dwconv(lx, lru_conv_w, lru_conv_b)
    o_lru = rg_lru(xc, gate_a_w, gate_a_b, gate_i_w, gate_i_b, lru_lambda) * jax.nn.gelu(ly)

    merged = jnp.concatenate([o_hg, o_ret, o_lru], axis=-1)
    return jnp.einsum('btc,cd->btd', merged, w_out)

def conv_glu_ffn(h, w_up, conv_w, conv_b, w_down):
    u = causal_dwconv(jnp.einsum('btd,df->btf', h, w_up), conv_w, conv_b)
    gate, val = jnp.split(u, 2, axis=-1)
    return jnp.einsum('btf,fd->btd', jax.nn.silu(gate) * val, w_down)

def second_inputs(seed: int = 0) -> dict:
    key = jax.random.key(seed)
    ks = jax.random.split(key, 24)
    f32 = jnp.float32

    def nrm(k, shape, scale):
        return scale * jax.random.normal(k, shape, f32)

    a_c = jax.random.uniform(ks[10], (DEPTH, LRU_WIDTH), f32, 0.9, 0.999)
    s = a_c ** (1.0 / LRU_C)
    return {
        "x": nrm(ks[0], (BATCH, SEQ, D_MODEL), 1.0),
        "meta_tokens": nrm(ks[1], (N_META, D_MODEL), 1.0),
        "norm_mix_g": 1.0 + nrm(ks[2], (DEPTH, D_MODEL), 0.02),
        "w_in": nrm(ks[3], (DEPTH, D_MODEL, IN_COLS), D_MODEL ** -0.5),
        "hg_lb_logits": nrm(ks[4], (DEPTH, HG_WIDTH), 0.1),
        "hg_norm_g": 1.0 + nrm(ks[5], (DEPTH, HG_DIM), 0.02),
        "ret_norm_g": 1.0 + nrm(ks[6], (DEPTH, RET_DV), 0.02),
        "lru_conv_w": nrm(ks[7], (DEPTH, LRU_CONV, LRU_WIDTH), LRU_CONV ** -0.5),
        "lru_conv_b": nrm(ks[8], (DEPTH, LRU_WIDTH), 0.01),
        "lru_gate_a_w": nrm(ks[9], (DEPTH, LRU_BLOCKS, LRU_BLOCK, LRU_BLOCK), LRU_BLOCK ** -0.5),
        "lru_gate_a_b": nrm(ks[11], (DEPTH, LRU_WIDTH), 0.01),
        "lru_gate_i_w": nrm(ks[12], (DEPTH, LRU_BLOCKS, LRU_BLOCK, LRU_BLOCK), LRU_BLOCK ** -0.5),
        "lru_gate_i_b": nrm(ks[13], (DEPTH, LRU_WIDTH), 0.01),
        "lru_lambda": jnp.log(s) - jnp.log1p(-s),
        "w_out": nrm(ks[14], (DEPTH, D_MIX, D_MODEL), D_MIX ** -0.5),
        "norm_ffn_g": 1.0 + nrm(ks[15], (DEPTH, D_MODEL), 0.02),
        "ffn_w_up": nrm(ks[16], (DEPTH, D_MODEL, 2 * D_FF_2), D_MODEL ** -0.5),
        "ffn_conv_w": nrm(ks[17], (DEPTH, FFN_CONV, 2 * D_FF_2), FFN_CONV ** -0.5),
        "ffn_conv_b": nrm(ks[18], (DEPTH, 2 * D_FF_2), 0.01),
        "ffn_w_down": nrm(ks[19], (DEPTH, D_FF_2, D_MODEL), D_FF_2 ** -0.5),
        "final_norm_g": 1.0 + nrm(ks[20], (D_MODEL,), 0.02),
    }

def second_block(x, meta_tokens, norm_mix_g, w_in, hg_lb_logits, hg_norm_g, ret_norm_g,
              lru_conv_w, lru_conv_b, lru_gate_a_w, lru_gate_a_b, lru_gate_i_w, lru_gate_i_b,
              lru_lambda, w_out, norm_ffn_g, ffn_w_up, ffn_conv_w, ffn_conv_b, ffn_w_down,
              final_norm_g):
    bsz = x.shape[0]
    meta = jnp.broadcast_to(meta_tokens[None].astype(x.dtype), (bsz, N_META, x.shape[-1]))
    h = jnp.concatenate([meta, x], axis=1)
    t = h.shape[1]

    pos = jnp.arange(t, dtype=jnp.float32)
    theta = ROPE_BASE ** (-jnp.linspace(0.0, 1.0, RET_DK // 2, dtype=jnp.float32))
    ang = pos[:, None] * theta[None, :]
    cos, sin = jnp.cos(ang), jnp.sin(ang)

    lb_all = jnp.cumsum(jax.nn.softmax(hg_lb_logits.astype(jnp.float32), axis=0), axis=0)
    lb_all = lb_all - lb_all[0:1]

    for l in range(DEPTH):
        h = h + hybrid_mixer(rmsnorm(h, norm_mix_g[l]), w_in[l], lb_all[l], hg_norm_g[l],
                             ret_norm_g[l], lru_conv_w[l], lru_conv_b[l], lru_gate_a_w[l],
                             lru_gate_a_b[l], lru_gate_i_w[l], lru_gate_i_b[l], lru_lambda[l],
                             w_out[l], cos, sin).astype(h.dtype)
        h = h + conv_glu_ffn(rmsnorm(h, norm_ffn_g[l]), ffn_w_up[l], ffn_conv_w[l],
                             ffn_conv_b[l], ffn_w_down[l]).astype(h.dtype)

    return rmsnorm(h, final_norm_g)[:, N_META:]


def setup_inputs(seed=0):
    out = dict(first_inputs(seed))
    for name, value in second_inputs(seed + 1).items():
        if name != "x":
            out[name + "_2"] = value
    return out


def reference(
    x, a_w_qkv, a_lambda, a_subln_g, a_w_o, kv_w, b_w_q, b_rel_bias, b_w_o, ln_g, ln_b,
    ffn_w_in, ffn_w_out, meta_tokens_2, norm_mix_g_2, w_in_2, hg_lb_logits_2, hg_norm_g_2,
    ret_norm_g_2, lru_conv_w_2, lru_conv_b_2, lru_gate_a_w_2, lru_gate_a_b_2, lru_gate_i_w_2,
    lru_gate_i_b_2, lru_lambda_2, w_out_2, norm_ffn_g_2, ffn_w_up_2, ffn_conv_w_2, ffn_conv_b_2,
    ffn_w_down_2, final_norm_g_2,
):
    x = first_block(
        x, a_w_qkv, a_lambda, a_subln_g, a_w_o, kv_w, b_w_q, b_rel_bias, b_w_o, ln_g, ln_b,
        ffn_w_in, ffn_w_out,
    )
    return second_block(
        x, meta_tokens_2, norm_mix_g_2, w_in_2, hg_lb_logits_2, hg_norm_g_2, ret_norm_g_2,
        lru_conv_w_2, lru_conv_b_2, lru_gate_a_w_2, lru_gate_a_b_2, lru_gate_i_w_2,
        lru_gate_i_b_2, lru_lambda_2, w_out_2, norm_ffn_g_2, ffn_w_up_2, ffn_conv_w_2,
        ffn_conv_b_2, ffn_w_down_2, final_norm_g_2,
    )


_drawn_inputs = setup_inputs


def setup_inputs(seed=0):
    import zlib

    import numpy as np

    out = dict(_drawn_inputs(seed))
    spreads = {}
    factors = {'a_subln_g': 4.776,
     'b_rel_bias': 4.545,
     'hg_lb_logits_2': 8.0,
     'hg_norm_g_2': 4.875,
     'ret_norm_g_2': 6.869,
     'lru_gate_a_b_2': 64.0,
     'lru_gate_i_b_2': 33.25,
     'norm_ffn_g_2': 2.955,
     'ffn_conv_b_2': 5.587,
     'final_norm_g_2': 8.014,
     'lru_conv_b_2': 5.985}
    for name, (base, spread) in spreads.items():
        noise = np.random.default_rng([zlib.crc32(name.encode()), seed]).standard_normal(out[name].shape)
        drawn = base * np.exp(spread * noise) if base else spread * noise
        out[name] = __import__('jax').numpy.asarray(drawn.astype(out[name].dtype))
    for name, factor in factors.items():
        out[name] = (out[name] * factor).astype(out[name].dtype)
    return out
```

```python
import math
from contextlib import ExitStack

import numpy as np
import concourse.bass as bass
from concourse import mybir

D = 1024
T = 528
META = 16
FF = 2816
NF = FF // 128
ALPHA = 4.0 ** 0.25
RAW = 3
NS = 3
NEG = -1.0e30


def unit_plan():
    plan = []

    def cols(name, c, nk=8, k0=0):
        plan.append((name, k0, nk, c, 128))

    def wide(name, c):
        plan.append((name, 0, 4, c, 256))
        plan.append((name, 4, 4, c, 256))

    def ffn(win, wout):
        for m in range(NF):
            cols(win, 128 * m)
            cols(win, FF + 128 * m)
        for m in range(8):
            for k0, nk in ((0, 8), (8, 8), (16, 6)):
                cols(wout, 128 * m, nk, k0)

    for g in range(4):
        for part in (0, 1):
            for j in range(2):
                cols("a_qkv", 1024 * part + 256 * g + 128 * j)
        wide("a_qkv", 2048 + 256 * g)
    for m in range(8):
        cols("a_o", 128 * m)
    ffn("f_in0", "f_out0")
    for g in range(4):
        for j in range(2):
            cols("b_q", 256 * g + 128 * j)
        for j in range(2):
            cols("kv", 256 * g + 128 * j)
        wide("kv", 1024 + 256 * g)
    for m in range(8):
        cols("b_o", 128 * m)
    ffn("f_in1", "f_out1")
    for l in range(2):
        w = f"m_in{l}"
        wide(w, 1024)
        wide(w, 1280)
        for h in range(4):
            for c in (512, 0, 1536):
                cols(w, c + 128 * h)
        for c in (2816, 2944, 3072, 3200, 2048, 2176):
            cols(w, c)
        wide(w, 2304)
        cols(w, 2560)
        cols(w, 2688)
        for m in range(8):
            cols(f"m_out{l}", 128 * m)
        ffn(f"g_in{l}", f"g_out{l}")
    return plan


def param_columns():
    at, n = {}, 0
    for name, k in (("ln_g", 32), ("ln_b", 32), ("subln", 1), ("lam", 256), ("nmix", 16), ("nffn", 16),
                    ("nfin", 8), ("lb", 8), ("hgn", 2), ("retn", 2), ("lcw", 16), ("lcb", 4), ("gab", 4),
                    ("gib", 4), ("lru", 4), ("fcw", 264), ("fcb", 88)):
        at[name] = n
        n += k
    return at, n


CI, CM, CG, CB, CPA, CPR, CU, CV, CE = 0, 128, 256, 384, 512, 640, 768, 896, 1024
CN = 1028


class Tok:

    def __init__(self, eng):
        self.eng, self.used, self.sem, self.val = eng, False, None, 0


def flatten(w):
    if isinstance(w, (list, tuple)):
        for x in w:
            yield from flatten(x)
    elif w is not None:
        yield w


def do(method, *args, **named):
    return method, args, named


class Queue:

    def __init__(self, name):
        self.name, self.items = name, []
        self.last = None

    def __call__(self, what, *waits):
        flat = list(flatten(waits))
        for w in flat:
            w.used = True
        t = Tok(self.name)
        self.items.append((what, flat, t))
        self.last = t
        return t


def build(nc, wts, xT, mT, pp, cst, cstm, tA, tR, dt_h, biasT, gates, out):
    F = mybir.dt.float32
    R = mybir.dt.float32r
    U8 = mybir.dt.uint8
    ALU = mybir.AluOpType
    ACT = mybir.ActivationFunctionType
    AX = mybir.AxisListType
    plan = unit_plan()
    pc, npp = param_columns()

    pe, act, dve, pool, sp = (Queue(n) for n in ("pe", "act", "dve", "pool", "sp"))
    ctx = ExitStack()
    with ctx:
        def sb(name, shape, dt=F, c=ctx):
            return c.enter_context(nc.sbuf_tensor(name, shape, dt))

        X = sb("X", [128, 8, T])
        XH = sb("XH", [128, 8, T], R)
        XL = sb("XL", [128, 8, T], R)
        raw = sb("raw", [128, RAW, 2048])
        WH = sb("WH", [128, NS, 1024], R)
        WL = sb("WL", [128, NS, 1024], R)
        PP = sb("PP", [128, npp])
        C = sb("C", [128, CN])
        rstd = sb("rstd", [128, T])
        small = sb("small", [128, 64])
        P = ctx.enter_context(nc.psum_tensor("P", [128, 4096], F))

        sems = {n: ctx.enter_context(nc.semaphore("s_" + n)) for n in ("pe", "act", "dve", "pool")}
        raw_sem = [ctx.enter_context(nc.semaphore(f"s_raw{i}")) for i in range(RAW)]
        out_sem = ctx.enter_context(nc.semaphore("s_out"))
        nload = [0]

        def load(queue, dst, src, *waits):
            s = ctx.enter_context(nc.semaphore(f"s_ld{nload[0]}"))
            nload[0] += 1
            t = queue(do(nc.sync.dma_start if queue is sp else nc.gpsimd.dma_start, dst, src), *waits)
            t.used, t.sem, t.val = False, s, 16
            return t

        ident = C[:, CI:CI + 128]
        ones_mean = C[:, CM:CM + 128]
        ones_head = C[:, CG:CG + 128]
        ones_ret = C[:, CB:CB + 128]
        perm_a = C[:, CPA:CPA + 128]
        perm_r = C[:, CPR:CPR + 128]
        mask_u = C[0:1, CU:CU + 128]
        mask_v = C[0:1, CV:CV + 128]
        eps5 = C[:, CE:CE + 1]
        eps6 = C[:, CE + 1:CE + 2]

        def par(name, i, n=1):
            return PP[:, pc[name] + i:pc[name] + i + n]

        ld_c = load(pool, C[:, :], cst)
        ld_p = load(pool, PP[:, :], pp)
        ld_x = load(pool, X[:, :, META:T], xT)
        ld_m = load(pool, X[:, :, 0:META], mT)

        bank_free = [[] for _ in range(8)]

        def one(b):
            return P[:, 512 * b:512 * b + 512], [(512 * b, META, T)], [b]

        def two(p):
            a = 1024 * p + 248
            return P[:, a:a + T], [(a, 0, 264), (a + 264, 264, T)], [2 * p, 2 * p + 1]

        def take(banks):
            w = [t for b in banks for t in bank_free[b]]
            return w

        def release(banks, *toks):
            for b in banks:
                bank_free[b] = list(toks)

        raw_tok = {}
        raw_done = {}
        conv = {}
        pe_done = {}
        st = {"conv": 0, "cur": -1, "load": 0}

        def length(u):
            return plan[u][2] * plan[u][4]

        def load_chunks(upto):
            while st["load"] <= upto and 2 * st["load"] < len(plan):
                c = st["load"]
                n = length(2 * c) + length(2 * c + 1)
                s = c % RAW
                t = sp(do(nc.sync.dma_start, raw[:, s, 0:n], wts[c, :, 0:n]),
                       raw_done.get(c - RAW))
                t.sem, t.val = raw_sem[s], 16 * (c // RAW + 1)
                raw_tok[c] = t
                st["load"] += 1

        def convert(u):
            c, s = u // 2, u % NS
            load_chunks(c)
            a = length(u - 1) if u % 2 else 0
            n = length(u)
            src = raw[:, c % RAW, a:a + n]
            th = act(do(nc.scalar.activation, WH[:, s, 0:n], src, ACT.Copy), raw_tok[c], pe_done.get(u - NS))
            tl = dve(do(nc.vector.tensor_tensor, WL[:, s, 0:n], src, WH[:, s, 0:n].bitcast(F), ALU.subtract), th)
            conv[u] = [th, tl]
            raw_done.setdefault(c, []).append(tl)

        def need(u):
            while st["conv"] <= u:
                convert(st["conv"])
                st["conv"] += 1

        def run_ahead():
            while st["conv"] < min(len(plan), st["cur"] + NS):
                convert(st["conv"])
                st["conv"] += 1

        background = []

        def step():
            if background:
                g = background.pop(0)
                try:
                    next(g)
                    background.append(g)
                except StopIteration:
                    pass

        def drain():
            while background:
                step()

        def product(units, xh, xl, xready, region, lo_col=0, steps=1):
            ap, segs, banks = region
            w0 = take(banks)
            kt = 0
            total = sum(plan[u][2] for u in units)
            for u in units:
                need(u)
                s = u % NS
                wt = conv[u]
                for k in range(plan[u][2]):
                    for i, (wb, xb) in enumerate(((WL, xh), (WH, xl), (WH, xh))):
                        for a, c0, c1 in segs:
                            first = kt == 0 and i == 0
                            lastm = kt == total - 1 and i == 2
                            t = pe(do(nc.tensor.matmul, P[:, a:a + c1 - c0], wb[:, s, 128 * k:128 * k + 128],
                                            xb[:, kt, c0 - lo_col:c1 - lo_col], start=first, stop=lastm),
                                   w0, wt, xready[kt])
                            w0, wt = None, None
                    kt += 1
                    if kt % 2 == 0:
                        for _ in range(steps):
                            step()
                pe_done[u] = t
                st["cur"] = u
                run_ahead()
            return t

        def wide_product(u, tiles, region_of, consume, xready):
            need(u + 1)
            for n, (c0, c1) in enumerate(tiles):
                o, banks = region_of(n)
                w0 = take(banks)
                for k in range(8):
                    s, kk = (u + k // 4) % NS, k % 4
                    for i, (xb, wb) in enumerate(((XL, WH), (XH, WL), (XH, WH))):
                        t = pe(do(nc.tensor.matmul, o, xb[:, k, c0:c1], wb[:, s, 256 * kk:256 * kk + 256],
                                        start=(k == 0 and i == 0), stop=(k == 7 and i == 2)),
                               w0, conv[u], conv[u + 1], xready[k])
                        w0 = None
                release(banks, *consume(n, o, t))
                step()
            pe_done[u] = pe_done[u + 1] = t
            st["cur"] = u + 1
            run_ahead()

        unit = [0]

        def units(n):
            u = unit[0]
            unit[0] += n
            return list(range(u, u + n))

        def ones_sum(m, src, region, first, last, waits, lo_col=0):
            ap, segs, banks = region
            for a, c0, c1 in segs:
                t = pe(do(nc.tensor.matmul, P[:, a:a + c1 - c0], m, src[:, c0 - lo_col:c1 - lo_col],
                                                             start=first, stop=last), waits)
            return t

        def inv_root(dst, src, eps, waits):
            a = act(do(nc.scalar.activation, dst, src, ACT.Ln, bias=eps), waits)
            return a, act(do(nc.scalar.activation, dst, dst, ACT.Exp, scale=-0.5), a)

        def split(src, h, l, waits, hw):
            th = act(do(nc.scalar.activation, h, src, ACT.Copy), waits, hw)
            tl = dve(do(nc.vector.tensor_tensor, l, src, h.bitcast(F), ALU.subtract), th, waits, hw)
            return th, tl

        tmp = [sb(f"tmp{i}", [128, T]) for i in range(4)]
        tmp_free = [[] for _ in range(4)]
        tmp_at = [0]

        def temp():
            i = tmp_at[0] % 4
            tmp_at[0] += 1
            return i, tmp[i], tmp_free[i]

        C1 = slice(META, T)
        xr = [None] * 8
        x_done = [[ld_x, ld_m, ld_c, ld_p]] * 8
        for k in range(8):
            th, tl = split(X[:, k, C1], XH[:, k, C1], XL[:, k, C1], [ld_x], None)
            xr[k] = [th, tl]

        need(0)
        run_ahead()

        def residual_ln(l, j, tiles):
            g0 = pc["ln_g"] + 16 * l + 8 * j
            b0 = pc["ln_b"] + 16 * l + 8 * j
            mean = one(6)
            var = one(7)
            evac, last = [], None
            pend = []

            def sum_tile(m):
                w = [evac[m], ld_c] + (take(mean[2]) if m == 0 else [])
                return ones_sum(ones_mean, X[:, m, :], mean, m == 0, m == 7, w)

            for m in range(8):
                r = one(m % 3)
                t = tiles(m, r)
                v = dve(do(nc.vector.scalar_tensor_tensor, X[:, m, C1], X[:, m, C1], float(ALPHA), r[0],
                                                                   ALU.mult, ALU.add), t, x_done[m])
                release(r[2], v)
                evac.append(v)
                if m >= 1:
                    tm = sum_tile(m - 1)
            tm = sum_tile(7)
            wv = take(var[2])
            cen = []
            for m in range(8):
                c = dve(do(nc.vector.tensor_tensor, X[:, m, C1], X[:, m, C1], mean[0], ALU.subtract), tm, evac[m])
                cen.append(c)
                i, q, fr = temp()
                s = act(do(nc.scalar.activation, q[:, C1], X[:, m, C1], ACT.Square), c, fr)
                tv = ones_sum(ones_mean, q, var, m == 0, m == 7, [s] + wv)
                wv = []
                tmp_free[i] = [tv]
            release(mean[2], cen[-1])
            tl_, te = inv_root(rstd[:, C1], var[0], eps5, [tv, ld_c, rstd_free])
            release(var[2], tl_)
            dn = []
            for m in range(8):
                i, q, fr = temp()
                a = dve(do(nc.vector.tensor_tensor, q[:, C1], X[:, m, C1], rstd[:, C1], ALU.mult), te, cen[m], fr)
                h = act(do(nc.scalar.activation, XH[:, m, C1], q[:, C1], ACT.Identity, bias=PP[:, b0 + m:b0 + m + 1],
                                                         scale=PP[:, g0 + m:g0 + m + 1]), a, x_read)
                f = act(do(nc.scalar.activation, X[:, m, C1], q[:, C1], ACT.Identity, bias=PP[:, b0 + m:b0 + m + 1],
                                                         scale=PP[:, g0 + m:g0 + m + 1]), a)
                d = dve(do(nc.vector.tensor_tensor, XL[:, m, C1], X[:, m, C1], XH[:, m, C1].bitcast(F), ALU.subtract), f, h, x_read)
                tmp_free[i] = [f]
                x_done[m] = [f, d, h]
                xr[m] = [h, d]
            rstd_free[:] = [a]

        rstd_free = []
        x_read = []

        def phase_fence():
            return [q.last for q in (pe, act, dve)]

        ph = ExitStack()
        QT = [sb(f"QT{i}", [128, 2, 512], F, ph) for i in range(2)]
        KT = [sb(f"KT{i}", [128, 2, 512], F, ph) for i in range(2)]
        VN = [sb(f"VN{i}", [128, 4, 256], F, ph) for i in range(2)]
        OH = sb("OH", [128, 8, 512], R, ph)
        OL = sb("OL", [128, 8, 512], R, ph)
        cosA = sb("cosA", [128, 2, 512], F, ph)
        qraw = [sb(f"qraw{i}", [128, 512], F, ph) for i in range(2)]
        pr = [sb(f"pr{i}", [128, 2, 512], F, ph) for i in range(2)]
        aTs = [sb(f"aT{i}", [128, 4, 512], F, ph) for i in range(2)]
        ld_t = load(pool, cosA[:, :, :], tA)

        lv = PP[:, pc["lam"]:pc["lam"] + 256]
        t0 = dve(do(nc.vector.tensor_tensor, qraw[0][:, 0:64], lv[:, 0:64], lv[:, 64:128], ALU.mult), ld_p)
        t1 = dve(do(nc.vector.tensor_tensor, qraw[0][:, 64:128], lv[:, 128:192], lv[:, 192:256], ALU.mult), ld_p)
        t2 = dve(do(nc.vector.tensor_reduce, small[:, 0:2], qraw[0][:, 0:128].rearrange("p (a b) -> p a b", a=2), AX.X, ALU.add), t0, t1)
        t3 = act(do(nc.scalar.activation, small[:, 0:2], small[:, 0:2], ACT.Exp), t2)
        t4 = dve(do(nc.vector.tensor_tensor, small[:, 2:3], small[:, 1:2], small[:, 0:1], ALU.subtract), t3)
        lam_init = 0.8 - 0.6 * math.exp(0.0)
        neglam = dve(do(nc.vector.tensor_scalar, small[:, 2:3], small[:, 2:3], -lam_init, None, ALU.add), t4)
        g8 = dve(do(nc.vector.tensor_scalar, small[:, 3:4], par("subln", 0), 1.0 - lam_init, None, ALU.mult), ld_p)

        qraw_free = [[t2], []]
        nrope = [0]

        def rope_tile(region, t, dst, dst_free, scale, table, perm, C0, prm_region):
            i = nrope[0] % 2
            nrope[0] += 1
            q = qraw[i]
            n = C0[1] - C0[0]
            a = act(do(nc.scalar.activation, q[:, 0:n], region[0], ACT.Copy, scale=scale), t, qraw_free[i])
            release(region[2], a)
            t_sw = ones_sum(perm, q, prm_region, True, True, [a] + take(prm_region[2]) + [ld_c], C0[0])
            j, w, fr = temp()
            b = dve(do(nc.vector.tensor_tensor, w[:, 0:n], q[:, 0:n], table[:, 0, :], ALU.mult), a, fr, ld_t)
            c = dve(do(nc.vector.tensor_tensor, dst, prm_region[0], table[:, 1, :], ALU.mult), t_sw, dst_free, ld_t)
            release(prm_region[2], c)
            d = dve(do(nc.vector.tensor_tensor, dst, dst, w[:, 0:n], ALU.add), b, c)
            tmp_free[j] = [d]
            qraw_free[i] = [b, t_sw]
            return d

        qk_free = [[], []]
        v_free = [[], []]
        pr_free = [[], []]
        aT_free = [[], []]
        o_ready = [None] * 8
        nat = [(META + 128 * i, META + 128 * i + 128) for i in range(4)]

        def nat_region(n):
            b = 7 if n // 2 == 0 else 6
            return P[:, 512 * b + 256 * (n % 2):512 * b + 256 * (n % 2) + 256], [b]

        def transposes(i, src, aT, bank, waits, afree):
            w = take([bank]) + waits
            for j in range(i + 1):
                t = pe(do(nc.tensor.transpose, P[:, 512 * bank + 128 * j:512 * bank + 128 * j + 128],
                                                  src[:, 128 * j:128 * j + 128], ident), w)
            v = act(do(nc.scalar.activation, aT[:, 0:i + 1, 128 * i:128 * i + 128],
                                           P[:, 512 * bank:512 * bank + 128 * (i + 1)].rearrange("p (j c) -> p j c", c=128),
                                           ACT.Copy), t, afree)
            release([bank], v)
            return t, v

        def attn_a(h, g, lane, qk_ready, v_ready):
            b0 = 2 + 2 * lane
            Q, K, V = QT[g % 2], KT[g % 2], VN[g % 2]
            hh = h % 2
            p, aT = pr[lane], aTs[lane]
            sm = small[:, 8 + 12 * lane:20 + 12 * lane]
            ev = []
            sfree = []
            for i in range(4):
                ke = 128 * (i + 1)
                w = take([b0, b0 + 1]) + qk_ready + [ld_c]
                for m in range(2):
                    o = 512 * (b0 + m)
                    pe(do(nc.tensor.matmul, P[:, o:o + ke], Q[64 * m:64 * m + 64, hh, 128 * i:128 * i + 128],
                                                                K[64 * m:64 * m + 64, hh, 0:ke], start=True, stop=False), w)
                    t = pe(do(nc.tensor.matmul, P[:, o + ke - 128:o + ke], mask_u, mask_v, start=False, stop=True))
                yield
                both = P[:, 512 * b0:512 * b0 + 1024].rearrange("p (m c) -> p m c", m=2)[:, :, 0:ke]
                a = dve(do(nc.vector.tensor_reduce, sm[:, 0:2], both, AX.X, ALU.max, negate=True), t, sfree)
                for m in range(2):
                    x = act(do(nc.scalar.activation, p[:, m, 0:ke], P[:, 512 * (b0 + m):512 * (b0 + m) + ke], ACT.Exp,
                                                               bias=sm[:, m:m + 1], accum_out=sm[:, 2 + m:3 + m]),
                            a, pr_free[lane])
                release([b0, b0 + 1], x)
                r = dve(do(nc.vector.reciprocal, sm[:, 4:6], sm[:, 2:4]), x)
                r1 = dve(do(nc.vector.tensor_tensor, sm[:, 6:7], sm[:, 5:6], small[:, 2:3], ALU.mult), r, neglam)
                c = dve(do(nc.vector.tensor_scalar, p[:, 0, 0:ke], p[:, 0, 0:ke], sm[:, 4:5], None, ALU.mult), r)
                c = dve(do(nc.vector.scalar_tensor_tensor, p[:, 0, 0:ke], p[:, 1, 0:ke], sm[:, 6:7], p[:, 0, 0:ke],
                                                                ALU.mult, ALU.add), c, r1)
                sfree = [c]
                yield
                yield
                t, v = transposes(i, p[:, 0, :], aT, b0, [c], aT_free[lane])
                pr_free[lane] = [t]
                ev.append(v)
                yield
            w = take([b0 + 1]) + ev + v_ready
            o = 512 * (b0 + 1)
            for j in range(4):
                t = pe(do(nc.tensor.matmul, P[:, o + 128 * j:o + 512], V[:, j, 128 * hh:128 * hh + 128],
                                               aT[:, j, 128 * j:512], start=(j == 0), stop=(j == 3)), w)
            aT_free[lane] = [t]
            att_last[lane] = t
            yield
            i1, q, fr = temp()
            s = act(do(nc.scalar.activation, q[:, 0:512], P[:, o:o + 512], ACT.Square), t, fr)
            t_ms = pe(do(nc.tensor.matmul, P[:, 512 * b0:512 * b0 + 512], ones_head, q[:, 0:512], start=True, stop=True),
                      s, take([b0]))
            yield
            a, b = inv_root(q[:, 0:512], P[:, 512 * b0:512 * b0 + 512], eps5, [t_ms])
            release([b0], a)
            n = dve(do(nc.vector.scalar_tensor_tensor, q[:, 0:512], P[:, o:o + 512], small[:, 3:4], q[:, 0:512],
                                                     ALU.mult, ALU.mult), b, g8)
            release([b0 + 1], n)
            th, tl = split(q[:, 0:512], OH[:, h, :], OL[:, h, :], [n], None)
            tmp_free[i1] = [th, tl]
            o_ready[h] = [th, tl]

        att_last = [None, None]
        for g in range(4):
            drain_before = g >= 2
            ready = []
            for part, dst in ((0, QT), (1, KT)):
                for j in range(2):
                    r = one((2 * part + j) % 2)
                    t = product(units(1), XH, XL, xr, r, steps=2)
                    ready.append(rope_tile(r, t, dst[g % 2][:, j, :], qk_free[g % 2], 0.125 if part == 0 else 1.0,
                                           cosA, perm_a, (META, T), one(6)))
            vt = []

            def keep_v(n, o, t, g=g, vt=vt):
                v = act(do(nc.scalar.activation, VN[g % 2][:, n, :], o, ACT.Copy), t, v_free[g % 2])
                vt.append(v)
                return [v]

            u = units(2)
            wide_product(u[0], nat, nat_region, keep_v, xr)
            drain()
            qk_free[(g + 1) % 2] = [x for x in att_last if x]
            v_free[(g + 1) % 2] = [x for x in att_last if x]
            background.append(attn_a(2 * g, g, 0, ready, vt))
            background.append(attn_a(2 * g + 1, g, 1, ready, vt))
        drain()
        x_read[:] = [pe_done[unit[0] - 1]]

        residual_ln(0, 0, lambda m, r: product(units(1), OH, OL, o_ready, r, lo_col=META))
        ph.close()

        def swiglu(l):
            ph = ExitStack()
            fence = phase_fence()
            HH = sb(f"HH{l}", [128, NF, 512], R, ph)
            HL = sb(f"HL{l}", [128, NF, 512], R, ph)
            hr = []
            for m in range(NF):
                rg, ru = one((2 * m) % 4), one((2 * m) % 4 + 1)
                tg = product(units(1), XH, XL, xr, rg)
                i, q, fr = temp()
                a = act(do(nc.scalar.activation, q[:, 0:512], rg[0], ACT.Silu), tg, fr)
                release(rg[2], a)
                tu = product(units(1), XH, XL, xr, ru)
                b = dve(do(nc.vector.tensor_tensor, q[:, 0:512], q[:, 0:512], ru[0], ALU.mult), a, tu)
                release(ru[2], b)
                th, tl = split(q[:, 0:512], HH[:, m, :], HL[:, m, :], [b], fence)
                tmp_free[i] = [th, tl]
                hr.append([th, tl])
            x_read[:] = [pe_done[unit[0] - 1]]
            residual_ln(l, 1, lambda m, r: product(units(3), HH, HL, hr, r, lo_col=META))
            ph.close()

        swiglu(0)

        ph = ExitStack()
        fence = phase_fence()
        QB = [sb(f"QB{i}", [128, 2, 512], F, ph) for i in range(2)]
        KB_ = [sb(f"KB{i}", [128, 2, 512], F, ph) for i in range(2)]
        VB = [sb(f"VB{i}", [128, 4, 256], F, ph) for i in range(2)]
        OH2 = sb("OH2", [128, 8, 512], R, ph)
        OL2 = sb("OL2", [128, 8, 512], R, ph)
        bT = sb("bT", [128, 4, 512], F, ph)
        prB = [sb(f"prB{i}", [128, 512], F, ph) for i in range(2)]
        aTB = [sb(f"aTB{i}", [128, 4, 512], F, ph) for i in range(2)]
        oB = [sb(f"oB{i}", [128, 512], F, ph) for i in range(2)]
        pr_free = [fence, fence]
        aT_free = [fence, fence]
        bt_free = [fence] * 4
        qk_free = [fence, fence]
        v_free = [fence, fence]
        ob_free = [fence, fence]
        att_last = [None, None]
        o_ready = [None] * 8

        def attn_b(tile, g, lane, qk_ready, v_ready):
            b0 = 2 + 2 * lane
            Q, K, V = QB[g % 2], KB_[g % 2], VB[g % 2]
            hh = tile % 2
            p, aT = prB[lane], aTB[lane]
            sm = small[:, 8 + 12 * lane:20 + 12 * lane]
            sfree = []
            oe = []
            for half in range(2):
                h = 2 * tile + half
                s0 = 64 * half
                slot = 2 * lane + half
                ld_b = load(pool, bT[:, slot, :], biasT[h, :, :], bt_free[slot])
                ev = []
                for i in range(4):
                    ke = 128 * (i + 1)
                    o = 512 * b0
                    pe(do(nc.tensor.matmul, P[:, o:o + ke], Q[s0:s0 + 64, hh, 128 * i:128 * i + 128],
                                                                  K[s0:s0 + 64, hh, 0:ke], start=True, stop=False),
                       take([b0]) + qk_ready)
                    t = pe(do(nc.tensor.matmul, P[:, o + ke - 128:o + ke], mask_u, mask_v, start=False, stop=True))
                    yield
                    c = dve(do(nc.vector.tensor_tensor, p[:, 0:ke], P[:, o:o + ke], bT[:, slot, 512 - ke:512], ALU.add), t, pr_free[lane], ld_b)
                    release([b0], c)
                    a = dve(do(nc.vector.tensor_reduce, sm[:, 0:1], p[:, 0:ke], AX.X, ALU.max, negate=True), c, sfree)
                    x = act(do(nc.scalar.activation, p[:, 0:ke], p[:, 0:ke], ACT.Exp, bias=sm[:, 0:1],
                                                          accum_out=sm[:, 2:3]), a)
                    r = dve(do(nc.vector.reciprocal, sm[:, 4:5], sm[:, 2:3]), x)
                    c = dve(do(nc.vector.tensor_scalar, p[:, 0:ke], p[:, 0:ke], sm[:, 4:5], None, ALU.mult), r)
                    sfree = [c]
                    yield
                    yield
                    t, v = transposes(i, p, aT, b0, [c], aT_free[lane])
                    pr_free[lane] = [t]
                    ev.append(v)
                    yield
                bt_free[slot] = [c]
                o = 512 * (b0 + 1)
                w = take([b0 + 1]) + ev + v_ready
                for j in range(4):
                    t = pe(do(nc.tensor.matmul, P[s0:s0 + 64, o + 128 * j:o + 512],
                                                          V[:, j, 128 * hh + s0:128 * hh + s0 + 64],
                                                          aT[:, j, 128 * j:512], start=(j == 0), stop=(j == 3)), w)
                aT_free[lane] = [t]
                yield
                oe.append(t)
            att_last[lane] = t
            ob = oB[lane]
            a = act(do(nc.scalar.activation, ob[:, :], P[:, o:o + 512], ACT.Copy), oe, ob_free[lane])
            release([b0 + 1], a)
            th, tl = split(ob[:, :], OH2[:, tile, :], OL2[:, tile, :], [a], fence)
            ob_free[lane] = [th, tl]
            o_ready[tile] = [th, tl]

        for g in range(4):
            ready = []
            for part, dst in ((0, QB), (1, KB_)):
                for j in range(2):
                    r = one((2 * part + j) % 2)
                    t = product(units(1), XH, XL, xr, r, steps=2)
                    a = act(do(nc.scalar.activation, dst[g % 2][:, j, :], r[0], ACT.Copy, scale=0.125 if part == 0 else 1.0), t, qk_free[g % 2])
                    release(r[2], a)
                    ready.append(a)
            vt = []

            def keep_vb(n, o, t, g=g, vt=vt):
                v = act(do(nc.scalar.activation, VB[g % 2][:, n, :], o, ACT.Copy), t, v_free[g % 2])
                vt.append(v)
                return [v]

            u = units(2)
            wide_product(u[0], nat, nat_region, keep_vb, xr)
            drain()
            qk_free[(g + 1) % 2] = [x for x in att_last if x] or fence
            v_free[(g + 1) % 2] = [x for x in att_last if x] or fence
            background.append(attn_b(2 * g, g, 0, ready, vt))
            background.append(attn_b(2 * g + 1, g, 1, ready, vt))
        drain()
        x_read[:] = [pe_done[unit[0] - 1]]
        residual_ln(1, 0, lambda m, r: product(units(1), OH2, OL2, o_ready, r, lo_col=META))
        ph.close()
        swiglu(1)

        def rms(g0, waits_x, final=False):
            ms = two(3)
            w = take(ms[2])
            for m in range(8):
                i, q, fr = temp()
                s = act(do(nc.scalar.activation, q[:, :], X[:, m, :], ACT.Square), waits_x[m], fr)
                t = ones_sum(ones_mean, q, ms, m == 0, m == 7, [s] + w)
                w = []
                tmp_free[i] = [t]
            a, b = inv_root(rstd[:, :], ms[0], eps6, [t, rstd_free])
            release(ms[2], a)
            for m in range(8):
                i, q, fr = temp()
                n = dve(do(nc.vector.scalar_tensor_tensor, q[:, :], X[:, m, :], PP[:, g0 + m:g0 + m + 1], rstd[:, :],
                                                                   ALU.mult, ALU.mult), b, fr, waits_x[m])
                if final:
                    tok = load(sp, out[:, m, :], q[:, C1], n)
                    outs.append(tok)
                    tmp_free[i] = [tok]
                else:
                    th, tl = split(q[:, :], XH[:, m, :], XL[:, m, :], [n], x_read)
                    tmp_free[i] = [th, tl]
                    xr[m] = [th, tl]
            rstd_free[:] = [n]

        outs = []
        nat5 = [(0, META)] + nat

        def mixer(l):
            ph = ExitStack()
            fence = phase_fence()
            GH = sb(f"GH{l}", [128, 8, T], R, ph)
            GL = sb(f"GL{l}", [128, 8, T], R, ph)
            VI = sb(f"VI{l}", [128, 5, 512], F, ph)
            VR = sb(f"VR{l}", [128, 5, 256], F, ph)
            maskw = sb(f"masks{l}", [128, 256], mybir.dt.int32, ph)
            masks = maskw[:, :].bitcast(U8).rearrange("p (l c) -> p l c", l=8)
            SC = sb(f"SC{l}", [128, 2560], F, ph)
            SM = sb(f"SM{l}", [16, T], F, ph)
            A, B, K, Q, G, QA, KB = (sb(f"{n}{l}", [128, T], F, ph) for n in ("hA", "hB", "hK", "hQ", "hG", "hQA", "hKB"))
            G2 = sb(f"hG2{l}", [128, T], F, ph)
            tab = sb(f"tab{l}", [128, 2, T], F, ph)
            dec = [sb(f"dec{l}{i}", [128, T], F, ph) for i in range(2)]
            gw = sb(f"gw{l}", [128, 4, 128], F, ph)
            lbv = sb(f"lbv{l}", [128, 32], F, ph)
            LX = sb(f"LX{l}", [128, 2, T + 3], F, ph)
            ld_mask = load(pool, maskw[:, :], cstm, fence)
            ld_tab = load(pool, tab[:, :, :], tR, fence)
            ld_gw = load(pool, gw[:, :, :], gates[l, :, :, :], fence)
            first = {}

            def fr(name):
                if name in first:
                    return first[name]
                return fence

            if l == 0:
                z0 = dve(do(nc.vector.memset, lbv[:, 0:4], 0.0), fence)
                z1 = dve(do(nc.vector.memset, lbv[:, 4:8], 1.0), fence)
                lb_ready = [z0, z1]
            else:
                l0, l1 = par("lb", 0, 4), par("lb", 4, 4)
                z0 = dve(do(nc.vector.tensor_tensor, lbv[:, 8:12], l0, l1, ALU.max), fence)
                z1 = dve(do(nc.vector.tensor_tensor, lbv[:, 12:16], l0, lbv[:, 8:12], ALU.subtract), z0)
                z2 = dve(do(nc.vector.tensor_tensor, lbv[:, 16:20], l1, lbv[:, 8:12], ALU.subtract), z0)
                z3 = act(do(nc.scalar.activation, lbv[:, 12:20], lbv[:, 12:20], ACT.Exp), z1, z2)
                z4 = dve(do(nc.vector.tensor_tensor, lbv[:, 20:24], lbv[:, 12:16], lbv[:, 16:20], ALU.add), z3)
                z5 = dve(do(nc.vector.reciprocal, lbv[:, 20:24], lbv[:, 20:24]), z4)
                z6 = dve(do(nc.vector.tensor_tensor, lbv[:, 0:4], lbv[:, 16:20], lbv[:, 20:24], ALU.mult), z5)
                z7 = dve(do(nc.vector.tensor_tensor, lbv[:, 4:8], lbv[:, 12:16], lbv[:, 20:24], ALU.mult), z5)
                lb_ready = [z6, z7]
            lam = par("lru", 2 * l, 2)
            a0 = dve(do(nc.vector.tensor_scalar, lbv[:, 24:26], lam, -1.0, 0.0, ALU.mult, ALU.max), fence, ld_p)
            a1 = dve(do(nc.vector.tensor_scalar, lbv[:, 26:28], lam, -1.0, None, ALU.mult), fence, ld_p)
            a2 = dve(do(nc.vector.tensor_tensor, lbv[:, 26:28], lbv[:, 26:28], lam, ALU.min), a1)
            a3 = act(do(nc.scalar.activation, lbv[:, 26:28], lbv[:, 26:28], ACT.Exp), a2)
            a4 = dve(do(nc.vector.tensor_scalar, lbv[:, 28:30], lbv[:, 26:28], 2.0, None, ALU.add), a3)
            a5 = dve(do(nc.vector.reciprocal, lbv[:, 28:30], lbv[:, 28:30]), a4)
            a6 = dve(do(nc.vector.tensor_tensor, lbv[:, 26:28], lbv[:, 26:28], lbv[:, 28:30], ALU.mult), a5)
            a7 = dve(do(nc.vector.tensor_tensor, lbv[:, 28:30], lbv[:, 26:28], lbv[:, 26:28], ALU.mult), a6)
            t = dve(do(nc.vector.tensor_scalar, lbv[:, 30:32], lbv[:, 28:30], 1.0 / 17, 1.0 / 15, ALU.mult, ALU.add), a7)
            for n in (13, 11, 9, 7, 5, 3, 1):
                t = dve(do(nc.vector.tensor_tensor, lbv[:, 30:32], lbv[:, 30:32], lbv[:, 28:30], ALU.mult), t)
                t = dve(do(nc.vector.tensor_scalar, lbv[:, 30:32], lbv[:, 30:32], 1.0 / n, None, ALU.add), t)
            t = dve(do(nc.vector.tensor_tensor, lbv[:, 30:32], lbv[:, 30:32], lbv[:, 26:28], ALU.mult), t)
            t = dve(do(nc.vector.tensor_scalar, lbv[:, 30:32], lbv[:, 30:32], 2.0, None, ALU.mult), t)
            t = dve(do(nc.vector.tensor_tensor, lbv[:, 30:32], lbv[:, 30:32], lbv[:, 24:26], ALU.add), t)
            a8 = dve(do(nc.vector.tensor_scalar, lbv[:, 24:26], lbv[:, 30:32], 8.0, None, ALU.mult), t)
            sp_ready = dve(do(nc.vector.tensor_scalar, lbv[:, 26:28], lbv[:, 24:26], -1.0, None, ALU.mult), a8)
            sc_zero = dve(do(nc.vector.memset, SC[:, :], 0.0), fence)
            sm_zero = dve(do(nc.vector.memset, SM[:, :], 0.0), fence)
            lx_zero = dve(do(nc.vector.memset, LX[:, :, 0:3], 0.0), fence)
            first["SC"] = [sc_zero]
            first["SM"] = [sm_zero]

            rot = [0]

            def region():
                rot[0] += 1
                return two(rot[0] % 2)

            vi_ready, vr_ready = [], []

            def nat5_region(n):
                b = 2 * (n % 2) + (n // 2) % 2
                return P[0:(16 if n == 0 else 128), 512 * b:512 * b + 256], [b]

            def keep(dst, c0, lst):
                def f(n, o, t):
                    k = 16 if n == 0 else 128
                    v = act(do(nc.scalar.activation, dst[0:k, n, c0:c0 + 256], o, ACT.Copy), t, fence)
                    lst.append(v)
                    return [v]
                return f

            for c in range(2):
                u = units(2)
                wide_product(u[0], nat5, nat5_region, keep(VI, 256 * c, vi_ready), xr)

            def out_split(src, k, waits, ti):
                th, tl = split(src, GH[:, k, :], GL[:, k, :], waits, fence)
                if ti is not None:
                    tmp_free[ti] = [th, tl]
                g_ready[k] = [th, tl]
                return [th, tl]

            g_ready = [None] * 8

            def segments(c0, c1):
                return [(a, b) for a, b in ((c0, min(c1, 264)), (max(c0, 264), c1)) if a < b]

            def level(src, sz, c0, c1):
                return src[:, c0:c1].rearrange("p (n h s) -> p n h s", h=2, s=sz)

            def hgrn(h, toks):
                zA, zK, zQ, zG = toks
                Gb = (G, G2)[h % 2]
                tB = dve(do(nc.vector.memset, B[:, :], 1.0), fr("B"))
                tA_ = zA
                scd = SC[:, 0:2560].rearrange("p (j c) -> p j c", c=640)[:, :, 0:128]
                bx, bm = 4, 5
                acc = []
                for lev in range(-1, 7):
                    if lev < 0:
                        qa, kb, wq = Q, K, [zQ, zK]
                    else:
                        d1 = dve(do(nc.vector.tensor_tensor, QA[:, :], Q[:, :], A[:, :], ALU.mult), tA_, zQ, fr("QA"))
                        if lev == 0:
                            kb, wq = K, [d1, zK]
                        else:
                            d2 = dve(do(nc.vector.tensor_tensor, KB[:, :], K[:, :], B[:, :], ALU.mult), tB, zK, fr("KB"))
                            kb, wq = KB, [d1, d2]
                        qa = QA
                    w = wq + take([bx])
                    for j in range(4):
                        c = META + 128 * j
                        t = pe(do(nc.tensor.matmul, P[:, 512 * bx + 128 * j:512 * bx + 128 * j + 128],
                                                                          kb[:, c:c + 128], qa[:, c:c + 128],
                                                                          start=(j == 0), stop=(j == 3), skip_group_check=True), w)
                    if lev < 4:
                        t = pe(do(nc.tensor.matmul, P[0:16, 512 * bm:512 * bm + 16], kb[:, 0:16], qa[:, 0:16],
                                                                start=True, stop=True), take([bm]))
                        mm = dve(do(nc.vector.copy_predicated, SM[:, 0:16], masks[0:16, lev + 1, 0:16],
                                                                      P[0:16, 512 * bm:512 * bm + 16]), t, fr("SM"), acc, ld_mask)
                        release([bm], mm)
                        acc.append(mm)
                    first["QA"] = first["KB"] = [t]
                    mk = masks[:, lev + 1, :].unsqueeze(1).broadcast_to([128, 4, 128])
                    cp = dve(do(nc.vector.copy_predicated, scd, mk, P[:, 512 * bx:512 * bx + 512].rearrange("p (j c) -> p j c", c=128)), t, fr("SC"), acc, ld_mask)
                    release([bx], cp)
                    acc.append(cp)
                    acc = acc[-2:]
                    yield
                    if lev >= 0:
                        sz = 1 << lev
                        c0 = 0 if lev < 4 else META
                        Av, Bv = level(A, sz, c0, T), level(B, sz, c0, T)
                        nb = (T - c0) // (2 * sz)
                        if True:
                            ea = Av[:, :, 1, sz - 1:sz].broadcast_to([128, nb, sz])
                            tB = dve(do(nc.vector.tensor_tensor, Bv[:, :, 0, :], Bv[:, :, 0, :], ea, ALU.mult),
                                     tA_, tB, first["KB"])
                            eb = Av[:, :, 0, sz - 1:sz].broadcast_to([128, nb, sz])
                            tA_ = dve(do(nc.vector.tensor_tensor, Av[:, :, 1, :], Av[:, :, 1, :], eb, ALU.mult), tB)
                dense = []

                def dense_level(blocks, meta=False):
                    d1 = dve(do(nc.vector.tensor_tensor, QA[:, META:T], Q[:, META:T], A[:, META:T], ALU.mult), tA_, first["QA"])
                    d2 = dve(do(nc.vector.tensor_tensor, KB[:, :], K[:, :], B[:, :], ALU.mult), tB, first["KB"])
                    if meta:
                        t = pe(do(nc.tensor.matmul, P[0:16, 512 * bm:512 * bm + 512], KB[:, 0:16], QA[:, META:T],
                                                  start=True, stop=True), d1, d2, take([bm]))
                        v = act(do(nc.scalar.activation, SM[:, META:T], P[0:16, 512 * bm:512 * bm + 512], ACT.Copy), t, fr("SM"))
                        release([bm], v)
                        dense.append(v)
                        first["QA"] = first["KB"] = [t]
                        return
                    w = [d1, d2] + take([bx])
                    o = 512 * bx
                    evs = []
                    for n, (js, c0, c1) in enumerate(blocks):
                        t = pe(do(nc.tensor.matmul, P[:, o:o + c1 - c0], KB[:, META + 128 * js:META + 128 * js + 128], QA[:, META + c0:META + c1],
                            start=(n == 0), stop=(n == len(blocks) - 1), skip_group_check=True), w)
                        evs.append((js, c0, c1, o))
                        o += c1 - c0
                    for js, c0, c1, oo in evs:
                        v = act(do(nc.scalar.activation, SC[:, 512 * js + c0:512 * js + c1], P[:, oo:oo + c1 - c0], ACT.Copy), t, fr("SC"))
                        dense.append(v)
                    release([bx], v)
                    first["QA"] = first["KB"] = [t]

                dense_level([(0, 128, 256), (2, 384, 512)])
                yield
                for sz, blocks in ((128, [(0, 256, 512), (1, 256, 512)]), (256, None)):
                    Av, Bv = level(A, sz, META, T), level(B, sz, META, T)
                    nb = 512 // (2 * sz)
                    ea = Av[:, :, 1, sz - 1:sz].broadcast_to([128, nb, sz])
                    tB = dve(do(nc.vector.tensor_tensor, Bv[:, :, 0, :], Bv[:, :, 0, :], ea, ALU.mult),
                             tA_, tB, first["KB"])
                    eb = Av[:, :, 0, sz - 1:sz].broadcast_to([128, nb, sz])
                    tA_ = dve(do(nc.vector.tensor_tensor, Av[:, :, 1, :], Av[:, :, 1, :], eb, ALU.mult), tB,
                              first["QA"])
                    dense_level(blocks, meta=blocks is None)
                    yield
                first["A"] = first["B"] = first["K"] = first["Q"] = [t for t in (dve.last, pe.last)]
                reg = two(3)
                w = take(reg[2]) + dense + acc + vi_ready
                o = 1024 * 3 + 248
                for a, b in segments(0, T):
                    t = pe(do(nc.tensor.matmul, P[:, o + a:o + b], VI[0:16, 0, 128 * h:128 * h + 128], SM[:, a:b],
                                                        start=True, stop=False, skip_group_check=True), w)
                for j in range(4):
                    s0 = META + 128 * j
                    for a, b in segments(s0, T):
                        t = pe(do(nc.tensor.matmul, P[:, o + a:o + b], VI[:, 1 + j, 128 * h:128 * h + 128], SC[:, 512 * j + a - META:512 * j + b - META],
                            start=False, stop=True, skip_group_check=True), w)
                first["SC"] = first["SM"] = [t]
                yield
                i, q, f_ = temp()
                s = act(do(nc.scalar.activation, q[:, :], reg[0], ACT.Square), t, f_)
                r2 = two(2)
                t2 = ones_sum(ones_head, q, r2, True, True, [s] + take(r2[2]))
                yield
                a_, b_ = inv_root(q[:, :], r2[0], eps6, [t2])
                release(r2[2], a_)
                n1 = dve(do(nc.vector.scalar_tensor_tensor, q[:, :], reg[0], par("hgn", l), q[:, :], ALU.mult, ALU.mult), b_)
                release(reg[2], n1)
                n2 = dve(do(nc.vector.tensor_tensor, q[:, :], q[:, :], Gb[:, :], ALU.mult), n1, zG)
                out_split(q[:, :], h, [n2], i)
                first[f"G{h % 2}"] = [n2]

            def last_of(name):
                return first.get(name, fence)

            for h in range(4):
                r = region()
                t = product(units(1), XH, XL, xr, r, steps=2)
                drain()
                i, q, f_ = temp()
                j, q2, f2 = temp()
                s1 = act(do(nc.scalar.activation, q[:, :], r[0], ACT.Sigmoid), t, f_)
                s2 = act(do(nc.scalar.activation, q2[:, :], r[0], ACT.Sigmoid, scale=-1.0), t, f2)
                release(r[2], s2)
                zA = dve(do(nc.vector.tensor_scalar, A[:, :], q[:, :], lbv[:, 4 + h:5 + h], lbv[:, h:h + 1],
                                                             ALU.mult, ALU.add), s1, lb_ready, last_of("A"))
                zK = dve(do(nc.vector.tensor_scalar, K[:, :], q2[:, :], lbv[:, 4 + h:5 + h], float(128 ** -0.5),
                                                               ALU.mult, ALU.mult), s2, lb_ready, last_of("K"))
                tmp_free[i], tmp_free[j] = [zA], [zK]
                r = region()
                t = product(units(1), XH, XL, xr, r, steps=2)
                zQ = act(do(nc.scalar.activation, Q[:, :], r[0], ACT.Silu), t, last_of("Q"))
                release(r[2], zQ)
                r = region()
                t = product(units(1), XH, XL, xr, r, steps=2)
                Gb = (G, G2)[h % 2]
                zG = act(do(nc.scalar.activation, Gb[:, :], r[0], ACT.Silu), t, last_of(f"G{h % 2}"))
                release(r[2], zG)
                background.append(hgrn(h, (zA, zK, zQ, zG)))

            drain()
            LY = SC[:, 0:2 * T].rearrange("p (n t) -> p n t", n=2)
            LR = [K, Q, dec[1]]
            lx_t, ly_t = [], []
            for n in range(2):
                r = region()
                t = product(units(1), XH, XL, xr, r, steps=2)
                v = act(do(nc.scalar.activation, LX[:, n, 3:T + 3], r[0], ACT.Copy), t, fence)
                release(r[2], v)
                lx_t.append(v)
            for n in range(2):
                r = region()
                t = product(units(1), XH, XL, xr, r, steps=2)
                v = act(do(nc.scalar.activation, LY[:, n, :], r[0], ACT.Gelu_apprx_tanh), t, first["SC"])
                release(r[2], v)
                ly_t.append(v)
            drain()

            def lru():
                lrf = [first["K"], first["Q"], fence]
                for n in range(2):
                    Y = LR[0]
                    x = LX[:, n, :]

                    def cw(j, n=n):
                        return PP[:, pc["lcw"] + 8 * l + 2 * j + n:pc["lcw"] + 8 * l + 2 * j + n + 1]

                    c = dve(do(nc.vector.tensor_scalar, Y[:, :], x[:, 3:T + 3], cw(3), par("lcb", 2 * l + n), ALU.mult, ALU.add),
                            lx_t[n], lx_zero, lrf[0])
                    for j in range(3):
                        c = dve(do(nc.vector.scalar_tensor_tensor, Y[:, :], x[:, j:j + T], cw(j), Y[:, :], ALU.mult, ALU.add), c)
                    rg_ = two(2)
                    t = ones_sum(gw[:, n, :], Y, rg_, True, True, [c, ld_gw] + take(rg_[2]))
                    s1 = act(do(nc.scalar.activation, LR[1][:, :], rg_[0], ACT.Sigmoid, bias=par("gab", 2 * l + n)), t, lrf[1])
                    release(rg_[2], s1)
                    ri = two(3)
                    t = ones_sum(gw[:, 2 + n, :], Y, ri, True, True, [c, ld_gw] + take(ri[2]))
                    s2 = act(do(nc.scalar.activation, LR[2][:, :], ri[0], ACT.Sigmoid, bias=par("gib", 2 * l + n)), t, lrf[2])
                    release(ri[2], s2)
                    yield
                    i, q, f1 = temp()
                    th = act(do(nc.scalar.activation, q[:, :], LR[1][:, :], ACT.Tanh, scale=lbv[:, 24 + n:25 + n]), s1, f1, sp_ready)
                    ea = act(do(nc.scalar.activation, LR[1][:, :], LR[1][:, :], ACT.Exp, scale=lbv[:, 26 + n:27 + n]), th, sp_ready)
                    ix = dve(do(nc.vector.tensor_tensor, Y[:, :], Y[:, :], LR[2][:, :], ALU.mult), s2, t)
                    a2 = dve(do(nc.vector.tensor_tensor, LR[2][:, :], LR[1][:, :], LR[1][:, :], ALU.mult), ea, ix)
                    a3 = dve(do(nc.vector.scalar_tensor_tensor, q[:, :], LR[2][:, :], 1.0, q[:, :], ALU.add, ALU.mult), a2, th)
                    a4 = act(do(nc.scalar.activation, q[:, :], q[:, :], ACT.Sqrt), a3)
                    a5 = dve(do(nc.vector.tensor_tensor, Y[:, :], Y[:, :], q[:, :], ALU.mult), a4, ix)
                    a6 = dve(do(nc.vector.tensor_tensor_scan, q[:, :], LR[1][:, :], Y[:, :], 0.0, ALU.mult, ALU.add), a5, ea)
                    a7 = dve(do(nc.vector.tensor_tensor, q[:, :], q[:, :], LY[:, n, :], ALU.mult), a6, ly_t[n])
                    o = out_split(q[:, :], 6 + n, [a7], i)
                    lrf = [[a5, a6], [a6], [a3]]
                    lr_end[:] = [a5, a6, a7]
                    yield

            lr_end = []
            background.append(lru())

            QR, KR = A, B
            rr = []
            nonlocal_qraw = (QA, KB)
            rope_free = [list(first["QA"]), list(first["KB"])]
            for n, (dst, name) in enumerate(((QR, "A"), (KR, "B"))):
                r = region()
                t = product(units(1), XH, XL, xr, r, steps=2)
                drain()
                qx = nonlocal_qraw[n]
                a = act(do(nc.scalar.activation, qx[:, :], r[0], ACT.Copy), t, rope_free[n])
                release(r[2], a)
                pr_ = two(2)
                ts = ones_sum(perm_r, qx, pr_, True, True, [a] + take(pr_[2]))
                i, w_, f1 = temp()
                b = dve(do(nc.vector.tensor_tensor, w_[:, :], qx[:, :], tab[:, 0, :], ALU.mult), a, f1, ld_tab)
                c = dve(do(nc.vector.tensor_tensor, dst[:, :], pr_[0], tab[:, 1, :], ALU.mult), ts, first[name], ld_tab)
                release(pr_[2], c)
                d = dve(do(nc.vector.tensor_tensor, dst[:, :], dst[:, :], w_[:, :], ALU.add), b, c)
                tmp_free[i] = [d]
                rr.append(d)
            u = units(2)
            wide_product(u[0], nat5, nat5_region, keep(VR, 0, vr_ready), xr)
            gr = []
            for n, Gb in enumerate((G, G2)):
                r = region()
                t = product(units(1), XH, XL, xr, r, steps=2)
                v = act(do(nc.scalar.activation, Gb[:, :], r[0], ACT.Silu), t, first[f"G{n}"])
                release(r[2], v)
                gr.append(v)
            drain()
            x_read[:] = [pe_done[unit[0] - 1]]

            first["SC"] = lr_end

            def retention():
                dfree = [fence, lr_end]
                for n in range(2):
                    reg = two(3)
                    wo = take(reg[2])
                    o = 1024 * 3 + 248
                    for half in range(2):
                        hh = 2 * n + half
                        dc = dec[half]
                        ld_d = load(pool, dc[:, :], dt_h[hh, :, :], dfree[half])
                        tl_ = []
                        r2 = two(2)
                        w = take(r2[2]) + rr
                        for a, b in segments(0, T):
                            t = pe(do(nc.tensor.matmul, P[0:16, 1024 * 2 + 248 + a:1024 * 2 + 248 + b], KR[32 * hh:32 * hh + 32, 0:16],
                                QR[32 * hh:32 * hh + 32, a:b], start=True, stop=True), w)
                        v = dve(do(nc.vector.tensor_tensor, SM[:, :], P[0:16, 2296:2296 + T], dc[0:16, :], ALU.mult),
                                t, ld_d, first["SM"])
                        release(r2[2], v)
                        tl_.append(v)
                        for j in range(4):
                            bk = (4, 5)[j % 2]
                            m = 512 - 128 * j
                            t = pe(do(nc.tensor.matmul, P[:, 512 * bk:512 * bk + m], KR[32 * hh:32 * hh + 32, META + 128 * j:META + 128 * j + 128],
                                QR[32 * hh:32 * hh + 32, META + 128 * j:T], start=True, stop=True), take([bk]))
                            v = dve(do(nc.vector.tensor_tensor, SC[:, 640 * j:640 * j + m], P[:, 512 * bk:512 * bk + m], dc[:, 0:m], ALU.mult), t, first["SC"])
                            release([bk], v)
                            tl_.append(v)
                        dfree[half] = [v]
                        yield
                        s0 = 64 * half
                        for a, b in segments(0, T):
                            t = pe(do(nc.tensor.matmul, P[s0:s0 + 64, o + a:o + b], VR[0:16, 0, 64 * hh:64 * hh + 64], SM[:, a:b],
                                start=True, stop=False, skip_group_check=True), wo + tl_ + vr_ready)
                        for j in range(4):
                            c0 = META + 128 * j
                            for a, b in segments(c0, T):
                                t = pe(do(nc.tensor.matmul, P[s0:s0 + 64, o + a:o + b], VR[:, 1 + j, 64 * hh:64 * hh + 64],
                                    SC[:, 640 * j + a - c0:640 * j + b - c0], start=False, stop=True, skip_group_check=True))
                        first["SC"] = first["SM"] = [t]
                        yield
                    i, q, f1 = temp()
                    a = act(do(nc.scalar.activation, q[:, :], reg[0], ACT.Copy), t, f1)
                    release(reg[2], a)
                    r2 = two(2)
                    t = ones_sum(ones_ret, q, r2, True, True, [a] + take(r2[2]))
                    c = dve(do(nc.vector.tensor_tensor, q[:, :], q[:, :], r2[0], ALU.subtract), t)
                    release(r2[2], c)
                    yield
                    k, q2, f2 = temp()
                    s = act(do(nc.scalar.activation, q2[:, :], q[:, :], ACT.Square), c, f2)
                    t = ones_sum(ones_ret, q2, r2, True, True, [s] + take(r2[2]))
                    x1, x2 = inv_root(q2[:, :], r2[0], eps6, [t])
                    release(r2[2], x1)
                    c = dve(do(nc.vector.scalar_tensor_tensor, q[:, :], q[:, :], par("retn", l), q2[:, :],
                                                                         ALU.mult, ALU.mult), x2, c)
                    tmp_free[k] = [c]
                    Gb = (G, G2)[n]
                    c = dve(do(nc.vector.tensor_tensor, q[:, :], q[:, :], Gb[:, :], ALU.mult), c, gr[n])
                    out_split(q[:, :], 4 + n, [c], i)
                    yield

            background.append(retention())
            drain()
            for m in range(8):
                r = region()
                t = product(units(1), GH, GL, g_ready, r)
                v = dve(do(nc.vector.tensor_tensor, X[:, m, :], X[:, m, :], r[0], ALU.add), t, x_done[m])
                release(r[2], v)
                x_done[m] = [v]
            ph.close()

        def conv_glu(l):
            ph = ExitStack()
            fence = phase_fence()
            HH = sb(f"GHH{l}", [128, NF, T], R, ph)
            HL = sb(f"GHL{l}", [128, NF, T], R, ph)
            hr = []

            def conv_tile(r, t, c):
                def w(j):
                    k = pc["fcw"] + 132 * l + 44 * j + c
                    return PP[:, k:k + 1]
                i, y, f_ = temp()
                p = r[0]
                a = act(do(nc.scalar.activation, y[:, :], p, ACT.Identity, bias=par("fcb", 44 * l + c), scale=w(2)), t, f_)
                b = dve(do(nc.vector.scalar_tensor_tensor, y[:, 1:T], p[:, 0:T - 1], w(1), y[:, 1:T], ALU.mult, ALU.add), a)
                b = dve(do(nc.vector.scalar_tensor_tensor, y[:, 2:T], p[:, 0:T - 2], w(0), y[:, 2:T], ALU.mult, ALU.add), b)
                release(r[2], b)
                return i, y, b

            for m in range(NF):
                r = two((2 * m) % 4)
                i, yg, tg = conv_tile(r, product(units(1), XH, XL, xr, r), m)
                a = act(do(nc.scalar.activation, yg[:, :], yg[:, :], ACT.Silu), tg)
                r = two((2 * m + 1) % 4)
                j, yv, tv = conv_tile(r, product(units(1), XH, XL, xr, r), NF + m)
                b = dve(do(nc.vector.tensor_tensor, yg[:, :], yg[:, :], yv[:, :], ALU.mult), a, tv)
                tmp_free[j] = [b]
                th, tl = split(yg[:, :], HH[:, m, :], HL[:, m, :], [b], fence)
                tmp_free[i] = [th, tl]
                hr.append([th, tl])
            x_read[:] = [pe_done[unit[0] - 1]]
            for m in range(8):
                r = two(m % 3)
                t = product(units(3), HH, HL, hr, r)
                v = dve(do(nc.vector.tensor_tensor, X[:, m, :], X[:, m, :], r[0], ALU.add), t, x_done[m])
                release(r[2], v)
                x_done[m] = [v]
            ph.close()

        x_done = [x + [ld_m, ld_x] for x in x_done]
        for l in range(2):
            rms(pc["nmix"] + 8 * l, x_done)
            mixer(l)
            rms(pc["nffn"] + 8 * l, x_done)
            conv_glu(l)
        rms(pc["nfin"], x_done, final=True)
        sp(None, outs)
        assert unit[0] == len(plan)

        for q in (pe, act, dve, pool):
            n = 0
            for _, _, t in q.items:
                if t.sem is None and t.used:
                    n += 1
                    t.sem, t.val = sems[q.name], n

        def emit(q, e):
            seen = {}
            mine = sems.get(q.name)
            for what, waits, t in q.items:
                need_ = {}
                for w in waits:
                    k = w.sem.num if hasattr(w.sem, "num") else id(w.sem)
                    if seen.get(k, 0) < w.val:
                        if k not in need_ or need_[k][1] < w.val:
                            need_[k] = (w.sem, w.val)
                for k, (s, v) in need_.items():
                    e.wait_ge(s, v)
                    seen[k] = v
                if what is None:
                    continue
                ins = what[0](*what[1], **what[2])
                if t.sem is not None:
                    ins.then_inc(t.sem, 1 if t.sem is mine else 16)

        block = ctx.enter_context(nc.Block())

        @block.sync
        def _(e):
            emit(sp, e)

        @block.gpsimd
        def _(e):
            emit(pool, e)

        @block.scalar
        def _(e):
            emit(act, e)

        @block.vector
        def _(e):
            emit(dve, e)

        @block.tensor
        def _(e):
            emit(pe, e)


def constants():
    f = np.float32
    c = np.zeros((128, CN), f)
    eye = np.eye(128, dtype=f)
    c[:, CI:CI + 128] = eye
    c[:, CM:CM + 128] = 1.0 / 1024
    c[:, CG:CG + 128] = 1.0 / 128
    c[0:64, CB:CB + 64] = 1.0 / 64
    c[64:128, CB + 64:CB + 128] = 1.0 / 64
    i = np.arange(128)
    c[i, CPA + (i ^ 32)] = 1.0
    c[i, CPR + (i ^ 16)] = 1.0
    c[0, CU:CU + 64] = 1.0
    c[0, CV + 64:CV + 128] = NEG
    c[:, CE] = 1e-5
    c[:, CE + 1] = 1e-6
    s, t = np.meshgrid(i, i, indexing="ij")
    m = np.zeros((128, 8, 128), np.uint8)
    m[:, 0] = s == t
    for lev in range(7):
        b = 1 << lev
        m[:, lev + 1] = (s < t) & (s // (2 * b) == t // (2 * b)) & (s // b != t // b)
    inv = (f(10000.0) ** (-np.arange(0, 64, 2, dtype=f) / f(64))).astype(f)
    ang = np.arange(512, dtype=f)[:, None] * inv[None, :]
    co, si = np.cos(ang).T, np.sin(ang).T
    ta = np.stack([np.concatenate([co] * 4), np.concatenate([-si, si, -si, si])], 1).astype(f)
    th = (f(10000.0) ** (-np.linspace(0.0, 1.0, 16, dtype=f))).astype(f)
    ang = np.arange(T, dtype=f)[:, None] * th[None, :]
    co, si = np.cos(ang).T, np.sin(ang).T
    tr = np.stack([np.concatenate([co] * 8), np.concatenate([-si, si] * 4)], 1).astype(f)
    h = np.arange(4, dtype=np.float64)
    lg = np.log1p(-np.exp2(-5.0 - h))
    rel = np.arange(T)[None, :] - i[:, None]
    d = np.where(rel >= 0, np.exp(lg[:, None, None] * np.maximum(rel, 0)), 0.0) * 32 ** -0.5
    return c, m.reshape(128, 1024).view(np.int32), ta, tr, d.astype(f)


def pack_weights(w):
    plan = unit_plan()
    out = np.zeros((len(plan) // 2, 128, 2048), np.float32)
    for c in range(len(plan) // 2):
        a = 0
        for name, k0, nk, c0, n in plan[2 * c:2 * c + 2]:
            blk = w[name][128 * k0:128 * (k0 + nk), c0:c0 + n].reshape(nk, 128, n).transpose(1, 0, 2)
            out[c, :, a:a + nk * n] = blk.reshape(128, nk * n)
            a += nk * n
    return out


def pack_params(p):
    at, n = param_columns()
    out = np.zeros((128, n), np.float32)

    def put(name, a):
        out[:, at[name]:at[name] + a.shape[1]] = a

    def tiles(a):
        return a.reshape(-1, 128).T

    put("ln_g", tiles(p["ln_g"]))
    put("ln_b", tiles(p["ln_b"]))
    put("subln", tiles(p["a_subln_g"]))
    put("lam", np.broadcast_to(p["a_lambda"].reshape(1, 256), (128, 256)))
    put("nmix", tiles(p["norm_mix_g_2"]))
    put("nffn", tiles(p["norm_ffn_g_2"]))
    put("nfin", tiles(p["final_norm_g_2"]))
    put("lb", tiles(p["hg_lb_logits_2"]))
    put("hgn", tiles(p["hg_norm_g_2"]))
    put("retn", np.concatenate([p["ret_norm_g_2"]] * 2, 1).T)
    put("lcw", tiles(p["lru_conv_w_2"]))
    put("lcb", tiles(p["lru_conv_b_2"]))
    put("gab", tiles(p["lru_gate_a_b_2"]))
    put("gib", tiles(p["lru_gate_i_b_2"]))
    put("lru", tiles(p["lru_lambda_2"]))
    put("fcw", tiles(p["ffn_conv_w_2"]))
    put("fcb", tiles(p["ffn_conv_b_2"]))
    return out


def kernel(**inputs):
    import concourse.bacc as _bacc
    from concourse.bass_utils import run_bass_kernel_spmd as _run

    p = {k: np.asarray(v) for k, v in inputs.items()}
    w = {"a_qkv": p["a_w_qkv"][0], "a_o": p["a_w_o"][0], "kv": p["kv_w"], "b_q": p["b_w_q"][0], "b_o": p["b_w_o"][0]}
    for l in range(2):
        w[f"f_in{l}"], w[f"f_out{l}"] = p["ffn_w_in"][l], p["ffn_w_out"][l]
        w[f"m_in{l}"], w[f"m_out{l}"] = p["w_in_2"][l], p["w_out_2"][l]
        w[f"g_in{l}"], w[f"g_out{l}"] = p["ffn_w_up_2"][l], p["ffn_w_down_2"][l]
    c, masks, ta, tr, dec = constants()
    idx = np.clip(np.arange(512)[None, :] - 384 - np.arange(128)[:, None], -256, 256) + 256
    gates = np.zeros((2, 128, 4, 128), np.float32)
    for l in range(2):
        for a, name in enumerate(("lru_gate_a_w_2", "lru_gate_i_w_2")):
            for b in range(4):
                o = 64 * (b % 2)
                gates[l, o:o + 64, 2 * a + b // 2, o:o + 64] = p[name][l, b]
    arrays = {
        "wts": pack_weights(w),
        "xT": np.ascontiguousarray(p["x"][0].T.reshape(8, 128, 512).transpose(1, 0, 2)),
        "mT": np.ascontiguousarray(p["meta_tokens_2"].T.reshape(8, 128, META).transpose(1, 0, 2)),
        "pp": pack_params(p),
        "cst": c, "cstm": masks, "tA": np.ascontiguousarray(ta), "tR": np.ascontiguousarray(tr), "dech": dec,
        "biasT": np.ascontiguousarray(p["b_rel_bias"][0][:, idx]),
        "gates": gates,
    }
    nc = _bacc.Bacc("TRN2", target_bir_lowering=False, num_devices=1)
    args = [nc.dram_tensor("in_" + k, a.shape, mybir.dt.from_np(a.dtype), kind="ExternalInput").ap()
            for k, a in arrays.items()]
    args.append(nc.dram_tensor("out_0", (128, 8, 512), mybir.dt.float32, kind="ExternalOutput").ap())
    build(nc, *args)
    r = _run(nc, [{"in_" + k: a for k, a in arrays.items()}], core_ids=[0])
    o = r.results[0]["out_0"]
    return np.ascontiguousarray(o.transpose(1, 0, 2).reshape(1024, 512).T)[None]
```

```python
import math
from contextlib import ExitStack

import numpy as np
import concourse.bass as bass
from concourse import mybir

D = 1024
T = 528
META = 16
FF = 2816
NF = FF // 128
ALPHA = 4.0 ** 0.25
RAW = 3
NS = 3
NEG = -1.0e30


def unit_plan():
    plan = []

    def cols(name, c, nk=8, k0=0):
        plan.append((name, k0, nk, c, 128))

    def wide(name, c):
        plan.append((name, 0, 4, c, 256))
        plan.append((name, 4, 4, c, 256))

    def ffn(win, wout):
        for m in range(NF):
            cols(win, 128 * m)
            cols(win, FF + 128 * m)
        for m in range(8):
            for k0, nk in ((0, 8), (8, 8), (16, 6)):
                cols(wout, 128 * m, nk, k0)

    for g in range(4):
        for part in (0, 1):
            for j in range(2):
                cols("a_qkv", 1024 * part + 256 * g + 128 * j)
        wide("a_qkv", 2048 + 256 * g)
    for m in range(8):
        cols("a_o", 128 * m)
    ffn("f_in0", "f_out0")
    for g in range(4):
        for j in range(2):
            cols("b_q", 256 * g + 128 * j)
        for j in range(2):
            cols("kv", 256 * g + 128 * j)
        wide("kv", 1024 + 256 * g)
    for m in range(8):
        cols("b_o", 128 * m)
    ffn("f_in1", "f_out1")
    for l in range(2):
        w = f"m_in{l}"
        for h in range(4):
            for c in (1536, 0, 512):
                cols(w, c + 128 * h)
            if h == 0:
                wide(w, 1024)
                wide(w, 1280)
        cols(w, 2816)
        cols(w, 2944)
        wide(w, 2304)
        for c in (2560, 2048, 2176, 3072, 3200, 2688):
            cols(w, c)
        for m in range(8):
            cols(f"m_out{l}", 128 * m)
        ffn(f"g_in{l}", f"g_out{l}")
    return plan


def param_columns():
    at, n = {}, 0
    for name, k in (("ln_g", 32), ("ln_b", 32), ("subln", 1), ("lam", 256), ("nmix", 16), ("nffn", 16),
                    ("nfin", 8), ("lb", 8), ("hgn", 2), ("retn", 2), ("lcw", 16), ("lcb", 4), ("gab", 4),
                    ("gib", 4), ("lru", 4), ("fcw", 264), ("fcb", 88)):
        at[name] = n
        n += k
    return at, n


CI, CM, CG, CB, CPA, CPR, CE = 0, 128, 256, 384, 512, 640, 768
CN = 772


class Tok:

    def __init__(self, eng):
        self.eng, self.used, self.sem, self.val = eng, False, None, 0


def flatten(w):
    if isinstance(w, (list, tuple)):
        for x in w:
            yield from flatten(x)
    elif w is not None:
        yield w


def do(method, *args, **named):
    return method, args, named


class Queue:

    def __init__(self, name):
        self.name, self.items = name, []
        self.last = None

    def __call__(self, what, *waits):
        flat = list(flatten(waits))
        for w in flat:
            w.used = True
        t = Tok(self.name)
        self.items.append((what, flat, t))
        self.last = t
        return t


def build(nc, wts, xT, mT, pp, cst, cstm, tA, tR, dt_h, biasT, gates, out):
    F = mybir.dt.float32
    R = mybir.dt.float32r
    U8 = mybir.dt.uint8
    ALU = mybir.AluOpType
    ACT = mybir.ActivationFunctionType
    AX = mybir.AxisListType
    plan = unit_plan()
    pc, npp = param_columns()

    pe, act, dve, pool, sp = (Queue(n) for n in ("pe", "act", "dve", "pool", "sp"))
    ctx = ExitStack()
    with ctx:
        def sb(name, shape, dt=F, c=ctx):
            return c.enter_context(nc.sbuf_tensor(name, shape, dt))

        X = sb("X", [128, 8, T])
        XH = sb("XH", [128, 8, T], R)
        XL = sb("XL", [128, 8, T], R)
        raw = sb("raw", [128, RAW, 2048])
        WH = sb("WH", [128, NS, 1024], R)
        WL = sb("WL", [128, NS, 1024], R)
        PP = sb("PP", [128, npp])
        C = sb("C", [128, CN])
        rstd = sb("rstd", [128, T])
        small = sb("small", [128, 64])
        lbvs = [sb(f"lbv{l}", [128, 32]) for l in range(2)]
        P = ctx.enter_context(nc.psum_tensor("P", [128, 4096], F))

        sems = {n: ctx.enter_context(nc.semaphore("s_" + n)) for n in ("pe", "act", "dve", "pool")}
        raw_sem = [ctx.enter_context(nc.semaphore(f"s_raw{i}")) for i in range(RAW)]
        out_sem = ctx.enter_context(nc.semaphore("s_out"))
        nload = [0]
        issue = {"sp": nc.sync.dma_start, "act": nc.scalar.dma_start, "pool": nc.gpsimd.dma_start}

        def load(queue, dst, src, *waits):
            s = ctx.enter_context(nc.semaphore(f"s_ld{nload[0]}"))
            nload[0] += 1
            t = queue(do(issue[queue.name], dst, src), *waits)
            t.used, t.sem, t.val = False, s, 16
            return t

        ident = C[:, CI:CI + 128]
        ones_mean = C[:, CM:CM + 128]
        ones_head = C[:, CG:CG + 128]
        ones_ret = C[:, CB:CB + 128]
        perm_a = C[:, CPA:CPA + 128]
        perm_r = C[:, CPR:CPR + 128]
        mask_uv = sb("mask_uv", [1, 192], mybir.dt.bfloat16)
        mask_u = mask_uv[:, 0:128]
        mask_v = mask_uv[:, 128:192]
        eps5 = C[:, CE:CE + 1]
        eps6 = C[:, CE + 1:CE + 2]

        def par(name, i, n=1):
            return PP[:, pc[name] + i:pc[name] + i + n]

        ld_x = [load(act, X[:, k, META:T], xT[:, k, :]) for k in range(8)]
        ld_c = load(pool, C[:, :], cst)
        ld_p = load(pool, PP[:, :], pp)
        ld_m = load(pool, X[:, :, 0:META], mT)

        bank_free = [[] for _ in range(8)]

        mask_ready = [pool(do(nc.gpsimd.memset, mask_uv[:, 0:64], 1.0)),
                      pool(do(nc.gpsimd.memset, mask_uv[:, 64:128], 0.0)),
                      pool(do(nc.gpsimd.memset, mask_uv[:, 128:192], NEG))]

        def one(b):
            return P[:, 512 * b:512 * b + 512], [(512 * b, META, T)], [b]

        def two(p):
            a = 1024 * p + 248
            return P[:, a:a + T], [(a, 0, 264), (a + 264, 264, T)], [2 * p, 2 * p + 1]

        def take(banks):
            w = [t for b in banks for t in bank_free[b]]
            return w

        def release(banks, *toks):
            for b in banks:
                bank_free[b] = list(toks)

        raw_tok = {}
        raw_done = {}
        conv = {}
        pe_done = {}
        st = {"conv": 0, "cur": -1, "load": 0, "share": False}

        def length(u):
            return plan[u][2] * plan[u][4]

        def load_chunks(upto):
            while st["load"] <= upto and 2 * st["load"] < len(plan):
                c = st["load"]
                n = length(2 * c) + length(2 * c + 1)
                s = c % RAW
                t = sp(do(nc.sync.dma_start, raw[:, s, 0:n], wts[c, :, 0:n]),
                       raw_done.get(c - RAW))
                t.sem, t.val = raw_sem[s], 16 * (c // RAW + 1)
                raw_tok[c] = t
                st["load"] += 1

        def convert(u):
            c, s = u // 2, u % NS
            load_chunks(c)
            a = length(u - 1) if u % 2 else 0
            n = length(u)
            src = raw[:, c % RAW, a:a + n]
            th = act(do(nc.scalar.activation, WH[:, s, 0:n], src, ACT.Copy), raw_tok[c], pe_done.get(u - NS))
            if st["share"] and u % 2:
                tl = pool(do(nc.gpsimd.tensor_tensor, WL[:, s, 0:n], src, WH[:, s, 0:n].bitcast(F), ALU.subtract), th)
            else:
                tl = dve(do(nc.vector.tensor_tensor, WL[:, s, 0:n], src, WH[:, s, 0:n].bitcast(F), ALU.subtract), th)
            conv[u] = [th, tl]
            raw_done.setdefault(c, []).append(tl)

        def need(u):
            while st["conv"] <= u:
                convert(st["conv"])
                st["conv"] += 1

        def run_ahead():
            while st["conv"] < min(len(plan), st["cur"] + NS):
                convert(st["conv"])
                st["conv"] += 1

        background = []

        def step():
            if background:
                g = background.pop(0)
                try:
                    next(g)
                    background.append(g)
                except StopIteration:
                    pass

        def drain():
            while background:
                step()

        soon = []
        pace = {"rate": 0.6, "due": 0.0}

        def tick(w=1.0):
            while soon:
                soon.pop(0)()
            pace["due"] = min(pace["due"] + w * pace["rate"], 3.0)
            while pace["due"] >= 1.0:
                pace["due"] -= 1.0
                step()

        def product(units, xh, xl, xready, region, lo_col=0):
            ap, segs, banks = region
            w0 = take(banks)
            kt = 0
            total = sum(plan[u][2] for u in units)
            for u in units:
                need(u)
                s = u % NS
                wt = conv[u]
                for k in range(plan[u][2]):
                    for i, (wb, xb) in enumerate(((WL, xh), (WH, xl), (WH, xh))):
                        for a, c0, c1 in segs:
                            first = kt == 0 and i == 0
                            lastm = kt == total - 1 and i == 2
                            t = pe(do(nc.tensor.matmul, P[:, a:a + c1 - c0], wb[:, s, 128 * k:128 * k + 128],
                                            xb[:, kt, c0 - lo_col:c1 - lo_col], start=first, stop=lastm),
                                   w0, wt, xready[kt])
                            w0, wt = None, None
                    kt += 1
                    tick()
                pe_done[u] = t
                st["cur"] = u
                run_ahead()
            return t

        def products(us, xh, xl, xready, regions, lo_col=0):
            need(us[-1])
            toks = [None] * len(us)
            wr = [take(r[2]) + conv[u] for u, r in zip(us, regions)]
            for k in range(8):
                for n, (u, (_, segs, _)) in enumerate(zip(us, regions)):
                    s = u % NS
                    for i, (wb, xb) in enumerate(((WL, xh), (WH, xl), (WH, xh))):
                        for a, c0, c1 in segs:
                            toks[n] = pe(do(nc.tensor.matmul, P[:, a:a + c1 - c0], wb[:, s, 128 * k:128 * k + 128],
                                            xb[:, k, c0 - lo_col:c1 - lo_col], start=(k == 0 and i == 0),
                                            stop=(k == 7 and i == 2)), wr[n], xready[k])
                    wr[n] = None
                tick()
            for u, t in zip(us, toks):
                pe_done[u] = t
            st["cur"] = us[-1]
            run_ahead()
            return toks

        def wide_product(u, tiles, region_of, consume, xready):
            need(u + 1)
            for n, (c0, c1) in enumerate(tiles):
                o, banks = region_of(n)
                w0 = take(banks)
                for k in range(8):
                    s, kk = (u + k // 4) % NS, k % 4
                    for i, (xb, wb) in enumerate(((XL, WH), (XH, WL), (XH, WH))):
                        t = pe(do(nc.tensor.matmul, o, xb[:, k, c0:c1], wb[:, s, 256 * kk:256 * kk + 256],
                                        start=(k == 0 and i == 0), stop=(k == 7 and i == 2)),
                               w0, conv[u], conv[u + 1], xready[k])
                        w0 = None
                    tick(0.5)
                release(banks, *consume(n, o, t))
            pe_done[u] = pe_done[u + 1] = t
            st["cur"] = u + 1
            run_ahead()

        unit = [0]

        def units(n):
            u = unit[0]
            unit[0] += n
            return list(range(u, u + n))

        def ones_sum(m, src, region, first, last, waits, lo_col=0):
            ap, segs, banks = region
            for a, c0, c1 in segs:
                t = pe(do(nc.tensor.matmul, P[:, a:a + c1 - c0], m, src[:, c0 - lo_col:c1 - lo_col],
                                                             start=first, stop=last), waits)
            return t

        def inv_root(dst, src, eps, waits):
            a = act(do(nc.scalar.activation, dst, src, ACT.Ln, bias=eps), waits)
            return a, act(do(nc.scalar.activation, dst, dst, ACT.Exp, scale=-0.5), a)

        def split(src, h, l, waits, hw):
            th = act(do(nc.scalar.activation, h, src, ACT.Copy), waits, hw)
            tl = dve(do(nc.vector.tensor_tensor, l, src, h.bitcast(F), ALU.subtract), th, waits, hw)
            return th, tl

        tmp = [sb(f"tmp{i}", [128, T]) for i in range(4)]
        tmp_free = [[] for _ in range(4)]
        tmp_at = [0]

        def temp():
            i = tmp_at[0] % 4
            tmp_at[0] += 1
            return i, tmp[i], tmp_free[i]

        C1 = slice(META, T)
        xr = [None] * 8
        x_done = [[ld_x, ld_m, ld_c, ld_p]] * 8
        need(0)
        for k in range(8):
            th, tl = split(X[:, k, C1], XH[:, k, C1], XL[:, k, C1], [ld_x[k]], None)
            xr[k] = [th, tl]
            if k in (1, 3):
                need((k + 1) // 2)

        def ln_exp_tables():
            act(do(nc.scalar.preload_act_table_set, "natural_log_exp_and_others"))

        def residual_ln(l, j, tiles):
            g0 = pc["ln_g"] + 16 * l + 8 * j
            b0 = pc["ln_b"] + 16 * l + 8 * j
            mean = one(6)
            var = one(7)
            evac = []
            feeds = not (l == 1 and j == 1)
            ln_exp_tables()

            def sum_tile(m):
                w = [evac[m], ld_c] + (take(mean[2]) if m == 0 else [])
                return ones_sum(ones_mean, X[:, m, :], mean, m == 0, m == 7, w)

            for m in range(8):
                r = one(m % 3)
                t = tiles(m, r)
                v = dve(do(nc.vector.scalar_tensor_tensor, X[:, m, C1], X[:, m, C1], float(ALPHA), r[0],
                                                                   ALU.mult, ALU.add), t, x_done[m])
                release(r[2], v)
                evac.append(v)
                if m >= 1:
                    tm = sum_tile(m - 1)
            tm = sum_tile(7)
            wv = take(var[2])
            cen = []
            for m in range(8):
                c = dve(do(nc.vector.tensor_tensor, X[:, m, C1], X[:, m, C1], mean[0], ALU.subtract), tm, evac[m])
                cen.append(c)
                i, q, fr = temp()
                s = act(do(nc.scalar.activation, q[:, C1], X[:, m, C1], ACT.Square), c, fr)
                tv = ones_sum(ones_mean, q, var, m == 0, m == 7, [s] + wv)
                wv = []
                tmp_free[i] = [tv]
            release(mean[2], cen[-1])
            need(st["cur"] + NS)
            tl_, te = inv_root(rstd[:, C1], var[0], eps5, [tv, ld_c, rstd_free])
            release(var[2], tl_)
            dn = []
            for m in range(8):
                i, q, fr = temp()
                a = dve(do(nc.vector.tensor_tensor, q[:, C1], X[:, m, C1], rstd[:, C1], ALU.mult), te, cen[m], fr)
                h = feeds and act(do(nc.scalar.activation, XH[:, m, C1], q[:, C1], ACT.Identity,
                                     bias=PP[:, b0 + m:b0 + m + 1], scale=PP[:, g0 + m:g0 + m + 1]), a, x_read)
                f = act(do(nc.scalar.activation, X[:, m, C1], q[:, C1], ACT.Identity, bias=PP[:, b0 + m:b0 + m + 1],
                                                         scale=PP[:, g0 + m:g0 + m + 1]), a)
                tmp_free[i] = [f]
                x_done[m] = [f]
                if feeds:
                    d = dve(do(nc.vector.tensor_tensor, XL[:, m, C1], X[:, m, C1], XH[:, m, C1].bitcast(F), ALU.subtract),
                            f, h, x_read)
                    x_done[m] = [f, d, h]
                    xr[m] = [h, d]
            rstd_free[:] = [a]

        rstd_free = []
        x_read = []

        def phase_fence():
            return [q.last for q in (pe, act, dve)]

        ph = ExitStack()
        QT = [sb(f"QT{i}", [128, 2, 512], F, ph) for i in range(2)]
        KT = [sb(f"KT{i}", [128, 2, 512], F, ph) for i in range(2)]
        VN = [sb(f"VN{i}", [128, 4, 256], F, ph) for i in range(2)]
        OH = sb("OH", [128, 8, 512], R, ph)
        OL = sb("OL", [128, 8, 512], R, ph)
        cosA = sb("cosA", [128, 2, 512], F, ph)
        qraw = [sb(f"qraw{i}", [128, 512], F, ph) for i in range(2)]
        pr = [sb(f"pr{i}", [128, 2, 512], F, ph) for i in range(2)]
        aTs = [sb(f"aT{i}", [128, 4, 512], F, ph) for i in range(2)]
        ld_t = load(pool, cosA[:, :, :], tA)

        lv = PP[:, pc["lam"]:pc["lam"] + 256]
        t0 = dve(do(nc.vector.tensor_tensor, qraw[0][:, 0:64], lv[:, 0:64], lv[:, 64:128], ALU.mult), ld_p)
        t1 = dve(do(nc.vector.tensor_tensor, qraw[0][:, 64:128], lv[:, 128:192], lv[:, 192:256], ALU.mult), ld_p)
        t2 = dve(do(nc.vector.tensor_reduce, small[:, 0:2], qraw[0][:, 0:128].rearrange("p (a b) -> p a b", a=2), AX.X, ALU.add), t0, t1)
        t3 = act(do(nc.scalar.activation, small[:, 0:2], small[:, 0:2], ACT.Exp), t2)
        t4 = dve(do(nc.vector.tensor_tensor, small[:, 2:3], small[:, 1:2], small[:, 0:1], ALU.subtract), t3)
        lam_init = 0.8 - 0.6 * math.exp(0.0)
        neglam = dve(do(nc.vector.tensor_scalar, small[:, 2:3], small[:, 2:3], -lam_init, None, ALU.add), t4)
        g8 = dve(do(nc.vector.tensor_scalar, small[:, 3:4], par("subln", 0), 1.0 - lam_init, None, ALU.mult), ld_p)

        qraw_free = [[t2], []]
        nrope = [0]

        def rope_tile(region, t, dst, dst_free, scale, table, perm, C0, prm_region):
            while len(soon) > 1:
                soon.pop(0)()
            i = nrope[0] % 2
            nrope[0] += 1
            q = qraw[i]
            n = C0[1] - C0[0]
            a = act(do(nc.scalar.activation, q[:, 0:n], region[0], ACT.Copy, scale=scale), t, qraw_free[i])
            release(region[2], a)
            out = []

            def rest():
                out.append(rope_rest(region, i, q, n, a, dst, dst_free, table, perm, C0, prm_region))

            soon.append(rest)
            return out

        def rope_rest(region, i, q, n, a, dst, dst_free, table, perm, C0, prm_region):
            t_sw = ones_sum(perm, q, prm_region, True, True, [a] + take(prm_region[2]) + [ld_c], C0[0])
            j, w, fr = temp()
            b = dve(do(nc.vector.tensor_tensor, w[:, 0:n], q[:, 0:n], table[:, 0, :], ALU.mult), a, fr, ld_t)
            c = dve(do(nc.vector.tensor_tensor, dst, prm_region[0], table[:, 1, :], ALU.mult), t_sw, dst_free, ld_t)
            release(prm_region[2], c)
            d = dve(do(nc.vector.tensor_tensor, dst, dst, w[:, 0:n], ALU.add), b, c)
            tmp_free[j] = [d]
            qraw_free[i] = [b, t_sw]
            return d

        layer_const = []

        def decays(l):
            lbv = lbvs[l]
            if l == 0:
                z0 = dve(do(nc.vector.memset, lbv[:, 0:4], 0.0), ld_p)
                z1 = dve(do(nc.vector.memset, lbv[:, 4:8], 1.0), ld_p)
                lb_ready = [z0, z1]
            else:
                l0, l1 = par("lb", 0, 4), par("lb", 4, 4)
                z0 = dve(do(nc.vector.tensor_tensor, lbv[:, 8:12], l0, l1, ALU.max), ld_p)
                z1 = dve(do(nc.vector.tensor_tensor, lbv[:, 12:16], l0, lbv[:, 8:12], ALU.subtract), z0)
                z2 = dve(do(nc.vector.tensor_tensor, lbv[:, 16:20], l1, lbv[:, 8:12], ALU.subtract), z0)
                z3 = act(do(nc.scalar.activation, lbv[:, 12:20], lbv[:, 12:20], ACT.Exp), z1, z2)
                z4 = dve(do(nc.vector.tensor_tensor, lbv[:, 20:24], lbv[:, 12:16], lbv[:, 16:20], ALU.add), z3)
                z5 = dve(do(nc.vector.reciprocal, lbv[:, 20:24], lbv[:, 20:24]), z4)
                z6 = dve(do(nc.vector.tensor_tensor, lbv[:, 0:4], lbv[:, 16:20], lbv[:, 20:24], ALU.mult), z5)
                z7 = dve(do(nc.vector.tensor_tensor, lbv[:, 4:8], lbv[:, 12:16], lbv[:, 20:24], ALU.mult), z5)
                lb_ready = [z6, z7]
            lam = par("lru", 2 * l, 2)
            a0 = dve(do(nc.vector.tensor_scalar, lbv[:, 24:26], lam, -1.0, 0.0, ALU.mult, ALU.max), ld_p)
            a1 = dve(do(nc.vector.tensor_scalar, lbv[:, 26:28], lam, -1.0, None, ALU.mult), ld_p)
            a2 = dve(do(nc.vector.tensor_tensor, lbv[:, 26:28], lbv[:, 26:28], lam, ALU.min), a1)
            a3 = act(do(nc.scalar.activation, lbv[:, 26:28], lbv[:, 26:28], ACT.Exp), a2)
            a4 = dve(do(nc.vector.tensor_scalar, lbv[:, 28:30], lbv[:, 26:28], 2.0, None, ALU.add), a3)
            a5 = dve(do(nc.vector.reciprocal, lbv[:, 28:30], lbv[:, 28:30]), a4)
            a6 = dve(do(nc.vector.tensor_tensor, lbv[:, 26:28], lbv[:, 26:28], lbv[:, 28:30], ALU.mult), a5)
            a7 = dve(do(nc.vector.tensor_tensor, lbv[:, 28:30], lbv[:, 26:28], lbv[:, 26:28], ALU.mult), a6)
            t = dve(do(nc.vector.tensor_scalar, lbv[:, 30:32], lbv[:, 28:30], 1.0 / 17, 1.0 / 15, ALU.mult, ALU.add), a7)
            for n in (13, 11, 9, 7, 5, 3, 1):
                t = dve(do(nc.vector.tensor_tensor, lbv[:, 30:32], lbv[:, 30:32], lbv[:, 28:30], ALU.mult), t)
                t = dve(do(nc.vector.tensor_scalar, lbv[:, 30:32], lbv[:, 30:32], 1.0 / n, None, ALU.add), t)
            t = dve(do(nc.vector.tensor_tensor, lbv[:, 30:32], lbv[:, 30:32], lbv[:, 26:28], ALU.mult), t)
            t = dve(do(nc.vector.tensor_scalar, lbv[:, 30:32], lbv[:, 30:32], 2.0, None, ALU.mult), t)
            t = dve(do(nc.vector.tensor_tensor, lbv[:, 30:32], lbv[:, 30:32], lbv[:, 24:26], ALU.add), t)
            a8 = dve(do(nc.vector.tensor_scalar, lbv[:, 24:26], lbv[:, 30:32], 8.0, None, ALU.mult), t)
            sp_ready = dve(do(nc.vector.tensor_scalar, lbv[:, 26:28], lbv[:, 24:26], -1.0, None, ALU.mult), a8)
            layer_const.append((lb_ready, sp_ready))

        qk_free = [[], []]
        v_free = [[], []]
        pr_free = [[], []]
        aT_free = [[], []]
        o_ready = [None] * 8
        nat = [(META + 128 * i, META + 128 * i + 128) for i in range(4)]

        def nat_region(n):
            b = 7 if n // 2 == 0 else 6
            return P[:, 512 * b + 256 * (n % 2):512 * b + 256 * (n % 2) + 256], [b]

        def transposes(i, src, aT, bank, waits, afree):
            w = take([bank]) + waits
            for j in range(i + 1):
                t = pe(do(nc.tensor.transpose, P[:, 512 * bank + 128 * j:512 * bank + 128 * j + 128],
                                                  src[:, 128 * j:128 * j + 128], ident), w)
            v = act(do(nc.scalar.activation, aT[:, 0:i + 1, 128 * i:128 * i + 128],
                                           P[:, 512 * bank:512 * bank + 128 * (i + 1)].rearrange("p (j c) -> p j c", c=128),
                                           ACT.Copy), t, afree)
            release([bank], v)
            return t, v

        def attn_a(h, g, lane, qk_ready, v_ready):
            b0 = 2 + 2 * lane
            Q, K, V = QT[g % 2], KT[g % 2], VN[g % 2]
            hh = h % 2
            p, aT = pr[lane], aTs[lane]
            sm = small[:, 8 + 12 * lane:20 + 12 * lane]
            ev = []
            sfree = []
            for i in range(4):
                ke = 128 * (i + 1)
                w = take([b0, b0 + 1]) + qk_ready + [ld_c]
                for m in range(2):
                    o = 512 * (b0 + m)
                    pe(do(nc.tensor.matmul, P[:, o:o + ke], Q[64 * m:64 * m + 64, hh, 128 * i:128 * i + 128],
                                                                K[64 * m:64 * m + 64, hh, 0:ke], start=True, stop=False), w)
                    t = pe(do(nc.tensor.matmul, P[:, o + ke - 64:o + ke], mask_u, mask_v, start=False, stop=True), mask_ready)
                both = P[:, 512 * b0:512 * b0 + 1024].rearrange("p (m c) -> p m c", m=2)[:, :, 0:ke]
                a = dve(do(nc.vector.tensor_reduce, sm[:, 0:2], both, AX.X, ALU.max, negate=True), t, sfree)
                for m in range(2):
                    x = act(do(nc.scalar.activation, p[:, m, 0:ke], P[:, 512 * (b0 + m):512 * (b0 + m) + ke], ACT.Exp,
                                                               bias=sm[:, m:m + 1], accum_out=sm[:, 2 + m:3 + m]),
                            a, pr_free[lane])
                release([b0, b0 + 1], x)
                r = dve(do(nc.vector.reciprocal, sm[:, 4:6], sm[:, 2:4]), x)
                r1 = dve(do(nc.vector.tensor_tensor, sm[:, 6:7], sm[:, 5:6], small[:, 2:3], ALU.mult), r, neglam)
                c = dve(do(nc.vector.tensor_scalar, p[:, 0, 0:ke], p[:, 0, 0:ke], sm[:, 4:5], None, ALU.mult), r)
                c = dve(do(nc.vector.scalar_tensor_tensor, p[:, 0, 0:ke], p[:, 1, 0:ke], sm[:, 6:7], p[:, 0, 0:ke],
                                                                ALU.mult, ALU.add), c, r1)
                sfree = [c]
                yield
                yield
                t, v = transposes(i, p[:, 0, :], aT, b0, [c], aT_free[lane])
                pr_free[lane] = [t]
                ev.append(v)
                yield
            w = take([b0 + 1]) + ev + v_ready
            o = 512 * (b0 + 1)
            for j in range(4):
                t = pe(do(nc.tensor.matmul, P[:, o + 128 * j:o + 512], V[:, j, 128 * hh:128 * hh + 128],
                                               aT[:, j, 128 * j:512], start=(j == 0), stop=(j == 3)), w)
            aT_free[lane] = [t]
            att_last[lane] = t
            yield
            i1, q, fr = temp()
            s = act(do(nc.scalar.activation, q[:, 0:512], P[:, o:o + 512], ACT.Square), t, fr)
            yield
            t_ms = pe(do(nc.tensor.matmul, P[:, 512 * b0:512 * b0 + 512], ones_head, q[:, 0:512], start=True, stop=True),
                      s, take([b0]))
            yield
            a, b = inv_root(q[:, 0:512], P[:, 512 * b0:512 * b0 + 512], eps5, [t_ms])
            release([b0], a)
            n = dve(do(nc.vector.scalar_tensor_tensor, q[:, 0:512], P[:, o:o + 512], small[:, 3:4], q[:, 0:512],
                                                     ALU.mult, ALU.mult), b, g8)
            release([b0 + 1], n)
            th, tl = split(q[:, 0:512], OH[:, h, :], OL[:, h, :], [n], None)
            tmp_free[i1] = [th, tl]
            o_ready[h] = [th, tl]

        att_last = [None, None]
        pace["rate"] = 0.7
        for g in range(4):
            ready = []
            early = products(units(3), XH, XL, xr, [one(0), one(1), one(2)]) if g == 0 else []
            for part, dst in ((0, QT), (1, KT)):
                for j in range(2):
                    n = 2 * part + j
                    if early and n < 3:
                        r, t = one(n), early[n]
                    else:
                        r = one(n % 2)
                        t = product(units(1), XH, XL, xr, r)
                    if g == 0 and n == 3:
                        decays(0)
                        decays(1)
                    ready.append(rope_tile(r, t, dst[g % 2][:, j, :], qk_free[g % 2], 0.125 if part == 0 else 1.0,
                                           cosA, perm_a, (META, T), one(6)))
            vt = []

            def keep_v(n, o, t, g=g, vt=vt):
                v = act(do(nc.scalar.activation, VN[g % 2][:, n, :], o, ACT.Copy), t, v_free[g % 2])
                vt.append(v)
                return [v]

            u = units(2)
            wide_product(u[0], nat, nat_region, keep_v, xr)
            drain()
            qk_free[(g + 1) % 2] = [x for x in att_last if x]
            v_free[(g + 1) % 2] = [x for x in att_last if x]
            background.append(attn_a(2 * g, g, 0, ready, vt))
            background.append(attn_a(2 * g + 1, g, 1, ready, vt))
        drain()
        x_read[:] = [pe_done[unit[0] - 1]]

        residual_ln(0, 0, lambda m, r: product(units(1), OH, OL, o_ready, r, lo_col=META))
        ph.close()

        def swiglu(l):
            ph = ExitStack()
            fence = phase_fence()
            HH = sb(f"HH{l}", [128, NF, 512], R, ph)
            HL = sb(f"HL{l}", [128, NF, 512], R, ph)
            hr = []
            early = products(units(3), XH, XL, xr, [one(0), one(1), one(2)])

            def tile(n):
                r = one(n % 4)
                return r, early[n] if n < 3 else product(units(1), XH, XL, xr, r)

            for m in range(NF):
                rg, tg = tile(2 * m)
                i, q, fr = temp()
                a = act(do(nc.scalar.activation, q[:, 0:512], rg[0], ACT.Silu), tg, fr)
                release(rg[2], a)
                ru, tu = tile(2 * m + 1)
                b = dve(do(nc.vector.tensor_tensor, q[:, 0:512], q[:, 0:512], ru[0], ALU.mult), a, tu)
                release(ru[2], b)
                th, tl = split(q[:, 0:512], HH[:, m, :], HL[:, m, :], [b], fence)
                tmp_free[i] = [th, tl]
                hr.append([th, tl])
            x_read[:] = [pe_done[unit[0] - 1]]
            residual_ln(l, 1, lambda m, r: product(units(3), HH, HL, hr, r, lo_col=META))
            ph.close()

        swiglu(0)

        ph = ExitStack()
        fence = phase_fence()
        QB = [sb(f"QB{i}", [128, 2, 512], F, ph) for i in range(2)]
        KB_ = [sb(f"KB{i}", [128, 2, 512], F, ph) for i in range(2)]
        VB = [sb(f"VB{i}", [128, 4, 256], F, ph) for i in range(2)]
        OH2 = sb("OH2", [128, 8, 512], R, ph)
        OL2 = sb("OL2", [128, 8, 512], R, ph)
        bT = sb("bT", [128, 4, 512], F, ph)
        prB = [sb(f"prB{i}", [128, 512], F, ph) for i in range(2)]
        aTB = [sb(f"aTB{i}", [128, 4, 512], F, ph) for i in range(2)]
        oB = [sb(f"oB{i}", [128, 512], F, ph) for i in range(2)]
        pr_free = [fence, fence]
        aT_free = [fence, fence]
        bt_free = [fence] * 4
        qk_free = [fence, fence]
        v_free = [fence, fence]
        ob_free = [fence, fence]
        att_last = [None, None]
        o_ready = [None] * 8

        def attn_b(tile, g, lane, qk_ready, v_ready):
            b0 = 2 + 2 * lane
            Q, K, V = QB[g % 2], KB_[g % 2], VB[g % 2]
            hh = tile % 2
            p, aT = prB[lane], aTB[lane]
            sm = small[:, 8 + 12 * lane:20 + 12 * lane]
            sfree = []
            oe = []
            for half in range(2):
                h = 2 * tile + half
                s0 = 64 * half
                slot = 2 * lane + half
                ld_b = load(pool, bT[:, slot, :], biasT[h, :, :], bt_free[slot])
                ev = []
                for i in range(4):
                    ke = 128 * (i + 1)
                    o = 512 * b0
                    pe(do(nc.tensor.matmul, P[:, o:o + ke], Q[s0:s0 + 64, hh, 128 * i:128 * i + 128],
                                                                  K[s0:s0 + 64, hh, 0:ke], start=True, stop=False),
                       take([b0]) + qk_ready)
                    t = pe(do(nc.tensor.matmul, P[:, o + ke - 64:o + ke], mask_u, mask_v, start=False, stop=True), mask_ready)
                    c = dve(do(nc.vector.tensor_tensor, p[:, 0:ke], P[:, o:o + ke], bT[:, slot, 512 - ke:512], ALU.add), t, pr_free[lane], ld_b)
                    release([b0], c)
                    a = dve(do(nc.vector.tensor_reduce, sm[:, 0:1], p[:, 0:ke], AX.X, ALU.max, negate=True), c, sfree)
                    x = act(do(nc.scalar.activation, p[:, 0:ke], p[:, 0:ke], ACT.Exp, bias=sm[:, 0:1],
                                                          accum_out=sm[:, 2:3]), a)
                    r = dve(do(nc.vector.reciprocal, sm[:, 4:5], sm[:, 2:3]), x)
                    c = dve(do(nc.vector.tensor_scalar, p[:, 0:ke], p[:, 0:ke], sm[:, 4:5], None, ALU.mult), r)
                    sfree = [c]
                    yield
                    yield
                    t, v = transposes(i, p, aT, b0, [c], aT_free[lane])
                    pr_free[lane] = [t]
                    ev.append(v)
                    yield
                bt_free[slot] = [c]
                o = 512 * (b0 + 1)
                w = take([b0 + 1]) + ev + v_ready
                for j in range(4):
                    t = pe(do(nc.tensor.matmul, P[s0:s0 + 64, o + 128 * j:o + 512],
                                                          V[:, j, 128 * hh + s0:128 * hh + s0 + 64],
                                                          aT[:, j, 128 * j:512], start=(j == 0), stop=(j == 3)), w)
                aT_free[lane] = [t]
                yield
                oe.append(t)
            att_last[lane] = t
            ob = oB[lane]
            a = act(do(nc.scalar.activation, ob[:, :], P[:, o:o + 512], ACT.Copy), oe, ob_free[lane])
            release([b0 + 1], a)
            th, tl = split(ob[:, :], OH2[:, tile, :], OL2[:, tile, :], [a], fence)
            ob_free[lane] = [th, tl]
            o_ready[tile] = [th, tl]

        for g in range(4):
            ready = []
            early = products(units(3), XH, XL, xr, [one(0), one(1), one(2)]) if g == 0 else []
            for part, dst in ((0, QB), (1, KB_)):
                for j in range(2):
                    n = 2 * part + j
                    if early and n < 3:
                        r, t = one(n), early[n]
                    else:
                        r = one(n % 2)
                        t = product(units(1), XH, XL, xr, r)
                    a = act(do(nc.scalar.activation, dst[g % 2][:, j, :], r[0], ACT.Copy, scale=0.125 if part == 0 else 1.0), t, qk_free[g % 2])
                    release(r[2], a)
                    ready.append(a)
            vt = []

            def keep_vb(n, o, t, g=g, vt=vt):
                v = act(do(nc.scalar.activation, VB[g % 2][:, n, :], o, ACT.Copy), t, v_free[g % 2])
                vt.append(v)
                return [v]

            u = units(2)
            wide_product(u[0], nat, nat_region, keep_vb, xr)
            drain()
            qk_free[(g + 1) % 2] = [x for x in att_last if x] or fence
            v_free[(g + 1) % 2] = [x for x in att_last if x] or fence
            background.append(attn_b(2 * g, g, 0, ready, vt))
            background.append(attn_b(2 * g + 1, g, 1, ready, vt))
        drain()
        x_read[:] = [pe_done[unit[0] - 1]]
        residual_ln(1, 0, lambda m, r: product(units(1), OH2, OL2, o_ready, r, lo_col=META))
        ph.close()
        swiglu(1)

        squares = {}

        def add_square(m):
            i, q, fr = temp()
            squares[m] = (i, q, act(do(nc.scalar.activation, q[:, :], X[:, m, :], ACT.Square), x_done[m], fr))

        def sum_square(m):
            i, q, s = squares.pop(m)
            ms = two(3)
            t = ones_sum(ones_mean, q, ms, m == 0, m == 7, [s, ld_c] + (take(ms[2]) if m == 0 else []))
            tmp_free[i] = [t]
            squares["all"] = t

        def rms(g0, final=False):
            ms = two(3)
            if not final:
                need(st["cur"] + NS)
            a, b = inv_root(rstd[:, :], ms[0], eps6, [squares.pop("all"), rstd_free])
            release(ms[2], a)
            for m in range(8):
                i, q, fr = temp()
                n = dve(do(nc.vector.scalar_tensor_tensor, q[:, :], X[:, m, :], PP[:, g0 + m:g0 + m + 1], rstd[:, :],
                           ALU.mult, ALU.mult), b, fr, x_done[m])
                if final:
                    tok = load(sp, out[:, m, :], q[:, C1], n)
                    outs.append(tok)
                    tmp_free[i] = [tok]
                else:
                    th, tl = split(q[:, :], XH[:, m, :], XL[:, m, :], [n], x_read)
                    tmp_free[i] = [th, tl]
                    xr[m] = [th, tl]
            rstd_free[:] = [n]

        def residual(tiles, pairs):
            ln_exp_tables()
            for m in range(8):
                r = two(m % pairs)
                t = tiles(m, r)
                v = dve(do(nc.vector.tensor_tensor, X[:, m, :], X[:, m, :], r[0], ALU.add), t, x_done[m])
                release(r[2], v)
                x_done[m] = [v]
                if m:
                    sum_square(m - 1)
                add_square(m)
            sum_square(7)

        outs = []
        nat5 = [(0, META)] + nat

        def mixer(l):
            ph = ExitStack()
            fence = phase_fence()
            GH = sb(f"GH{l}", [128, 8, T], R, ph)
            GL = sb(f"GL{l}", [128, 8, T], R, ph)
            VI = sb(f"VI{l}", [128, 5, 512], F, ph)
            VR = sb(f"VR{l}", [128, 5, 256], F, ph)
            maskw = sb(f"masks{l}", [128, 256], mybir.dt.int32, ph)
            masks = maskw[:, :].bitcast(U8).rearrange("p (l c) -> p l c", l=8)
            SC = sb(f"SC{l}", [128, 2560], F, ph)
            SM = sb(f"SM{l}", [16, T], F, ph)
            A, B, K, Q0, G, QA, KB = (sb(f"{n}{l}", [128, T], F, ph) for n in ("hA", "hB", "hK", "hQ", "hG", "hQA", "hKB"))
            Qs = (Q0, rstd)
            G2 = sb(f"hG2{l}", [128, T], F, ph)
            tab = sb(f"tab{l}", [128, 2, T], F, ph)
            dec = [sb(f"dec{l}{i}", [128, T], F, ph) for i in range(2)]
            gw = sb(f"gw{l}", [128, 4, 128], F, ph)
            LX = sb(f"LX{l}", [128, 2, T + 3], F, ph)
            ld_mask = load(pool, maskw[:, :], cstm, fence)
            ld_tab = load(pool, tab[:, :, :], tR, fence)
            ld_gw = load(pool, gw[:, :, :], gates[l, :, :, :], fence)
            first = {}

            def fr(name):
                if name in first:
                    return first[name]
                return fence

            lb_ready, sp_ready = layer_const[l]
            lbv = lbvs[l]
            sc_zero = pool(do(nc.gpsimd.memset, SC[:, :], 0.0), fence)
            sm_zero = pool(do(nc.gpsimd.memset, SM[:, :], 0.0), fence)
            lx_zero = pool(do(nc.gpsimd.memset, LX[:, :, 0:3], 0.0), fence)
            first["SC"] = [sc_zero]
            first["SM"] = [sm_zero]

            rot = [0]
            st["share"] = True
            pace["rate"] = 0.65

            def region():
                rot[0] += 1
                return two(rot[0] % 2)

            vi_ready, vr_ready = [], []

            def nat5_region(n):
                b = 2 * (n % 2) + (n // 2) % 2
                return P[0:(16 if n == 0 else 128), 512 * b:512 * b + 256], [b]

            def keep(dst, c0, lst):
                def f(n, o, t):
                    k = 16 if n == 0 else 128
                    v = act(do(nc.scalar.activation, dst[0:k, n, c0:c0 + 256], o, ACT.Copy), t, fence)
                    lst.append(v)
                    return [v]
                return f

            def out_split(src, k, waits, ti):
                th, tl = split(src, GH[:, k, :], GL[:, k, :], waits, fence)
                if ti is not None:
                    tmp_free[ti] = [th, tl]
                g_ready[k] = [th, tl]
                return [th, tl]

            g_ready = [None] * 8

            def segments(c0, c1):
                return [(a, b) for a, b in ((c0, min(c1, 264)), (max(c0, 264), c1)) if a < b]

            def level(src, sz, c0, c1):
                return src[:, c0:c1].rearrange("p (n h s) -> p n h s", h=2, s=sz)

            QAs, KBs = (QA, dec[0]), (KB, dec[1])
            qb_free = [fence, fence]

            def hgrn(h, toks):
                zA, zK, zQ, zG = toks
                Q = Qs[h % 2]
                Gb = (G, G2)[h % 2]
                now = {"A": zA, "B": pool(do(nc.gpsimd.memset, B[:, :], 1.0), fr("B"))}
                scd = SC[:, 0:2560].rearrange("p (j c) -> p j c", c=640)[:, :, 0:128]
                done = []

                def prep(lev):
                    if lev < 0:
                        return Q, K, [zQ, zK]
                    b, sz, c0 = lev % 2, 1 << lev, 0 if lev < 4 else META
                    qa, kb = QAs[b], KBs[b]
                    Av, Bv, Qv, Kv, QAv, KBv = (level(x, sz, c0, T) for x in (A, B, Q, K, qa, kb))
                    if lev < 2:
                        d1 = dve(do(nc.vector.tensor_tensor, qa[:, :], Q[:, :], A[:, :], ALU.mult), now["A"], zQ, qb_free[b])
                    else:
                        d1 = dve(do(nc.vector.tensor_tensor, QAv[:, :, 1, :], Qv[:, :, 1, :], Av[:, :, 1, :], ALU.mult),
                                 now["A"], zQ, qb_free[b])
                    if lev == 0:
                        kb, d2 = K, zK
                    elif lev < 3:
                        d2 = dve(do(nc.vector.tensor_tensor, kb[:, :], K[:, :], B[:, :], ALU.mult), now["B"], zK, qb_free[b])
                    else:
                        d2 = dve(do(nc.vector.tensor_tensor, KBv[:, :, 0, :], Kv[:, :, 0, :], Bv[:, :, 0, :], ALU.mult),
                                 now["B"], zK, qb_free[b])
                    nb = (T - c0) // (2 * sz)
                    if lev < 8:
                        ea = Av[:, :, 1, sz - 1:sz].broadcast_to([128, nb, sz])
                        now["B"] = dve(do(nc.vector.tensor_tensor, Bv[:, :, 0, :], Bv[:, :, 0, :], ea, ALU.mult),
                                       now["A"], now["B"], d2)
                    eb = Av[:, :, 0, sz - 1:sz].broadcast_to([128, nb, sz])
                    now["A"] = dve(do(nc.vector.tensor_tensor, Av[:, :, 1, :], Av[:, :, 1, :], eb, ALU.mult),
                                   now["A"], now["B"], d1)
                    return qa, kb, [d1, d2]

                p = prep(-1)
                for lev in range(-1, 7):
                    qa, kb, wq = p
                    p = prep(lev + 1)
                    bx, bm = ((4, 5), (6, 7))[lev % 2]
                    w = wq + take([bx])
                    for j in range(4):
                        c = META + 128 * j
                        t = pe(do(nc.tensor.matmul, P[:, 512 * bx + 128 * j:512 * bx + 128 * j + 128], kb[:, c:c + 128],
                                  qa[:, c:c + 128], start=(j == 0), stop=(j == 3), skip_group_check=True), w)
                    if lev < 4:
                        tm = pe(do(nc.tensor.matmul, P[0:16, 512 * bm:512 * bm + 16], kb[:, 0:16], qa[:, 0:16],
                                   start=True, stop=True), take([bm]))
                        mm = dve(do(nc.vector.copy_predicated, SM[:, 0:16], masks[0:16, lev + 1, 0:16],
                                    P[0:16, 512 * bm:512 * bm + 16]), tm, fr("SM"), done, ld_mask)
                        release([bm], mm)
                        t = tm
                    if lev >= 0:
                        qb_free[lev % 2] = [t]
                    mk = masks[:, lev + 1, :].unsqueeze(1).broadcast_to([128, 4, 128])
                    cp = dve(do(nc.vector.copy_predicated, scd, mk,
                                P[:, 512 * bx:512 * bx + 512].rearrange("p (j c) -> p j c", c=128)), t, fr("SC"), done, ld_mask)
                    release([bx], cp)
                    done = [mm, cp]
                    yield
                dense = []
                for lev, blocks in ((7, ((0, 128, 256), (2, 384, 512))), (8, ((0, 256, 512), (1, 256, 512)))):
                    qa, kb, wq = p
                    if lev == 7:
                        p = prep(8)
                    else:
                        d1 = dve(do(nc.vector.tensor_tensor, QAs[1][:, META:T], Q[:, META:T], A[:, META:T], ALU.mult),
                                 now["A"], qb_free[1])
                        d2 = dve(do(nc.vector.tensor_tensor, KBs[1][:, 0:META], K[:, 0:META], B[:, 0:META], ALU.mult),
                                 now["B"], qb_free[1])
                    bx = (4, 6)[lev % 2]
                    w = wq + take([bx])
                    o = 512 * bx
                    evs = []
                    for n, (js, c0, c1) in enumerate(blocks):
                        t = pe(do(nc.tensor.matmul, P[:, o:o + c1 - c0], kb[:, META + 128 * js:META + 128 * js + 128],
                                  qa[:, META + c0:META + c1], start=(n == 0), stop=(n == 1), skip_group_check=True), w)
                        evs.append((js, c0, c1, o))
                        o += c1 - c0
                    qb_free[lev % 2] = [t]
                    for js, c0, c1, oo in evs:
                        v = act(do(nc.scalar.activation, SC[:, 512 * js + c0:512 * js + c1], P[:, oo:oo + c1 - c0], ACT.Copy),
                                t, fr("SC"))
                        dense.append(v)
                    release([bx], v)
                    yield
                t = pe(do(nc.tensor.matmul, P[0:16, 512 * 5:512 * 6], KBs[1][:, 0:16], QAs[1][:, META:T], start=True, stop=True),
                       d1, d2, take([5]))
                v = act(do(nc.scalar.activation, SM[:, META:T], P[0:16, 512 * 5:512 * 6], ACT.Copy), t, fr("SM"))
                release([5], v)
                dense.append(v)
                qb_free[1] = [t]
                acc = done
                yield
                while len(vi_ready) < 10:
                    yield
                first["A"] = first["B"] = first["K"] = first[f"Q{h % 2}"] = [d1, d2, t]
                reg = two(3)
                w = take(reg[2]) + dense + acc + vi_ready
                o = 1024 * 3 + 248
                for a, b in segments(0, T):
                    t = pe(do(nc.tensor.matmul, P[:, o + a:o + b], VI[0:16, 0, 128 * h:128 * h + 128], SM[:, a:b],
                                                        start=True, stop=False, skip_group_check=True), w)
                for j in range(4):
                    s0 = META + 128 * j
                    for a, b in segments(s0, T):
                        t = pe(do(nc.tensor.matmul, P[:, o + a:o + b], VI[:, 1 + j, 128 * h:128 * h + 128], SC[:, 512 * j + a - META:512 * j + b - META],
                            start=False, stop=True, skip_group_check=True), w)
                first["SC"] = first["SM"] = [t]
                yield
                i, q, f_ = temp()
                s = act(do(nc.scalar.activation, q[:, :], reg[0], ACT.Square), t, f_)
                yield
                r2 = two(2)
                t2 = ones_sum(ones_head, q, r2, True, True, [s] + take(r2[2]))
                yield
                a_, b_ = inv_root(q[:, :], r2[0], eps6, [t2])
                release(r2[2], a_)
                n1 = dve(do(nc.vector.scalar_tensor_tensor, q[:, :], reg[0], par("hgn", l), q[:, :], ALU.mult, ALU.mult), b_)
                release(reg[2], n1)
                n2 = dve(do(nc.vector.tensor_tensor, q[:, :], q[:, :], Gb[:, :], ALU.mult), n1, zG)
                out_split(q[:, :], h, [n2], i)
                first[f"G{h % 2}"] = [n2]

            def last_of(name):
                return first.get(name, fence)

            for h in range(4):
                early = products(units(3), XH, XL, xr, [two(0), two(1), two(2)]) if h == 0 else []

                def tile(n):
                    r = two(n) if early else region()
                    return r, early[n] if early else product(units(1), XH, XL, xr, r)

                r, t = tile(0)
                Gb = (G, G2)[h % 2]
                zG = act(do(nc.scalar.activation, Gb[:, :], r[0], ACT.Silu), t, last_of(f"G{h % 2}"))
                release(r[2], zG)
                r, t = tile(1)
                zQ = act(do(nc.scalar.activation, Qs[h % 2][:, :], r[0], ACT.Silu), t, last_of(f"Q{h % 2}"), rstd_free)
                release(r[2], zQ)
                r, t = tile(2)
                drain()
                i, q, f_ = temp()
                j, q2, f2 = temp()
                s1 = act(do(nc.scalar.activation, q[:, :], r[0], ACT.Sigmoid), t, f_)
                s2 = act(do(nc.scalar.activation, q2[:, :], r[0], ACT.Sigmoid, scale=-1.0), t, f2)
                release(r[2], s2)
                zA = dve(do(nc.vector.tensor_scalar, A[:, :], q[:, :], lbv[:, 4 + h:5 + h], lbv[:, h:h + 1],
                            ALU.mult, ALU.add), s1, lb_ready, last_of("A"))
                zK = dve(do(nc.vector.tensor_scalar, K[:, :], q2[:, :], lbv[:, 4 + h:5 + h], float(128 ** -0.5),
                            ALU.mult, ALU.mult), s2, lb_ready, last_of("K"))
                tmp_free[i], tmp_free[j] = [zA], [zK]
                background.append(hgrn(h, (zA, zK, zQ, zG)))
                if h == 0:
                    for c in range(2):
                        u = units(2)
                        wide_product(u[0], nat5, nat5_region, keep(VI, 256 * c, vi_ready), xr)

            lx_t, ly_t, gr = [], [], []
            for n in range(2):
                r = region()
                t = product(units(1), XH, XL, xr, r)
                v = act(do(nc.scalar.activation, LX[:, n, 3:T + 3], r[0], ACT.Copy), t, fence)
                release(r[2], v)
                lx_t.append(v)
            u = units(2)
            wide_product(u[0], nat5, nat5_region, keep(VR, 0, vr_ready), xr)

            def ret_gate(n):
                r = region()
                t = product(units(1), XH, XL, xr, r)
                v = act(do(nc.scalar.activation, (G, G2)[n][:, :], r[0], ACT.Silu), t, first[f"G{n}"])
                release(r[2], v)
                gr.append(v)

            ret_gate(0)
            drain()
            LY = (QA, KB)
            LR = [K, Q0, rstd]

            def lru():
                lrf = [first["K"], first["Q0"], first["Q1"]]
                for n in range(2):
                    Y = LR[0]
                    x = LX[:, n, :]

                    def cw(j, n=n):
                        return PP[:, pc["lcw"] + 8 * l + 2 * j + n:pc["lcw"] + 8 * l + 2 * j + n + 1]

                    c = dve(do(nc.vector.tensor_scalar, Y[:, :], x[:, 3:T + 3], cw(3), par("lcb", 2 * l + n), ALU.mult, ALU.add),
                            lx_t[n], lx_zero, lrf[0])
                    for j in range(3):
                        c = dve(do(nc.vector.scalar_tensor_tensor, Y[:, :], x[:, j:j + T], cw(j), Y[:, :], ALU.mult, ALU.add), c)
                    rg_ = two(2)
                    t = ones_sum(gw[:, n, :], Y, rg_, True, True, [c, ld_gw] + take(rg_[2]))
                    s1 = act(do(nc.scalar.activation, LR[1][:, :], rg_[0], ACT.Sigmoid, bias=par("gab", 2 * l + n)), t, lrf[1])
                    release(rg_[2], s1)
                    ri = two(2)
                    t = ones_sum(gw[:, 2 + n, :], Y, ri, True, True, [c, ld_gw] + take(ri[2]))
                    s2 = act(do(nc.scalar.activation, LR[2][:, :], ri[0], ACT.Sigmoid, bias=par("gib", 2 * l + n)), t, lrf[2])
                    release(ri[2], s2)
                    yield
                    i, q, f1 = temp()
                    th = act(do(nc.scalar.activation, q[:, :], LR[1][:, :], ACT.Tanh, scale=lbv[:, 24 + n:25 + n]), s1, f1, sp_ready)
                    ea = act(do(nc.scalar.activation, LR[1][:, :], LR[1][:, :], ACT.Exp, scale=lbv[:, 26 + n:27 + n]), th, sp_ready)
                    ix = dve(do(nc.vector.tensor_tensor, Y[:, :], Y[:, :], LR[2][:, :], ALU.mult), s2, t)
                    a2 = dve(do(nc.vector.tensor_tensor, LR[2][:, :], LR[1][:, :], LR[1][:, :], ALU.mult), ea, ix)
                    a3 = dve(do(nc.vector.scalar_tensor_tensor, q[:, :], LR[2][:, :], 1.0, q[:, :], ALU.add, ALU.mult), a2, th)
                    a4 = act(do(nc.scalar.activation, q[:, :], q[:, :], ACT.Sqrt), a3)
                    a5 = dve(do(nc.vector.tensor_tensor, Y[:, :], Y[:, :], q[:, :], ALU.mult), a4, ix)
                    a6 = dve(do(nc.vector.tensor_tensor_scan, q[:, :], LR[1][:, :], Y[:, :], 0.0, ALU.mult, ALU.add), a5, ea)
                    a7 = dve(do(nc.vector.tensor_tensor, q[:, :], q[:, :], LY[n][:, :], ALU.mult), a6, ly_t[n])
                    o = out_split(q[:, :], 6 + n, [a7], i)
                    lrf = [[a5, a6], [a6], [a3]]
                    lr_end[:] = [a5, a6, a7]
                    yield

            lr_end = []
            dec_free = []
            QR, KR = A, B
            rr = []
            for n, (dst, name) in enumerate(((QR, "A"), (KR, "B"))):
                r = region()
                t = product(units(1), XH, XL, xr, r)
                qx = dec[n]
                a = act(do(nc.scalar.activation, qx[:, :], r[0], ACT.Copy), t, qb_free)
                release(r[2], a)

                def rest(qx=qx, a=a, dst=dst, name=name):
                    pr_ = two(2)
                    ts = ones_sum(perm_r, qx, pr_, True, True, [a] + take(pr_[2]))
                    i, w_, f1 = temp()
                    b = dve(do(nc.vector.tensor_tensor, w_[:, :], qx[:, :], tab[:, 0, :], ALU.mult), a, f1, ld_tab)
                    c = dve(do(nc.vector.tensor_tensor, dst[:, :], pr_[0], tab[:, 1, :], ALU.mult), ts, first[name], ld_tab)
                    release(pr_[2], c)
                    d = dve(do(nc.vector.tensor_tensor, dst[:, :], dst[:, :], w_[:, :], ALU.add), b, c)
                    tmp_free[i] = [d]
                    rr.append(d)
                    dec_free.append([b, ts])

                soon.append(rest)

            def retention():
                while len(dec_free) < 2:
                    yield
                dfree = list(dec_free)
                for n in range(2):
                    reg = two(3)
                    wo = take(reg[2])
                    o = 1024 * 3 + 248
                    for half in range(2):
                        hh = 2 * n + half
                        dc = dec[half]
                        ld_d = load(pool, dc[:, :], dt_h[hh, :, :], dfree[half])
                        tl_ = []
                        r2 = two(2)
                        w = take(r2[2]) + rr
                        for a, b in segments(0, T):
                            t = pe(do(nc.tensor.matmul, P[0:16, 1024 * 2 + 248 + a:1024 * 2 + 248 + b], KR[32 * hh:32 * hh + 32, 0:16],
                                QR[32 * hh:32 * hh + 32, a:b], start=True, stop=True), w)
                        v = dve(do(nc.vector.tensor_tensor, SM[:, :], P[0:16, 2296:2296 + T], dc[0:16, :], ALU.mult),
                                t, ld_d, first["SM"])
                        release(r2[2], v)
                        tl_.append(v)
                        for j in range(4):
                            bk = (4, 5)[j % 2]
                            m = 512 - 128 * j
                            t = pe(do(nc.tensor.matmul, P[:, 512 * bk:512 * bk + m], KR[32 * hh:32 * hh + 32, META + 128 * j:META + 128 * j + 128],
                                QR[32 * hh:32 * hh + 32, META + 128 * j:T], start=True, stop=True), take([bk]))
                            v = dve(do(nc.vector.tensor_tensor, SC[:, 640 * j:640 * j + m], P[:, 512 * bk:512 * bk + m], dc[:, 0:m], ALU.mult), t, first["SC"])
                            release([bk], v)
                            tl_.append(v)
                        dfree[half] = [v]
                        yield
                        s0 = 64 * half
                        for a, b in segments(0, T):
                            t = pe(do(nc.tensor.matmul, P[s0:s0 + 64, o + a:o + b], VR[0:16, 0, 64 * hh:64 * hh + 64], SM[:, a:b],
                                start=True, stop=False, skip_group_check=True), wo + tl_ + vr_ready)
                        for j in range(4):
                            c0 = META + 128 * j
                            for a, b in segments(c0, T):
                                t = pe(do(nc.tensor.matmul, P[s0:s0 + 64, o + a:o + b], VR[:, 1 + j, 64 * hh:64 * hh + 64],
                                    SC[:, 640 * j + a - c0:640 * j + b - c0], start=False, stop=True, skip_group_check=True))
                        first["SC"] = first["SM"] = [t]
                        yield
                    i, q, f1 = temp()
                    a = act(do(nc.scalar.activation, q[:, :], reg[0], ACT.Copy), t, f1)
                    release(reg[2], a)
                    r2 = two(2)
                    t = ones_sum(ones_ret, q, r2, True, True, [a] + take(r2[2]))
                    c = dve(do(nc.vector.tensor_tensor, q[:, :], q[:, :], r2[0], ALU.subtract), t)
                    release(r2[2], c)
                    yield
                    k, q2, f2 = temp()
                    s = act(do(nc.scalar.activation, q2[:, :], q[:, :], ACT.Square), c, f2)
                    t = ones_sum(ones_ret, q2, r2, True, True, [s] + take(r2[2]))
                    x1, x2 = inv_root(q2[:, :], r2[0], eps6, [t])
                    release(r2[2], x1)
                    c = dve(do(nc.vector.scalar_tensor_tensor, q[:, :], q[:, :], par("retn", l), q2[:, :],
                                                                         ALU.mult, ALU.mult), x2, c)
                    tmp_free[k] = [c]
                    Gb = (G, G2)[n]
                    while len(gr) <= n:
                        yield
                    c = dve(do(nc.vector.tensor_tensor, q[:, :], q[:, :], Gb[:, :], ALU.mult), c, gr[n])
                    out_split(q[:, :], 4 + n, [c], i)
                    yield

            background.append(retention())
            for n in range(2):
                r = region()
                t = product(units(1), XH, XL, xr, r)
                v = act(do(nc.scalar.activation, LY[n][:, :], r[0], ACT.Gelu_apprx_tanh), t, qb_free)
                release(r[2], v)
                ly_t.append(v)
            background.append(lru())
            ret_gate(1)
            x_read[:] = [pe_done[unit[0] - 1]]
            drain()
            rstd_free[:] = lr_end
            residual(lambda m, r: product(units(1), GH, GL, g_ready, r), 3)
            st["share"] = False
            ph.close()

        def conv_glu(l):
            ph = ExitStack()
            fence = phase_fence()
            HH = sb(f"GHH{l}", [128, NF, T], R, ph)
            HL = sb(f"GHL{l}", [128, NF, T], R, ph)
            hr = []

            def conv_tile(r, t, c):
                def w(j):
                    k = pc["fcw"] + 132 * l + 44 * j + c
                    return PP[:, k:k + 1]
                i, y, f_ = temp()
                p = r[0]
                a = act(do(nc.scalar.activation, y[:, :], p, ACT.Identity, bias=par("fcb", 44 * l + c), scale=w(2)), t, f_)
                b = dve(do(nc.vector.scalar_tensor_tensor, y[:, 1:T], p[:, 0:T - 1], w(1), y[:, 1:T], ALU.mult, ALU.add), a)
                b = dve(do(nc.vector.scalar_tensor_tensor, y[:, 2:T], p[:, 0:T - 2], w(0), y[:, 2:T], ALU.mult, ALU.add), b)
                release(r[2], b)
                return i, y, b

            early = products(units(3), XH, XL, xr, [two(0), two(1), two(2)])

            def tile(n):
                r = two(n % 4)
                return r, early[n] if n < 3 else product(units(1), XH, XL, xr, r)

            for m in range(NF):
                r, t = tile(2 * m)
                i, yg, tg = conv_tile(r, t, m)
                a = act(do(nc.scalar.activation, yg[:, :], yg[:, :], ACT.Silu), tg)
                r, t = tile(2 * m + 1)
                j, yv, tv = conv_tile(r, t, NF + m)
                b = dve(do(nc.vector.tensor_tensor, yg[:, :], yg[:, :], yv[:, :], ALU.mult), a, tv)
                tmp_free[j] = [b]
                th, tl = split(yg[:, :], HH[:, m, :], HL[:, m, :], [b], fence)
                tmp_free[i] = [th, tl]
                hr.append([th, tl])
            x_read[:] = [pe_done[unit[0] - 1]]
            residual(lambda m, r: product(units(3), HH, HL, hr, r), 3)
            ph.close()

        x_done = [x + [ld_m, ld_x] for x in x_done]
        for m in range(8):
            add_square(m)
            sum_square(m)
        for l in range(2):
            rms(pc["nmix"] + 8 * l)
            mixer(l)
            rms(pc["nffn"] + 8 * l)
            conv_glu(l)
        rms(pc["nfin"], final=True)
        sp(None, outs)
        assert unit[0] == len(plan)

        for q in (pe, act, dve, pool):
            n = 0
            for _, _, t in q.items:
                if t.sem is None and t.used:
                    n += 1
                    t.sem, t.val = sems[q.name], n

        def emit(q, e):
            seen = {}
            mine = sems.get(q.name)
            for what, waits, t in q.items:
                need_ = {}
                for w in waits:
                    k = w.sem.num if hasattr(w.sem, "num") else id(w.sem)
                    if seen.get(k, 0) < w.val:
                        if k not in need_ or need_[k][1] < w.val:
                            need_[k] = (w.sem, w.val)
                for k, (s, v) in need_.items():
                    e.wait_ge(s, v)
                    seen[k] = v
                if what is None:
                    continue
                ins = what[0](*what[1], **what[2])
                if t.sem is not None:
                    ins.then_inc(t.sem, 1 if t.sem is mine else 16)

        block = ctx.enter_context(nc.Block())

        @block.sync
        def _(e):
            emit(sp, e)

        @block.gpsimd
        def _(e):
            emit(pool, e)

        @block.scalar
        def _(e):
            emit(act, e)

        @block.vector
        def _(e):
            emit(dve, e)

        @block.tensor
        def _(e):
            emit(pe, e)


def constants():
    f = np.float32
    c = np.zeros((128, CN), f)
    eye = np.eye(128, dtype=f)
    c[:, CI:CI + 128] = eye
    c[:, CM:CM + 128] = 1.0 / 1024
    c[:, CG:CG + 128] = 1.0 / 128
    c[0:64, CB:CB + 64] = 1.0 / 64
    c[64:128, CB + 64:CB + 128] = 1.0 / 64
    i = np.arange(128)
    c[i, CPA + (i ^ 32)] = 1.0
    c[i, CPR + (i ^ 16)] = 1.0
    c[:, CE] = 1e-5
    c[:, CE + 1] = 1e-6
    s, t = np.meshgrid(i, i, indexing="ij")
    m = np.zeros((128, 8, 128), np.uint8)
    m[:, 0] = s == t
    for lev in range(7):
        b = 1 << lev
        m[:, lev + 1] = (s < t) & (s // (2 * b) == t // (2 * b)) & (s // b != t // b)
    inv = (f(10000.0) ** (-np.arange(0, 64, 2, dtype=f) / f(64))).astype(f)
    ang = np.arange(512, dtype=f)[:, None] * inv[None, :]
    co, si = np.cos(ang).T, np.sin(ang).T
    ta = np.stack([np.concatenate([co] * 4), np.concatenate([-si, si, -si, si])], 1).astype(f)
    th = (f(10000.0) ** (-np.linspace(0.0, 1.0, 16, dtype=f))).astype(f)
    ang = np.arange(T, dtype=f)[:, None] * th[None, :]
    co, si = np.cos(ang).T, np.sin(ang).T
    tr = np.stack([np.concatenate([co] * 8), np.concatenate([-si, si] * 4)], 1).astype(f)
    h = np.arange(4, dtype=np.float64)
    lg = np.log1p(-np.exp2(-5.0 - h))
    rel = np.arange(T)[None, :] - i[:, None]
    d = np.where(rel >= 0, np.exp(lg[:, None, None] * np.maximum(rel, 0)), 0.0) * 32 ** -0.5
    return c, m.reshape(128, 1024).view(np.int32), ta, tr, d.astype(f)


def pack_weights(w):
    plan = unit_plan()
    out = np.zeros((len(plan) // 2, 128, 2048), np.float32)
    for c in range(len(plan) // 2):
        a = 0
        for name, k0, nk, c0, n in plan[2 * c:2 * c + 2]:
            blk = w[name][128 * k0:128 * (k0 + nk), c0:c0 + n].reshape(nk, 128, n).transpose(1, 0, 2)
            out[c, :, a:a + nk * n] = blk.reshape(128, nk * n)
            a += nk * n
    return out


def pack_params(p):
    at, n = param_columns()
    out = np.zeros((128, n), np.float32)

    def put(name, a):
        out[:, at[name]:at[name] + a.shape[1]] = a

    def tiles(a):
        return a.reshape(-1, 128).T

    put("ln_g", tiles(p["ln_g"]))
    put("ln_b", tiles(p["ln_b"]))
    put("subln", tiles(p["a_subln_g"]))
    put("lam", np.broadcast_to(p["a_lambda"].reshape(1, 256), (128, 256)))
    put("nmix", tiles(p["norm_mix_g_2"]))
    put("nffn", tiles(p["norm_ffn_g_2"]))
    put("nfin", tiles(p["final_norm_g_2"]))
    put("lb", tiles(p["hg_lb_logits_2"]))
    put("hgn", tiles(p["hg_norm_g_2"]))
    put("retn", np.concatenate([p["ret_norm_g_2"]] * 2, 1).T)
    put("lcw", tiles(p["lru_conv_w_2"]))
    put("lcb", tiles(p["lru_conv_b_2"]))
    put("gab", tiles(p["lru_gate_a_b_2"]))
    put("gib", tiles(p["lru_gate_i_b_2"]))
    put("lru", tiles(p["lru_lambda_2"]))
    put("fcw", tiles(p["ffn_conv_w_2"]))
    put("fcb", tiles(p["ffn_conv_b_2"]))
    return out


def kernel(**inputs):
    import concourse.bacc as _bacc
    from concourse.bass_utils import run_bass_kernel_spmd as _run

    p = {k: np.asarray(v) for k, v in inputs.items()}
    w = {"a_qkv": p["a_w_qkv"][0], "a_o": p["a_w_o"][0], "kv": p["kv_w"], "b_q": p["b_w_q"][0], "b_o": p["b_w_o"][0]}
    for l in range(2):
        w[f"f_in{l}"], w[f"f_out{l}"] = p["ffn_w_in"][l], p["ffn_w_out"][l]
        w[f"m_in{l}"], w[f"m_out{l}"] = p["w_in_2"][l], p["w_out_2"][l]
        w[f"g_in{l}"], w[f"g_out{l}"] = p["ffn_w_up_2"][l], p["ffn_w_down_2"][l]
    c, masks, ta, tr, dec = constants()
    idx = np.clip(np.arange(512)[None, :] - 384 - np.arange(128)[:, None], -256, 256) + 256
    gates = np.zeros((2, 128, 4, 128), np.float32)
    for l in range(2):
        for a, name in enumerate(("lru_gate_a_w_2", "lru_gate_i_w_2")):
            for b in range(4):
                o = 64 * (b % 2)
                gates[l, o:o + 64, 2 * a + b // 2, o:o + 64] = p[name][l, b]
    arrays = {
        "wts": pack_weights(w),
        "xT": np.ascontiguousarray(p["x"][0].T.reshape(8, 128, 512).transpose(1, 0, 2)),
        "mT": np.ascontiguousarray(p["meta_tokens_2"].T.reshape(8, 128, META).transpose(1, 0, 2)),
        "pp": pack_params(p),
        "cst": c, "cstm": masks, "tA": np.ascontiguousarray(ta), "tR": np.ascontiguousarray(tr), "dech": dec,
        "biasT": np.ascontiguousarray(p["b_rel_bias"][0][:, idx]),
        "gates": gates,
    }
    nc = _bacc.Bacc("TRN2", target_bir_lowering=False, num_devices=1)
    args = [nc.dram_tensor("in_" + k, a.shape, mybir.dt.from_np(a.dtype), kind="ExternalInput").ap()
            for k, a in arrays.items()]
    args.append(nc.dram_tensor("out_0", (128, 8, 512), mybir.dt.float32, kind="ExternalOutput").ap())
    build(nc, *args)
    r = _run(nc, [{"in_" + k: a for k, a in arrays.items()}], core_ids=[0])
    o = r.results[0]["out_0"]
    return np.ascontiguousarray(o.transpose(1, 0, 2).reshape(1024, 512).T)[None]
```

```python
import math
from contextlib import ExitStack

import numpy as np
import concourse.bass as bass
from concourse import mybir

D = 1024
T = 528
META = 16
FF = 2816
NF = FF // 128
ALPHA = 4.0 ** 0.25
RAW = 3
NS = 3
NEG = -1.0e30


def unit_plan():
    plan = []

    def cols(name, c, nk=8, k0=0):
        plan.append((name, k0, nk, c, 128))

    def wide(name, c):
        plan.append((name, 0, 4, c, 256))
        plan.append((name, 4, 4, c, 256))

    def widest(name, c):
        for k0 in range(0, 8, 2):
            plan.append((name, k0, 2, c, 512))

    def ffn(win, wout):
        for m in range(NF):
            cols(win, 128 * m)
            cols(win, FF + 128 * m)
        for m in range(8):
            for k0, nk in ((0, 8), (8, 8), (16, 6)):
                cols(wout, 128 * m, nk, k0)

    for g in range(4):
        for part in (0, 1):
            for j in range(2):
                cols("a_qkv", 1024 * part + 256 * g + 128 * j)
        if g % 2 == 0:
            widest("a_qkv", 2048 + 256 * g)
    for m in range(8):
        cols("a_o", 128 * m)
    ffn("f_in0", "f_out0")
    for g in range(4):
        for j in range(2):
            cols("b_q", 256 * g + 128 * j)
        for j in range(2):
            cols("kv", 256 * g + 128 * j)
        if g % 2 == 0:
            widest("kv", 1024 + 256 * g)
    for m in range(8):
        cols("b_o", 128 * m)
    ffn("f_in1", "f_out1")
    for l in range(2):
        w = f"m_in{l}"
        widest(w, 1024)
        for h in range(4):
            for c in (1536, 0, 512):
                cols(w, c + 128 * h)
        cols(w, 2816)
        cols(w, 2944)
        wide(w, 2304)
        for c in (2560, 2048, 2176, 3072, 3200, 2688):
            cols(w, c)
        for m in range(8):
            cols(f"m_out{l}", 128 * m)
        ffn(f"g_in{l}", f"g_out{l}")
    return plan


def param_columns():
    at, n = {}, 0
    for name, k in (("ln_g", 32), ("ln_b", 32), ("subln", 1), ("lam", 256), ("nmix", 16), ("nffn", 16),
                    ("nfin", 8), ("lb", 8), ("hgn", 2), ("retn", 2), ("lcw", 16), ("lcb", 4), ("gab", 4),
                    ("gib", 4), ("lru", 4), ("fcw", 264), ("fcb", 88)):
        at[name] = n
        n += k
    return at, n


CI, CM, CG, CB, CPA, CPR, CE = 0, 128, 256, 384, 512, 640, 768
CN = 772




class Tok:

    def __init__(self, eng):
        self.eng, self.used, self.sem, self.val, self.time = eng, False, None, 0, 0.0


def flatten(w):
    if isinstance(w, (list, tuple)):
        for x in w:
            yield from flatten(x)
    elif w is not None:
        yield w


def do(method, *args, **named):
    return method, args, named


def columns(ap):
    n = 1
    for x in ap.shape[1:]:
        n *= x
    return n


def length_us(name, what):
    method, args, _ = what
    if name == "pe":
        last = args[-1]
        return (0.21 if last.dtype == mybir.dt.float32r else 0.85) * columns(args[0]) / 512 + 0.01
    if name == "sp" or len(args) < 2:
        return 3.0
    if name == "act":
        return 0.2 + columns(args[0]) / 1400
    if name == "dve":
        return 0.08 + max(columns(args[0]), columns(args[1]) if isinstance(args[1], bass.AP) else 0) / 960
    return 1.0


class Queue:

    def __init__(self, name):
        self.name, self.items = name, []
        self.last = None
        self.clock, self.func = 0.0, None

    def advance(self, what, waits):
        t = max([self.clock] + [w.time + 0.1 for w in waits]) + length_us(self.name, what)
        f = what[1][2] if self.name == "act" and len(what[1]) > 2 else None
        if f is not None and f not in (mybir.ActivationFunctionType.Copy, mybir.ActivationFunctionType.Square,
                                       mybir.ActivationFunctionType.Identity):
            t += 0 if f == self.func else 1.3
            self.func = f
        self.clock = t
        return t

    def __call__(self, what, *waits):
        flat = list(flatten(waits))
        for w in flat:
            w.used = True
        t = Tok(self.name)
        t.time = self.advance(what, flat) if what else self.clock
        self.items.append((what, flat, t))
        self.last = t
        return t


def build(nc, wts, xT, mT, pp, cst, cstm, tA, tR, dt_h, biasT, gates, out):
    F = mybir.dt.float32
    R = mybir.dt.float32r
    U8 = mybir.dt.uint8
    ALU = mybir.AluOpType
    ACT = mybir.ActivationFunctionType
    AX = mybir.AxisListType
    plan = unit_plan()
    pc, npp = param_columns()

    pe, act, dve, pool, sp = (Queue(n) for n in ("pe", "act", "dve", "pool", "sp"))
    ctx = ExitStack()
    with ctx:
        def sb(name, shape, dt=F, c=ctx):
            return c.enter_context(nc.sbuf_tensor(name, shape, dt))

        X = sb("X", [128, 8, T])
        XH = sb("XH", [128, 8, T], R)
        XL = sb("XL", [128, 8, T], R)
        raw = sb("raw", [128, RAW, 2048])
        WH = sb("WH", [128, NS, 1024], R)
        WL = sb("WL", [128, NS, 1024], R)
        PP = sb("PP", [128, npp])
        C = sb("C", [128, CN])
        rstd = sb("rstd", [128, T])
        small = sb("small", [128, 64])
        lbvs = [sb(f"lbv{l}", [128, 32]) for l in range(2)]
        P = ctx.enter_context(nc.psum_tensor("P", [128, 4096], F))

        sems = {n: ctx.enter_context(nc.semaphore("s_" + n)) for n in ("pe", "act", "dve", "pool")}
        raw_sem = [ctx.enter_context(nc.semaphore(f"s_raw{i}")) for i in range(RAW)]
        nload = [0]
        issue = {"sp": nc.sync.dma_start, "act": nc.scalar.dma_start, "pool": nc.gpsimd.dma_start}

        def load(queue, dst, src, *waits):
            s = ctx.enter_context(nc.semaphore(f"s_ld{nload[0]}"))
            nload[0] += 1
            c = queue.clock
            t = queue(do(issue[queue.name], dst, src), *waits)
            t.time, queue.clock = t.time + 1.0, c + 0.1
            t.used, t.sem, t.val = False, s, 16
            return t

        ident = C[:, CI:CI + 128]
        ones_mean = C[:, CM:CM + 128]
        ones_head = C[:, CG:CG + 128]
        ones_ret = C[:, CB:CB + 128]
        perm_a = C[:, CPA:CPA + 128]
        perm_r = C[:, CPR:CPR + 128]
        mask_uv = sb("mask_uv", [1, 192], mybir.dt.bfloat16)
        mask_u = mask_uv[:, 0:128]
        mask_v = mask_uv[:, 128:192]
        eps5 = C[:, CE:CE + 1]
        eps6 = C[:, CE + 1:CE + 2]

        def par(name, i, n=1):
            return PP[:, pc[name] + i:pc[name] + i + n]

        ld_x = [load(act, X[:, k, META:T], xT[:, k, :]) for k in range(8)]
        ld_c = load(pool, C[:, :], cst)
        ld_p = load(pool, PP[:, :], pp)
        ld_m = load(pool, X[:, :, 0:META], mT)

        bank_free = [[] for _ in range(8)]

        mask_ready = [pool(do(nc.gpsimd.memset, mask_uv[:, 0:64], 1.0)),
                      pool(do(nc.gpsimd.memset, mask_uv[:, 64:128], 0.0)),
                      pool(do(nc.gpsimd.memset, mask_uv[:, 128:192], NEG))]

        def one(b):
            return P[:, 512 * b:512 * b + 512], [(512 * b, META, T)], [b]

        def two(p):
            a = 1024 * p + 248
            return P[:, a:a + T], [(a, 0, 264), (a + 264, 264, T)], [2 * p, 2 * p + 1]

        def take(banks):
            w = [t for b in banks for t in bank_free[b]]
            return w

        def release(banks, *toks):
            for b in banks:
                bank_free[b] = list(toks)

        raw_tok = {}
        raw_done = {}
        conv = {}
        pe_done = {}
        st = {"conv": 0, "cur": -1, "load": 0, "share": False}

        def length(u):
            return plan[u][2] * plan[u][4]

        def load_chunks(upto):
            while st["load"] <= upto and 2 * st["load"] < len(plan):
                c = st["load"]
                n = length(2 * c) + length(2 * c + 1)
                s = c % RAW
                t = sp(do(nc.sync.dma_start, raw[:, s, 0:n], wts[c, :, 0:n]),
                       raw_done.get(c - RAW))
                t.sem, t.val = raw_sem[s], 16 * (c // RAW + 1)
                raw_tok[c] = t
                st["load"] += 1

        def convert(u):
            c, s = u // 2, u % NS
            load_chunks(c)
            a = length(u - 1) if u % 2 else 0
            n = length(u)
            src = raw[:, c % RAW, a:a + n]
            th = act(do(nc.scalar.activation, WH[:, s, 0:n], src, ACT.Copy), raw_tok[c], pe_done.get(u - NS))
            if st["share"] and u % 2:
                tl = pool(do(nc.gpsimd.tensor_tensor, WL[:, s, 0:n], src, WH[:, s, 0:n].bitcast(F), ALU.subtract), th)
            else:
                tl = dve(do(nc.vector.tensor_tensor, WL[:, s, 0:n], src, WH[:, s, 0:n].bitcast(F), ALU.subtract), th)
            conv[u] = [th, tl]
            raw_done.setdefault(c, []).append(tl)

        def need(u):
            while st["conv"] <= u:
                convert(st["conv"])
                st["conv"] += 1

        def run_ahead():
            while st["conv"] < min(len(plan), st["cur"] + NS):
                convert(st["conv"])
                st["conv"] += 1

        background = []

        def step(entry=None):
            if not background:
                return
            e = entry or min(background, key=lambda x: x[1])
            counts = [len(q.items) for q in (act, dve, pool, pe)]
            try:
                asks = next(e[0])
            except StopIteration:
                background.remove(e)
                return
            grown = [len(q.items) - c for q, c in zip((act, dve, pool, pe), counts)]
            if asks is not None:
                e[1] = max((w.time + 0.1 for w in flatten(asks)), default=0.0)
                return
            times = [q.clock for q, g in zip((act, dve, pool), grown) if g]
            if times:
                e[1] = max(times)
            elif not grown[3]:
                e[1] = max(e[1], pe.clock) + 0.05

        def behind(gen):
            background.append([gen, 0.0])

        def drain():
            while background:
                step()

        def until(condition):
            while not condition():
                step()

        class Lanes:

            def __init__(self):
                self.tasks, self.done, self.closed = [[], []], [0, 0], False
                for n in range(2):
                    behind(self.run(n))

            def run(self, n):
                while self.tasks[n] or not self.closed:
                    if self.tasks[n]:
                        yield from self.tasks[n].pop(0)
                        self.done[n] += 1
                    else:
                        yield

            def wait(self, pairs):
                until(lambda: min(self.done) >= pairs)

            def finish(self):
                self.closed = True
                drain()

        soon = []

        def tick():
            while soon:
                soon.pop(0)()
            for e in list(background):
                if e[1] <= pe.clock:
                    step(e)

        def product(units, xh, xl, xready, region, lo_col=0):
            ap, segs, banks = region
            w0 = take(banks)
            kt = 0
            total = sum(plan[u][2] for u in units)
            for u in units:
                need(u)
                s = u % NS
                wt = conv[u]
                for k in range(plan[u][2]):
                    for i, (wb, xb) in enumerate(((WL, xh), (WH, xl), (WH, xh))):
                        for a, c0, c1 in segs:
                            first = kt == 0 and i == 0
                            lastm = kt == total - 1 and i == 2
                            t = pe(do(nc.tensor.matmul, P[:, a:a + c1 - c0], wb[:, s, 128 * k:128 * k + 128],
                                            xb[:, kt, c0 - lo_col:c1 - lo_col], start=first, stop=lastm),
                                   w0, wt, xready[kt])
                            w0, wt = None, None
                    kt += 1
                    tick()
                pe_done[u] = t
                st["cur"] = u
                run_ahead()
            return t

        def products(us, xh, xl, xready, regions, lo_col=0):
            need(us[-1])
            toks = [None] * len(us)
            wr = [take(r[2]) + conv[u] for u, r in zip(us, regions)]
            for k in range(8):
                for n, (u, (_, segs, _)) in enumerate(zip(us, regions)):
                    s = u % NS
                    for i, (wb, xb) in enumerate(((WL, xh), (WH, xl), (WH, xh))):
                        for a, c0, c1 in segs:
                            toks[n] = pe(do(nc.tensor.matmul, P[:, a:a + c1 - c0], wb[:, s, 128 * k:128 * k + 128],
                                            xb[:, k, c0 - lo_col:c1 - lo_col], start=(k == 0 and i == 0),
                                            stop=(k == 7 and i == 2)), wr[n], xready[k])
                    wr[n] = None
                tick()
            for u, t in zip(us, toks):
                pe_done[u] = t
            st["cur"] = us[-1]
            run_ahead()
            return toks

        def widest_product(tiles, banks, xready):
            w0 = take(banks)
            for n in range(4):
                u = unit[0]
                unit[0] += 1
                need(u)
                for kk in range(2):
                    k = 2 * n + kk
                    for (c0, c1), b in zip(tiles, banks):
                        for i, (xb, wb) in enumerate(((XL, WH), (XH, WL), (XH, WH))):
                            t = pe(do(nc.tensor.matmul, P[0:c1 - c0, 512 * b:512 * b + 512], xb[:, k, c0:c1],
                                      wb[:, u % NS, 512 * kk:512 * kk + 512], start=(k == 0 and i == 0),
                                      stop=(k == 7 and i == 2)), w0, conv[u], xready[k])
                    w0 = None
                    for _ in tiles:
                        tick()
                pe_done[u] = t
                st["cur"] = u
                run_ahead()
            return t

        def begin_tiles(us, xh, xl, xready, regions, k1, lo_col=0):
            need(us[-1])
            wr = [take(r[2]) + conv[u] for u, r in zip(us, regions)]
            for k in range(k1):
                for n, (u, r) in enumerate(zip(us, regions)):
                    part_tile(u, xh, xl, xready, r, k, lo_col, wr[n])
                    wr[n] = None
                    tick()

        def part_tile(u, xh, xl, xready, region, k, lo_col, waits):
            for i, (wb, xb) in enumerate(((WL, xh), (WH, xl), (WH, xh))):
                for a, c0, c1 in region[1]:
                    t = pe(do(nc.tensor.matmul, P[:, a:a + c1 - c0], wb[:, u % NS, 128 * k:128 * k + 128],
                              xb[:, k, c0 - lo_col:c1 - lo_col], start=(k == 0 and i == 0), stop=(k == 7 and i == 2)),
                           waits, xready[k])
            return t

        def end_tile(u, xh, xl, xready, region, k1, lo_col=0):
            for k in range(k1, 8):
                t = part_tile(u, xh, xl, xready, region, k, lo_col, None)
                tick()
            pe_done[u] = t
            st["cur"] = u
            run_ahead()
            return t

        def wide_product(u, tiles, region_of, consume, xready):
            need(u + 1)
            for n, (c0, c1) in enumerate(tiles):
                o, banks = region_of(n)
                w0 = take(banks)
                for k in range(8):
                    s, kk = (u + k // 4) % NS, k % 4
                    for i, (xb, wb) in enumerate(((XL, WH), (XH, WL), (XH, WH))):
                        t = pe(do(nc.tensor.matmul, o, xb[:, k, c0:c1], wb[:, s, 256 * kk:256 * kk + 256],
                                        start=(k == 0 and i == 0), stop=(k == 7 and i == 2)),
                               w0, conv[u], conv[u + 1], xready[k])
                        w0 = None
                    tick()
                release(banks, *consume(n, o, t))
            pe_done[u] = pe_done[u + 1] = t
            st["cur"] = u + 1
            run_ahead()

        unit = [0]

        def units(n):
            u = unit[0]
            unit[0] += n
            return list(range(u, u + n))

        def ones_sum(m, src, region, first, last, waits, lo_col=0):
            ap, segs, banks = region
            for a, c0, c1 in segs:
                t = pe(do(nc.tensor.matmul, P[:, a:a + c1 - c0], m, src[:, c0 - lo_col:c1 - lo_col],
                                                             start=first, stop=last), waits)
            return t

        def inv_root(dst, src, eps, waits):
            a = act(do(nc.scalar.activation, dst, src, ACT.Ln, bias=eps), waits)
            return a, act(do(nc.scalar.activation, dst, dst, ACT.Exp, scale=-0.5), a)

        def split(src, h, l, waits, hw):
            th = act(do(nc.scalar.activation, h, src, ACT.Copy), waits, hw)
            tl = dve(do(nc.vector.tensor_tensor, l, src, h.bitcast(F), ALU.subtract), th, waits, hw)
            return th, tl

        tmp = [sb(f"tmp{i}", [128, T]) for i in range(4)]
        tmp_free = [[] for _ in range(4)]
        tmp_at = [0]

        def temp():
            i = tmp_at[0] % 4
            tmp_at[0] += 1
            return i, tmp[i], tmp_free[i]

        C1 = slice(META, T)
        xr = [None] * 8
        x_done = [[ld_x, ld_m, ld_c, ld_p]] * 8
        need(0)
        for k in range(8):
            th, tl = split(X[:, k, C1], XH[:, k, C1], XL[:, k, C1], [ld_x[k]], None)
            xr[k] = [th, tl]
            if k in (1, 3):
                need((k + 1) // 2)

        def ln_exp_tables():
            act(do(nc.scalar.preload_act_table_set, "natural_log_exp_and_others"))

        def ln_region(m):
            return one((0, 1, 7)[m % 3])

        def residual_ln(l, j, tiles):
            g0 = pc["ln_g"] + 16 * l + 8 * j
            b0 = pc["ln_b"] + 16 * l + 8 * j
            mean = one(6)
            var = one(7)
            evac = []
            feeds = not (l == 1 and j == 1)
            ln_exp_tables()

            def sum_tile(m):
                if 1 <= m < 7:
                    a = X[:, 0, C1] if m == 1 else rstd[:, C1]
                    mean_sum.append(dve(do(nc.vector.tensor_tensor, rstd[:, C1], a, X[:, m, C1], ALU.add),
                                        evac[m], evac[0], mean_sum[-1:], rstd_free))
                elif m == 7:
                    ones_sum(ones_mean, rstd, mean, True, False, [mean_sum[-1], ld_c] + take(mean[2]))
                    return ones_sum(ones_mean, X[:, 7, :], mean, False, True, [evac[7]])

            mean_sum = []

            for m in range(8):
                r = ln_region(m)
                t = tiles(m, r)
                v = dve(do(nc.vector.scalar_tensor_tensor, X[:, m, C1], X[:, m, C1], float(ALPHA), r[0],
                                                                   ALU.mult, ALU.add), t, x_done[m])
                release(r[2], v)
                evac.append(v)
                tm = sum_tile(m)
            wv = take(var[2])
            cen = []
            for m in range(8):
                c = dve(do(nc.vector.tensor_tensor, X[:, m, C1], X[:, m, C1], mean[0], ALU.subtract), tm, evac[m])
                cen.append(c)
                i, q, fr = temp()
                s = act(do(nc.scalar.activation, q[:, C1], X[:, m, C1], ACT.Square), c, fr)
                tv = ones_sum(ones_mean, q, var, m == 0, m == 7, [s] + wv)
                wv = []
                tmp_free[i] = [tv]
            release(mean[2], cen[-1])
            need(st["cur"] + NS)
            tl_, te = inv_root(rstd[:, C1], var[0], eps5, [tv, ld_c, tm, rstd_free])
            release(var[2], tl_)
            dn = []
            for m in range(8):
                i, q, fr = temp()
                a = dve(do(nc.vector.tensor_tensor, q[:, C1], X[:, m, C1], rstd[:, C1], ALU.mult), te, cen[m], fr)
                h = feeds and act(do(nc.scalar.activation, XH[:, m, C1], q[:, C1], ACT.Identity,
                                     bias=PP[:, b0 + m:b0 + m + 1], scale=PP[:, g0 + m:g0 + m + 1]), a, x_read)
                f = act(do(nc.scalar.activation, X[:, m, C1], q[:, C1], ACT.Identity, bias=PP[:, b0 + m:b0 + m + 1],
                                                         scale=PP[:, g0 + m:g0 + m + 1]), a)
                tmp_free[i] = [f]
                x_done[m] = [f]
                if not feeds:
                    x_done[m] = [f, ld_m, ld_x]
                    sum_square(m)
                if feeds:
                    d = dve(do(nc.vector.tensor_tensor, XL[:, m, C1], X[:, m, C1], XH[:, m, C1].bitcast(F), ALU.subtract),
                            f, h, x_read)
                    x_done[m] = [f, d, h]
                    xr[m] = [h, d]
            rstd_free[:] = [a]

        squares = {}

        def sum_square(m):
            ms = two(3)
            i, q, fr = temp()
            s = act(do(nc.scalar.activation, q[:, :], X[:, m, :], ACT.Square), x_done[m], fr)
            squares["all"] = ones_sum(ones_mean, q, ms, m == 0, m == 7, [s, ld_c] + (take(ms[2]) if m == 0 else []))
            tmp_free[i] = [squares["all"]]

        rstd_free = []
        x_read = []

        def phase_fence():
            return [q.last for q in (pe, act, dve)]

        ph = ExitStack()
        QT = [sb(f"QT{i}", [128, 2, 512], F, ph) for i in range(2)]
        KT = [sb(f"KT{i}", [128, 2, 512], F, ph) for i in range(2)]
        VN = sb("VN", [128, 4, 512], F, ph)
        OH = sb("OH", [128, 8, 512], R, ph)
        OL = sb("OL", [128, 8, 512], R, ph)
        cosA = sb("cosA", [128, 2, 512], F, ph)
        qraw = [sb(f"qraw{i}", [128, 512], F, ph) for i in range(2)]
        pr = [sb(f"pr{i}", [128, 3, 512], F, ph) for i in range(2)]
        aTs = [sb(f"aT{i}", [128, 4, 512], F, ph) for i in range(2)]
        ld_t = load(pool, cosA[:, :, :], tA)

        lv = PP[:, pc["lam"]:pc["lam"] + 256]
        t0 = dve(do(nc.vector.tensor_tensor, qraw[0][:, 0:64], lv[:, 0:64], lv[:, 64:128], ALU.mult), ld_p)
        t1 = dve(do(nc.vector.tensor_tensor, qraw[0][:, 64:128], lv[:, 128:192], lv[:, 192:256], ALU.mult), ld_p)
        t2 = dve(do(nc.vector.tensor_reduce, small[:, 0:2], qraw[0][:, 0:128].rearrange("p (a b) -> p a b", a=2), AX.X, ALU.add), t0, t1)
        t3 = act(do(nc.scalar.activation, small[:, 0:2], small[:, 0:2], ACT.Exp), t2)
        t4 = dve(do(nc.vector.tensor_tensor, small[:, 2:3], small[:, 1:2], small[:, 0:1], ALU.subtract), t3)
        lam_init = 0.8 - 0.6 * math.exp(0.0)
        neglam = dve(do(nc.vector.tensor_scalar, small[:, 2:3], small[:, 2:3], -lam_init, None, ALU.add), t4)
        g8 = dve(do(nc.vector.tensor_scalar, small[:, 3:4], par("subln", 0), 1.0 - lam_init, None, ALU.mult), ld_p)

        qraw_free = [[t2], []]
        nrope = [0]

        def rope_tile(region, t, dst, dst_free, scale, table, perm, C0, prm_region):
            while len(soon) > 1:
                soon.pop(0)()
            i = nrope[0] % 2
            nrope[0] += 1
            q = qraw[i]
            n = C0[1] - C0[0]
            a = act(do(nc.scalar.activation, q[:, 0:n], region[0], ACT.Copy, scale=scale), t, qraw_free[i])
            release(region[2], a)
            out = []

            def rest():
                out.append(rope_rest(region, i, q, n, a, dst, dst_free, table, perm, C0, prm_region))

            soon.append(rest)
            return out

        def rope_rest(region, i, q, n, a, dst, dst_free, table, perm, C0, prm_region):
            t_sw = ones_sum(perm, q, prm_region, True, True, [a] + take(prm_region[2]) + [ld_c], C0[0])
            j, w, fr = temp()
            b = dve(do(nc.vector.tensor_tensor, w[:, 0:n], q[:, 0:n], table[:, 0, :], ALU.mult), a, fr, ld_t)
            c = dve(do(nc.vector.tensor_tensor, dst, prm_region[0], table[:, 1, :], ALU.mult), t_sw, dst_free, ld_t)
            release(prm_region[2], c)
            d = dve(do(nc.vector.tensor_tensor, dst, dst, w[:, 0:n], ALU.add), b, c)
            tmp_free[j] = [d]
            qraw_free[i] = [b, t_sw]
            return d

        layer_const = []

        def decays(l):
            lbv = lbvs[l]
            if l == 0:
                z0 = dve(do(nc.vector.memset, lbv[:, 0:4], 0.0), ld_p)
                z1 = dve(do(nc.vector.memset, lbv[:, 4:8], 1.0), ld_p)
                lb_ready = [z0, z1]
            else:
                l0, l1 = par("lb", 0, 4), par("lb", 4, 4)
                z0 = dve(do(nc.vector.tensor_tensor, lbv[:, 8:12], l0, l1, ALU.max), ld_p)
                z1 = dve(do(nc.vector.tensor_tensor, lbv[:, 12:16], l0, lbv[:, 8:12], ALU.subtract), z0)
                z2 = dve(do(nc.vector.tensor_tensor, lbv[:, 16:20], l1, lbv[:, 8:12], ALU.subtract), z0)
                z3 = act(do(nc.scalar.activation, lbv[:, 12:20], lbv[:, 12:20], ACT.Exp), z1, z2)
                z4 = dve(do(nc.vector.tensor_tensor, lbv[:, 20:24], lbv[:, 12:16], lbv[:, 16:20], ALU.add), z3)
                z5 = dve(do(nc.vector.reciprocal, lbv[:, 20:24], lbv[:, 20:24]), z4)
                z6 = dve(do(nc.vector.tensor_tensor, lbv[:, 0:4], lbv[:, 16:20], lbv[:, 20:24], ALU.mult), z5)
                z7 = dve(do(nc.vector.tensor_tensor, lbv[:, 4:8], lbv[:, 12:16], lbv[:, 20:24], ALU.mult), z5)
                lb_ready = [z6, z7]
            lam = par("lru", 2 * l, 2)
            a0 = dve(do(nc.vector.tensor_scalar, lbv[:, 24:26], lam, -1.0, 0.0, ALU.mult, ALU.max), ld_p)
            a1 = dve(do(nc.vector.tensor_scalar, lbv[:, 26:28], lam, -1.0, None, ALU.mult), ld_p)
            a2 = dve(do(nc.vector.tensor_tensor, lbv[:, 26:28], lbv[:, 26:28], lam, ALU.min), a1)
            a3 = act(do(nc.scalar.activation, lbv[:, 26:28], lbv[:, 26:28], ACT.Exp), a2)
            a4 = dve(do(nc.vector.tensor_scalar, lbv[:, 28:30], lbv[:, 26:28], 2.0, None, ALU.add), a3)
            a5 = dve(do(nc.vector.reciprocal, lbv[:, 28:30], lbv[:, 28:30]), a4)
            a6 = dve(do(nc.vector.tensor_tensor, lbv[:, 26:28], lbv[:, 26:28], lbv[:, 28:30], ALU.mult), a5)
            a7 = dve(do(nc.vector.tensor_tensor, lbv[:, 28:30], lbv[:, 26:28], lbv[:, 26:28], ALU.mult), a6)
            t = dve(do(nc.vector.tensor_scalar, lbv[:, 30:32], lbv[:, 28:30], 1.0 / 17, 1.0 / 15, ALU.mult, ALU.add), a7)
            for n in (13, 11, 9, 7, 5, 3, 1):
                t = dve(do(nc.vector.tensor_tensor, lbv[:, 30:32], lbv[:, 30:32], lbv[:, 28:30], ALU.mult), t)
                t = dve(do(nc.vector.tensor_scalar, lbv[:, 30:32], lbv[:, 30:32], 1.0 / n, None, ALU.add), t)
            t = dve(do(nc.vector.tensor_tensor, lbv[:, 30:32], lbv[:, 30:32], lbv[:, 26:28], ALU.mult), t)
            t = dve(do(nc.vector.tensor_scalar, lbv[:, 30:32], lbv[:, 30:32], 2.0, None, ALU.mult), t)
            t = dve(do(nc.vector.tensor_tensor, lbv[:, 30:32], lbv[:, 30:32], lbv[:, 24:26], ALU.add), t)
            a8 = dve(do(nc.vector.tensor_scalar, lbv[:, 24:26], lbv[:, 30:32], 8.0, None, ALU.mult), t)
            sp_ready = dve(do(nc.vector.tensor_scalar, lbv[:, 26:28], lbv[:, 24:26], -1.0, None, ALU.mult), a8)
            layer_const.append((lb_ready, sp_ready))

        qk_free = [[], []]
        pr_free = [[], []]
        aT_free = [[], []]
        o_ready = [None] * 8
        nat = [(META + 128 * i, META + 128 * i + 128) for i in range(4)]

        def transposes(i, src, aT, bank, waits, afree):
            w = take([bank]) + waits
            for j in range(i + 1):
                t = pe(do(nc.tensor.transpose, P[:, 512 * bank + 128 * j:512 * bank + 128 * j + 128],
                                                  src[:, 128 * j:128 * j + 128], ident), w)
            v = act(do(nc.scalar.activation, aT[:, 0:i + 1, 128 * i:128 * i + 128],
                                           P[:, 512 * bank:512 * bank + 128 * (i + 1)].rearrange("p (j c) -> p j c", c=128),
                                           ACT.Copy), t, afree)
            release([bank], v)
            return t, v

        spare = {"on": True}

        def attn_a(h, g, lane, qk_ready, v_ready):
            b0 = 2 + 2 * lane
            Q, K, V = QT[g % 2], KT[g % 2], VN
            vc = 256 * (g % 2) + 128 * (h % 2)
            hh = h % 2
            p, aT = pr[lane], aTs[lane]
            sm = small[:, 8 + 12 * lane:20 + 12 * lane]
            ev = []
            sfree = [[], []]
            pfree = [pr_free[lane], pr_free[lane]]
            p1_free = [pr_free[lane]]

            def scores(i):
                ke = 128 * (i + 1)
                s = sm[:, 6 * (i % 2):6 * (i % 2) + 6]
                w = take([b0, b0 + 1]) + qk_ready + [ld_c]
                for m in range(2):
                    o = 512 * (b0 + m)
                    pe(do(nc.tensor.matmul, P[:, o:o + ke], Q[64 * m:64 * m + 64, hh, 128 * i:128 * i + 128],
                                                                K[64 * m:64 * m + 64, hh, 0:ke], start=True, stop=False), w)
                    t = pe(do(nc.tensor.matmul, P[:, o + ke - 64:o + ke], mask_u, mask_v, start=False, stop=True), mask_ready)
                both = P[:, 512 * b0:512 * b0 + 1024].rearrange("p (m c) -> p m c", m=2)[:, :, 0:ke]
                return dve(do(nc.vector.tensor_reduce, s[:, 0:2], both, AX.X, ALU.max, negate=True), t, sfree[i % 2])

            def exponentials(i, a):
                ke = 128 * (i + 1)
                s = sm[:, 6 * (i % 2):6 * (i % 2) + 6]
                for m in range(2):
                    x = act(do(nc.scalar.activation, p[:, (i % 2, 2)[m], 0:ke], P[:, 512 * (b0 + m):512 * (b0 + m) + ke], ACT.Exp,
                                                               bias=s[:, m:m + 1], accum_out=s[:, 2 + m:3 + m]),
                            a, (pfree[i % 2], p1_free)[m])
                release([b0, b0 + 1], x)
                return x

            def difference(i, x):
                ke = 128 * (i + 1)
                s = sm[:, 6 * (i % 2):6 * (i % 2) + 6]
                r = dve(do(nc.vector.reciprocal, s[:, 4:6], s[:, 2:4]), x)
                r1 = dve(do(nc.vector.tensor_tensor, s[:, 3:4], s[:, 5:6], small[:, 2:3], ALU.mult), r, neglam)
                c = dve(do(nc.vector.tensor_scalar, p[:, i % 2, 0:ke], p[:, i % 2, 0:ke], s[:, 4:5], None, ALU.mult), r)
                c = dve(do(nc.vector.scalar_tensor_tensor, p[:, i % 2, 0:ke], p[:, 2, 0:ke], s[:, 3:4], p[:, i % 2, 0:ke],
                                                                ALU.mult, ALU.add), c, r1)
                sfree[i % 2] = [c]
                p1_free[:] = [c]
                return c

            x = exponentials(0, scores(0))
            for i in range(4):
                yield [x]
                c = difference(i, x)
                ahead = spare["on"] and i < 3
                if ahead:
                    a = scores(i + 1)
                yield [c]
                if ahead and not spare["on"]:
                    x = exponentials(i + 1, a)
                t, v = transposes(i, p[:, i % 2, :], aT, 6 if spare["on"] else b0, [c], aT_free[lane])
                pfree[i % 2] = [t]
                ev.append(v)
                if ahead and spare["on"]:
                    x = exponentials(i + 1, a)
                if i < 3 and not ahead:
                    x = exponentials(i + 1, scores(i + 1))
            pr_free[lane] = pfree + p1_free
            yield [ev]
            w = take([b0 + 1]) + ev + v_ready
            o = 512 * (b0 + 1)
            for j in range(4):
                t = pe(do(nc.tensor.matmul, P[:, o + 128 * j:o + 512], V[:, j, vc:vc + 128],
                                               aT[:, j, 128 * j:512], start=(j == 0), stop=(j == 3)), w)
            aT_free[lane] = [t]
            att_last[lane] = t
            att_of.setdefault(g, []).append(t)
            yield []
            i1, q, fr = temp()
            s = act(do(nc.scalar.activation, q[:, 0:512], P[:, o:o + 512], ACT.Square), t, fr)
            yield
            t_ms = pe(do(nc.tensor.matmul, P[:, 512 * b0:512 * b0 + 512], ones_head, q[:, 0:512], start=True, stop=True),
                      s, take([b0]))
            yield
            a, b = inv_root(q[:, 0:512], P[:, 512 * b0:512 * b0 + 512], eps5, [t_ms])
            release([b0], a)
            n = dve(do(nc.vector.scalar_tensor_tensor, q[:, 0:512], P[:, o:o + 512], small[:, 3:4], q[:, 0:512],
                                                     ALU.mult, ALU.mult), b, g8)
            release([b0 + 1], n)
            th, tl = split(q[:, 0:512], OH[:, h, :], OL[:, h, :], [n], None)
            tmp_free[i1] = [th, tl]
            o_ready[h] = [th, tl]

        att_last = [None, None]
        att_of = {}
        lanes = Lanes()
        for g in range(4):
            ready = []
            early = products(units(3), XH, XL, xr, [one(0), one(1), one(2)]) if g == 0 else []
            for part, dst in ((0, QT), (1, KT)):
                for j in range(2):
                    n = 2 * part + j
                    if early and n < 3:
                        r, t = one(n), early[n]
                    else:
                        r = one(n % 2)
                        t = product(units(1), XH, XL, xr, r)
                    if n == 0 and g >= 2:
                        lanes.wait(g - 1)
                        qk_free[g % 2] = att_of[g - 2]
                    ready.append(rope_tile(r, t, dst[g % 2][:, j, :], qk_free[g % 2], 0.125 if part == 0 else 1.0,
                                           cosA, perm_a, (META, T), one(6)))
            while soon:
                soon.pop(0)()
            if g % 2 == 0:
                spare["on"] = False
                t = widest_product(nat, (0, 1, 6, 7), xr)
                lanes.wait(g)
                vt = []
                for n, bk in enumerate((0, 1, 6, 7)):
                    v = act(do(nc.scalar.activation, VN[:, n, :], P[:, 512 * bk:512 * bk + 512], ACT.Copy), t, att_last)
                    release([bk], v)
                    vt.append(v)
                spare["on"] = True
            for n in range(2):
                lanes.tasks[n].append(attn_a(2 * g + n, g, n, ready, vt))
        x_read[:] = [pe_done[unit[0] - 1]]
        us = units(3)
        lanes.wait(3)
        begin_tiles(us, OH, OL, o_ready, [ln_region(m) for m in range(3)], 6, META)
        lanes.finish()
        residual_ln(0, 0, lambda m, r: end_tile(us[m], OH, OL, o_ready, r, 6, META) if m < 3 else
                    product(units(1), OH, OL, o_ready, r, lo_col=META))
        ph.close()

        def swiglu(l):
            ph = ExitStack()
            fence = phase_fence()
            HH = sb(f"HH{l}", [128, NF, 512], R, ph)
            HL = sb(f"HL{l}", [128, NF, 512], R, ph)
            hr = []
            early = products(units(3), XH, XL, xr, [one(0), one(1), one(2)])

            def tile(n):
                if n == 5 + 2 * l:
                    decays(l)
                r = one(n % 4)
                return r, early[n] if n < 3 else product(units(1), XH, XL, xr, r)

            for m in range(NF):
                rg, tg = tile(2 * m)
                i, q, fr = temp()
                a = act(do(nc.scalar.activation, q[:, 0:512], rg[0], ACT.Silu), tg, fr)
                release(rg[2], a)
                ru, tu = tile(2 * m + 1)
                b = dve(do(nc.vector.tensor_tensor, q[:, 0:512], q[:, 0:512], ru[0], ALU.mult), a, tu)
                release(ru[2], b)
                th, tl = split(q[:, 0:512], HH[:, m, :], HL[:, m, :], [b], fence)
                tmp_free[i] = [th, tl]
                hr.append([th, tl])
            x_read[:] = [pe_done[unit[0] - 1]]
            residual_ln(l, 1, lambda m, r: product(units(3), HH, HL, hr, r, lo_col=META))
            ph.close()

        swiglu(0)

        ph = ExitStack()
        fence = phase_fence()
        QB = [sb(f"QB{i}", [128, 2, 512], F, ph) for i in range(2)]
        KB_ = [sb(f"KB{i}", [128, 2, 512], F, ph) for i in range(2)]
        VB = sb("VB", [128, 4, 512], F, ph)
        OH2 = sb("OH2", [128, 8, 512], R, ph)
        OL2 = sb("OL2", [128, 8, 512], R, ph)
        bT = sb("bT", [128, 4, 512], F, ph)
        prB = [sb(f"prB{i}", [128, 2, 512], F, ph) for i in range(2)]
        aTB = [sb(f"aTB{i}", [128, 4, 512], F, ph) for i in range(2)]
        oB = [sb(f"oB{i}", [128, 512], F, ph) for i in range(2)]
        pr_free = [fence, fence]
        aT_free = [fence, fence]
        bt_free = [fence] * 4
        qk_free = [fence, fence]
        ob_free = [fence, fence]
        att_last = [None, None]
        o_ready = [None] * 8

        def attn_b(tile, g, lane, qk_ready, v_ready):
            b0 = 2 + 2 * lane
            Q, K, V = QB[g % 2], KB_[g % 2], VB
            vc = 256 * (g % 2) + 128 * (tile % 2)
            hh = tile % 2
            p, aT = prB[lane], aTB[lane]
            sm = small[:, 8 + 12 * lane:20 + 12 * lane]
            ob = oB[lane]
            sfree = [[], []]
            pfree = [pr_free[lane], pr_free[lane]]
            cut = []
            for half in range(2):
                h = 2 * tile + half
                s0 = 64 * half
                slot = 2 * lane + half
                ld_b = load(pool, bT[:, slot, :], biasT[h, :, :], bt_free[slot])
                ev = []

                def scores(i):
                    ke = 128 * (i + 1)
                    o = 512 * b0
                    q, m = p[:, i % 2, 0:ke], sm[:, 6 * (i % 2):6 * (i % 2) + 6]
                    pe(do(nc.tensor.matmul, P[:, o:o + ke], Q[s0:s0 + 64, hh, 128 * i:128 * i + 128],
                          K[s0:s0 + 64, hh, 0:ke], start=True, stop=False), take([b0]) + qk_ready)
                    t = pe(do(nc.tensor.matmul, P[:, o + ke - 64:o + ke], mask_u, mask_v, start=False, stop=True), mask_ready)
                    c = dve(do(nc.vector.tensor_tensor, q, P[:, o:o + ke], bT[:, slot, 512 - ke:512], ALU.add),
                            t, pfree[i % 2], ld_b)
                    release([b0], c)
                    return dve(do(nc.vector.tensor_reduce, m[:, 0:1], q, AX.X, ALU.max, negate=True), c, sfree[i % 2]), c

                def exponentials(i, a):
                    q, m = p[:, i % 2, 0:128 * (i + 1)], sm[:, 6 * (i % 2):6 * (i % 2) + 6]
                    return act(do(nc.scalar.activation, q, q, ACT.Exp, bias=m[:, 0:1], accum_out=m[:, 1:2]), a)

                def normal(i, x):
                    ke = 128 * (i + 1)
                    q, m = p[:, i % 2, 0:ke], sm[:, 6 * (i % 2):6 * (i % 2) + 6]
                    r = dve(do(nc.vector.reciprocal, m[:, 2:3], m[:, 1:2]), x)
                    c = dve(do(nc.vector.tensor_scalar, q, q, m[:, 2:3], None, ALU.mult), r)
                    sfree[i % 2] = [c]
                    return c

                a, fb = scores(0)
                x = exponentials(0, a)
                for i in range(4):
                    yield [x]
                    c = normal(i, x)
                    if i < 3:
                        a, fb = scores(i + 1)
                    yield [c]
                    t, v = transposes(i, p[:, i % 2, :], aT, b0 + 1, [c], aT_free[lane])
                    pfree[i % 2] = [t]
                    ev.append(v)
                    if i < 3:
                        x = exponentials(i + 1, a)
                yield ev
                bt_free[slot] = [fb]
                o = 512 * (b0 + 1)
                w = take([b0 + 1]) + ev + v_ready
                for j in range(4):
                    t = pe(do(nc.tensor.matmul, P[s0:s0 + 64, o + 128 * j:o + 512],
                                                          V[:, j, vc + s0:vc + s0 + 64],
                                                          aT[:, j, 128 * j:512], start=(j == 0), stop=(j == 3)), w)
                aT_free[lane] = [t]
                a = act(do(nc.scalar.activation, ob[s0:s0 + 64, :], P[s0:s0 + 64, o:o + 512], ACT.Copy), t, ob_free[lane])
                release([b0 + 1], a)
                cut.append(a)
                pfree = [pfree[0], pfree[1]]
                yield []
            pr_free[lane] = pfree
            att_last[lane] = t
            att_of.setdefault(g, []).append(t)
            a = cut
            th, tl = split(ob[:, :], OH2[:, tile, :], OL2[:, tile, :], [a], fence)
            ob_free[lane] = [th, tl]
            o_ready[tile] = [th, tl]

        att_of = {}
        lanes = Lanes()
        for g in range(4):
            ready = []
            early = products(units(3), XH, XL, xr, [one(0), one(1), one(2)]) if g == 0 else []
            for part, dst in ((0, QB), (1, KB_)):
                for j in range(2):
                    n = 2 * part + j
                    if early and n < 3:
                        r, t = one(n), early[n]
                    else:
                        r = one(n % 2)
                        t = product(units(1), XH, XL, xr, r)
                    if n == 0 and g >= 2:
                        lanes.wait(g - 1)
                        qk_free[g % 2] = att_of[g - 2]
                    a = act(do(nc.scalar.activation, dst[g % 2][:, j, :], r[0], ACT.Copy, scale=0.125 if part == 0 else 1.0), t, qk_free[g % 2])
                    release(r[2], a)
                    ready.append(a)
            if g % 2 == 0:
                t = widest_product(nat, (0, 1, 6, 7), xr)
                lanes.wait(g)
                vt = []
                for n, bk in enumerate((0, 1, 6, 7)):
                    v = act(do(nc.scalar.activation, VB[:, n, :], P[:, 512 * bk:512 * bk + 512], ACT.Copy), t, fence, att_last)
                    release([bk], v)
                    vt.append(v)
            for n in range(2):
                lanes.tasks[n].append(attn_b(2 * g + n, g, n, ready, vt))
        x_read[:] = [pe_done[unit[0] - 1]]
        us = units(3)
        lanes.wait(3)
        begin_tiles(us, OH2, OL2, o_ready, [ln_region(m) for m in range(3)], 6, META)
        lanes.finish()
        residual_ln(1, 0, lambda m, r: end_tile(us[m], OH2, OL2, o_ready, r, 6, META) if m < 3 else
                    product(units(1), OH2, OL2, o_ready, r, lo_col=META))
        ph.close()
        swiglu(1)

        def add_square(m):
            if m == 0:
                squares["sum"] = act(do(nc.scalar.activation, rstd[:, :], X[:, 0, :], ACT.Square), x_done[0], rstd_free)
                return
            i, q, fr = temp()
            s = act(do(nc.scalar.activation, q[:, :], X[:, m, :], ACT.Square), x_done[m], fr)
            if m < 7:
                squares["sum"] = dve(do(nc.vector.tensor_tensor, rstd[:, :], rstd[:, :], q[:, :], ALU.add), s, squares["sum"])
                tmp_free[i] = [squares["sum"]]
                return
            ms = two(3)
            ones_sum(ones_mean, rstd, ms, True, False, [squares["sum"], ld_c] + take(ms[2]))
            squares["all"] = ones_sum(ones_mean, q, ms, False, True, [s])
            tmp_free[i] = [squares["all"]]

        def rms(g0, final=False):
            ms = two(3)
            if not final:
                need(st["cur"] + NS)
            a, b = inv_root(rstd[:, :], ms[0], eps6, [squares.pop("all"), rstd_free])
            release(ms[2], a)
            for m in range(8):
                i, q, fr = temp()
                n = dve(do(nc.vector.scalar_tensor_tensor, q[:, :], X[:, m, :], PP[:, g0 + m:g0 + m + 1], rstd[:, :],
                           ALU.mult, ALU.mult), b, fr, x_done[m])
                if final:
                    tok = load(sp, out[:, m, :], q[:, C1], n)
                    outs.append(tok)
                    tmp_free[i] = [tok]
                else:
                    th, tl = split(q[:, :], XH[:, m, :], XL[:, m, :], [n], x_read)
                    tmp_free[i] = [th, tl]
                    xr[m] = [th, tl]
            rstd_free[:] = [n]

        def residual(tiles, pairs):
            ln_exp_tables()
            for m in range(8):
                r = two(m % pairs)
                t = tiles(m, r)
                v = dve(do(nc.vector.tensor_tensor, X[:, m, :], X[:, m, :], r[0], ALU.add), t, x_done[m])
                release(r[2], v)
                x_done[m] = [v]
                add_square(m)

        outs = []
        nat5 = [(0, META)] + nat

        def mixer(l):
            ph = ExitStack()
            fence = phase_fence()
            GH = sb(f"GH{l}", [128, 8, T], R, ph)
            GL = sb(f"GL{l}", [128, 8, T], R, ph)
            VI = sb(f"VI{l}", [128, 5, 512], F, ph)
            VR = sb(f"VR{l}", [128, 5, 256], F, ph)
            maskw = sb(f"masks{l}", [128, 256], mybir.dt.int32, ph)
            masks = maskw[:, :].bitcast(U8).rearrange("p (l c) -> p l c", l=8)
            SC = sb(f"SC{l}", [128, 2560], F, ph)
            SM = sb(f"SM{l}", [16, T], F, ph)
            A, B, K, Q0, G, QA, KB = (sb(f"{n}{l}", [128, T], F, ph) for n in ("hA", "hB", "hK", "hQ", "hG", "hQA", "hKB"))
            Qs = (Q0, rstd)
            G2 = sb(f"hG2{l}", [128, T], F, ph)
            tab = sb(f"tab{l}", [128, 2, T], F, ph)
            dec = [sb(f"dec{l}{i}", [128, T], F, ph) for i in range(2)]
            gw = sb(f"gw{l}", [128, 4, 128], F, ph)
            LX = sb(f"LX{l}", [128, 2, T + 3], F, ph)
            ld_mask = load(pool, maskw[:, :], cstm, fence)
            ld_tab = load(pool, tab[:, :, :], tR, fence)
            ld_gw = load(pool, gw[:, :, :], gates[l, :, :, :], fence)
            first = {}

            def fr(name):
                if name in first:
                    return first[name]
                return fence

            lb_ready, sp_ready = layer_const[l]
            lbv = lbvs[l]
            sc_zero = pool(do(nc.gpsimd.memset, SC[:, :], 0.0), fence)
            sm_zero = pool(do(nc.gpsimd.memset, SM[:, :], 0.0), fence)
            lx_zero = pool(do(nc.gpsimd.memset, LX[:, :, 0:3], 0.0), fence)
            first["SC"] = [sc_zero]
            first["SM"] = [sm_zero]

            rot = [0]
            st["share"] = True

            def region():
                rot[0] += 1
                return two(rot[0] % 2)

            vi_ready, vr_ready = [], []

            def nat5_region(n):
                b = 2 * (n % 2) + (n // 2) % 2
                return P[0:(16 if n == 0 else 128), 512 * b:512 * b + 256], [b]

            def keep(dst, c0, lst):
                def f(n, o, t):
                    k = 16 if n == 0 else 128
                    v = act(do(nc.scalar.activation, dst[0:k, n, c0:c0 + 256], o, ACT.Copy), t, fence)
                    lst.append(v)
                    return [v]
                return f

            def out_split(src, k, waits, ti):
                th, tl = split(src, GH[:, k, :], GL[:, k, :], waits, fence)
                if ti is not None:
                    tmp_free[ti] = [th, tl]
                g_ready[k] = [th, tl]
                return [th, tl]

            g_ready = [None] * 8

            def segments(c0, c1):
                return [(a, b) for a, b in ((c0, min(c1, 264)), (max(c0, 264), c1)) if a < b]

            def level(src, sz, c0, c1):
                return src[:, c0:c1].rearrange("p (n h s) -> p n h s", h=2, s=sz)

            hg_scored, hg_done = [], []
            QAs, KBs = (QA, dec[0]), (KB, dec[1])
            qb_free = [fence, fence]

            def hgrn(h, toks):
                zA, zK, zQ, zG = toks
                Q = Qs[h % 2]
                Gb = (G, G2)[h % 2]
                now = {"A": zA, "B": pool(do(nc.gpsimd.memset, B[:, :], 1.0), fr("B"))}
                scd = SC[:, 0:2560].rearrange("p (j c) -> p j c", c=640)[:, :, 0:128]
                done = []

                def prep(lev):
                    if lev < 0:
                        return Q, K, [zQ, zK]
                    b, sz, c0 = lev % 2, 1 << lev, 0 if lev < 4 else META
                    qa, kb = QAs[b], KBs[b]
                    Av, Bv, Qv, Kv, QAv, KBv = (level(x, sz, c0, T) for x in (A, B, Q, K, qa, kb))
                    if lev < 2:
                        d1 = dve(do(nc.vector.tensor_tensor, qa[:, :], Q[:, :], A[:, :], ALU.mult), now["A"], zQ, qb_free[b])
                    else:
                        d1 = dve(do(nc.vector.tensor_tensor, QAv[:, :, 1, :], Qv[:, :, 1, :], Av[:, :, 1, :], ALU.mult),
                                 now["A"], zQ, qb_free[b])
                    if lev == 0:
                        kb, d2 = K, zK
                    elif lev < 3:
                        d2 = dve(do(nc.vector.tensor_tensor, kb[:, :], K[:, :], B[:, :], ALU.mult), now["B"], zK, qb_free[b])
                    else:
                        d2 = dve(do(nc.vector.tensor_tensor, KBv[:, :, 0, :], Kv[:, :, 0, :], Bv[:, :, 0, :], ALU.mult),
                                 now["B"], zK, qb_free[b])
                    nb = (T - c0) // (2 * sz)
                    if lev < 8:
                        ea = Av[:, :, 1, sz - 1:sz].broadcast_to([128, nb, sz])
                        now["B"] = dve(do(nc.vector.tensor_tensor, Bv[:, :, 0, :], Bv[:, :, 0, :], ea, ALU.mult),
                                       now["A"], now["B"], d2)
                    eb = Av[:, :, 0, sz - 1:sz].broadcast_to([128, nb, sz])
                    now["A"] = dve(do(nc.vector.tensor_tensor, Av[:, :, 1, :], Av[:, :, 1, :], eb, ALU.mult),
                                   now["A"], now["B"], d1)
                    return qa, kb, [d1, d2]

                p = prep(-1)
                for lev in range(-1, 7):
                    qa, kb, wq = p
                    p = prep(lev + 1)
                    bx, bm = 4, 5
                    w = wq + take([bx])
                    for j in range(4):
                        c = META + 128 * j
                        t = pe(do(nc.tensor.matmul, P[:, 512 * bx + 128 * j:512 * bx + 128 * j + 128], kb[:, c:c + 128],
                                  qa[:, c:c + 128], start=(j == 0), stop=(j == 3), skip_group_check=True), w)
                    if lev < 4:
                        tm = pe(do(nc.tensor.matmul, P[0:16, 512 * bm:512 * bm + 16], kb[:, 0:16], qa[:, 0:16],
                                   start=True, stop=True), take([bm]))
                        mm = dve(do(nc.vector.copy_predicated, SM[:, 0:16], masks[0:16, lev + 1, 0:16],
                                    P[0:16, 512 * bm:512 * bm + 16]), tm, fr("SM"), done, ld_mask)
                        release([bm], mm)
                        t = tm
                    if lev >= 0:
                        qb_free[lev % 2] = [t]
                    mk = masks[:, lev + 1, :].unsqueeze(1).broadcast_to([128, 4, 128])
                    cp = dve(do(nc.vector.copy_predicated, scd, mk,
                                P[:, 512 * bx:512 * bx + 512].rearrange("p (j c) -> p j c", c=128)), t, fr("SC"), done, ld_mask)
                    release([bx], cp)
                    done = [mm, cp]
                    yield
                dense = []
                for lev, blocks in ((7, ((0, 128, 256), (2, 384, 512))), (8, ((0, 256, 512), (1, 256, 512)))):
                    qa, kb, wq = p
                    if lev == 7:
                        p = prep(8)
                    else:
                        d1 = dve(do(nc.vector.tensor_tensor, QAs[1][:, META:T], Q[:, META:T], A[:, META:T], ALU.mult),
                                 now["A"], qb_free[1])
                        d2 = dve(do(nc.vector.tensor_tensor, KBs[1][:, 0:META], K[:, 0:META], B[:, 0:META], ALU.mult),
                                 now["B"], qb_free[1])
                    bx = 4
                    w = wq + take([bx])
                    o = 512 * bx
                    evs = []
                    for n, (js, c0, c1) in enumerate(blocks):
                        t = pe(do(nc.tensor.matmul, P[:, o:o + c1 - c0], kb[:, META + 128 * js:META + 128 * js + 128],
                                  qa[:, META + c0:META + c1], start=(n == 0), stop=(n == 1), skip_group_check=True), w)
                        evs.append((js, c0, c1, o))
                        o += c1 - c0
                    qb_free[lev % 2] = [t]
                    for js, c0, c1, oo in evs:
                        v = act(do(nc.scalar.activation, SC[:, 512 * js + c0:512 * js + c1], P[:, oo:oo + c1 - c0], ACT.Copy),
                                t, fr("SC"))
                        dense.append(v)
                    release([bx], v)
                    yield
                t = pe(do(nc.tensor.matmul, P[0:16, 512 * 5:512 * 6], KBs[1][:, 0:16], QAs[1][:, META:T], start=True, stop=True),
                       d1, d2, take([5]))
                v = act(do(nc.scalar.activation, SM[:, META:T], P[0:16, 512 * 5:512 * 6], ACT.Copy), t, fr("SM"))
                release([5], v)
                dense.append(v)
                qb_free[1] = [t]
                acc = done
                yield
                first["A"] = first["B"] = first["K"] = first[f"Q{h % 2}"] = [d1, d2, t]
                reg = two(3)
                w = take(reg[2]) + dense + acc + vi_ready
                o = 1024 * 3 + 248
                for a, b in segments(0, T):
                    t = pe(do(nc.tensor.matmul, P[:, o + a:o + b], VI[0:16, 0, 128 * h:128 * h + 128], SM[:, a:b],
                                                        start=True, stop=False, skip_group_check=True), w)
                for j in range(4):
                    s0 = META + 128 * j
                    for a, b in segments(s0, T):
                        t = pe(do(nc.tensor.matmul, P[:, o + a:o + b], VI[:, 1 + j, 128 * h:128 * h + 128], SC[:, 512 * j + a - META:512 * j + b - META],
                            start=False, stop=True, skip_group_check=True), w)
                first["SC"] = first["SM"] = [t]
                hg_scored.append(h)
                yield
                i, q, f_ = temp()
                s = act(do(nc.scalar.activation, q[:, :], reg[0], ACT.Square), t, f_)
                yield
                r2 = two(2)
                t2 = ones_sum(ones_head, q, r2, True, True, [s] + take(r2[2]))
                a_, b_ = inv_root(q[:, :], r2[0], eps6, [t2])
                release(r2[2], a_)
                n1 = dve(do(nc.vector.scalar_tensor_tensor, q[:, :], reg[0], par("hgn", l), q[:, :], ALU.mult, ALU.mult), b_)
                release(reg[2], n1)
                n2 = dve(do(nc.vector.tensor_tensor, q[:, :], q[:, :], Gb[:, :], ALU.mult), n1, zG)
                out_split(q[:, :], h, [n2], i)
                first[f"G{h % 2}"] = [n2]
                hg_done.append(h)

            def last_of(name):
                return first.get(name, fence)

            t = widest_product([nat5[1], nat5[2], nat5[3], nat5[4], nat5[0]], (0, 1, 2, 3, 4), xr)
            for n, bk in ((1, 0), (2, 1), (3, 2), (4, 3), (0, 4)):
                k = 128 if n else META
                v = act(do(nc.scalar.activation, VI[0:k, n, :], P[0:k, 512 * bk:512 * bk + 512], ACT.Copy), t, fence)
                release([bk], v)
                vi_ready.append(v)

            for h in range(4):

                def tile():
                    r = region()
                    return r, product(units(1), XH, XL, xr, r)

                if h >= 2:
                    until(lambda: h - 2 in hg_done)
                r, t = tile()
                Gb = (G, G2)[h % 2]
                zG = act(do(nc.scalar.activation, Gb[:, :], r[0], ACT.Silu), t, last_of(f"G{h % 2}"))
                release(r[2], zG)
                r, t = tile()
                zQ = act(do(nc.scalar.activation, Qs[h % 2][:, :], r[0], ACT.Silu), t, last_of(f"Q{h % 2}"), rstd_free)
                release(r[2], zQ)
                r, t = tile()
                until(lambda: h == 0 or h - 1 in hg_scored)
                i, q, f_ = temp()
                j, q2, f2 = temp()
                s1 = act(do(nc.scalar.activation, q[:, :], r[0], ACT.Sigmoid), t, f_)
                s2 = act(do(nc.scalar.activation, q2[:, :], r[0], ACT.Sigmoid, scale=-1.0), t, f2)
                release(r[2], s2)
                zA = dve(do(nc.vector.tensor_scalar, A[:, :], q[:, :], lbv[:, 4 + h:5 + h], lbv[:, h:h + 1],
                            ALU.mult, ALU.add), s1, lb_ready, last_of("A"))
                zK = dve(do(nc.vector.tensor_scalar, K[:, :], q2[:, :], lbv[:, 4 + h:5 + h], float(128 ** -0.5),
                            ALU.mult, ALU.mult), s2, lb_ready, last_of("K"))
                tmp_free[i], tmp_free[j] = [zA], [zK]
                behind(hgrn(h, (zA, zK, zQ, zG)))

            lx_t, ly_t, gr = [], [], []
            for n in range(2):
                r = region()
                t = product(units(1), XH, XL, xr, r)
                v = act(do(nc.scalar.activation, LX[:, n, 3:T + 3], r[0], ACT.Copy), t, fence)
                release(r[2], v)
                lx_t.append(v)
            u = units(2)
            wide_product(u[0], nat5, nat5_region, keep(VR, 0, vr_ready), xr)

            def ret_gate(n):
                r = region()
                t = product(units(1), XH, XL, xr, r)
                v = act(do(nc.scalar.activation, (G, G2)[n][:, :], r[0], ACT.Silu), t, first[f"G{n}"])
                release(r[2], v)
                gr.append(v)

            until(lambda: 2 in hg_done)
            ret_gate(0)
            until(lambda: 3 in hg_scored)
            LY = (QA, KB)
            LR = [K, Q0, rstd]

            def lru():
                lrf = [first["K"], first["Q0"], first["Q1"]]
                for n in range(2):
                    Y = LR[0]
                    x = LX[:, n, :]

                    def cw(j, n=n):
                        return PP[:, pc["lcw"] + 8 * l + 2 * j + n:pc["lcw"] + 8 * l + 2 * j + n + 1]

                    c = dve(do(nc.vector.tensor_scalar, Y[:, :], x[:, 3:T + 3], cw(3), par("lcb", 2 * l + n), ALU.mult, ALU.add),
                            lx_t[n], lx_zero, lrf[0])
                    for j in range(3):
                        c = dve(do(nc.vector.scalar_tensor_tensor, Y[:, :], x[:, j:j + T], cw(j), Y[:, :], ALU.mult, ALU.add), c)
                    yield
                    rg_ = two(2)
                    t = ones_sum(gw[:, n, :], Y, rg_, True, True, [c, ld_gw] + take(rg_[2]))
                    s1 = act(do(nc.scalar.activation, LR[1][:, :], rg_[0], ACT.Sigmoid, bias=par("gab", 2 * l + n)), t, lrf[1])
                    release(rg_[2], s1)
                    ri = two(2)
                    t = ones_sum(gw[:, 2 + n, :], Y, ri, True, True, [c, ld_gw] + take(ri[2]))
                    s2 = act(do(nc.scalar.activation, LR[2][:, :], ri[0], ACT.Sigmoid, bias=par("gib", 2 * l + n)), t, lrf[2])
                    release(ri[2], s2)
                    yield
                    i, q, f1 = temp()
                    th = act(do(nc.scalar.activation, q[:, :], LR[1][:, :], ACT.Tanh, scale=lbv[:, 24 + n:25 + n]), s1, f1, sp_ready)
                    ea = act(do(nc.scalar.activation, LR[1][:, :], LR[1][:, :], ACT.Exp, scale=lbv[:, 26 + n:27 + n]), th, sp_ready)
                    ix = dve(do(nc.vector.tensor_tensor, Y[:, :], Y[:, :], LR[2][:, :], ALU.mult), s2, t)
                    a2 = dve(do(nc.vector.tensor_tensor, LR[2][:, :], LR[1][:, :], LR[1][:, :], ALU.mult), ea, ix)
                    a3 = dve(do(nc.vector.scalar_tensor_tensor, q[:, :], LR[2][:, :], 1.0, q[:, :], ALU.add, ALU.mult), a2, th)
                    a4 = act(do(nc.scalar.activation, q[:, :], q[:, :], ACT.Sqrt), a3)
                    a5 = dve(do(nc.vector.tensor_tensor, Y[:, :], Y[:, :], q[:, :], ALU.mult), a4, ix)
                    a6 = dve(do(nc.vector.tensor_tensor_scan, q[:, :], LR[1][:, :], Y[:, :], 0.0, ALU.mult, ALU.add), a5, ea)
                    a7 = dve(do(nc.vector.tensor_tensor, q[:, :], q[:, :], LY[n][:, :], ALU.mult), a6, ly_t[n])
                    o = out_split(q[:, :], 6 + n, [a7], i)
                    lrf = [[a5, a6], [a6], [a3]]
                    lr_end[:] = [a5, a6, a7]
                    yield

            lr_end = []
            dec_free = []
            QR, KR = A, B
            rr = []
            for n, (dst, name) in enumerate(((QR, "A"), (KR, "B"))):
                r = region()
                t = product(units(1), XH, XL, xr, r)
                qx = dec[n]
                a = act(do(nc.scalar.activation, qx[:, :], r[0], ACT.Copy), t, qb_free)
                release(r[2], a)

                def rest(qx=qx, a=a, dst=dst, name=name):
                    pr_ = two(2)
                    ts = ones_sum(perm_r, qx, pr_, True, True, [a] + take(pr_[2]))
                    i, w_, f1 = temp()
                    b = dve(do(nc.vector.tensor_tensor, w_[:, :], qx[:, :], tab[:, 0, :], ALU.mult), a, f1, ld_tab)
                    c = dve(do(nc.vector.tensor_tensor, dst[:, :], pr_[0], tab[:, 1, :], ALU.mult), ts, first[name], ld_tab)
                    release(pr_[2], c)
                    d = dve(do(nc.vector.tensor_tensor, dst[:, :], dst[:, :], w_[:, :], ALU.add), b, c)
                    tmp_free[i] = [d]
                    rr.append(d)
                    dec_free.append([b, ts])

                soon.append(rest)

            def retention():
                while len(dec_free) < 2 or 3 not in hg_done:
                    yield
                dfree = list(dec_free)
                for n in range(2):
                    reg = two(3)
                    wo = take(reg[2])
                    o = 1024 * 3 + 248
                    for half in range(2):
                        hh = 2 * n + half
                        dc = dec[half]
                        ld_d = load(pool, dc[:, :], dt_h[hh, :, :], dfree[half])
                        tl_ = []
                        r2 = two(2)
                        w = take(r2[2]) + rr
                        for a, b in segments(0, T):
                            t = pe(do(nc.tensor.matmul, P[0:16, 1024 * 2 + 248 + a:1024 * 2 + 248 + b], KR[32 * hh:32 * hh + 32, 0:16],
                                QR[32 * hh:32 * hh + 32, a:b], start=True, stop=True), w)
                        v = dve(do(nc.vector.tensor_tensor, SM[:, :], P[0:16, 2296:2296 + T], dc[0:16, :], ALU.mult),
                                t, ld_d, first["SM"])
                        release(r2[2], v)
                        tl_.append(v)
                        for j in range(4):
                            bk = (4, 5)[j % 2]
                            m = 512 - 128 * j
                            t = pe(do(nc.tensor.matmul, P[:, 512 * bk:512 * bk + m], KR[32 * hh:32 * hh + 32, META + 128 * j:META + 128 * j + 128],
                                QR[32 * hh:32 * hh + 32, META + 128 * j:T], start=True, stop=True), take([bk]))
                            v = dve(do(nc.vector.tensor_tensor, SC[:, 640 * j:640 * j + m], P[:, 512 * bk:512 * bk + m], dc[:, 0:m], ALU.mult), t, first["SC"])
                            release([bk], v)
                            tl_.append(v)
                        dfree[half] = [v]
                        yield
                        s0 = 64 * half
                        for a, b in segments(0, T):
                            t = pe(do(nc.tensor.matmul, P[s0:s0 + 64, o + a:o + b], VR[0:16, 0, 64 * hh:64 * hh + 64], SM[:, a:b],
                                start=True, stop=False, skip_group_check=True), wo + tl_ + vr_ready)
                        for j in range(4):
                            c0 = META + 128 * j
                            for a, b in segments(c0, T):
                                t = pe(do(nc.tensor.matmul, P[s0:s0 + 64, o + a:o + b], VR[:, 1 + j, 64 * hh:64 * hh + 64],
                                    SC[:, 640 * j + a - c0:640 * j + b - c0], start=False, stop=True, skip_group_check=True))
                        first["SC"] = first["SM"] = [t]
                        yield
                    i, q, f1 = temp()
                    a = act(do(nc.scalar.activation, q[:, :], reg[0], ACT.Copy), t, f1)
                    release(reg[2], a)
                    yield
                    r2 = two(2)
                    t = ones_sum(ones_ret, q, r2, True, True, [a] + take(r2[2]))
                    c = dve(do(nc.vector.tensor_tensor, q[:, :], q[:, :], r2[0], ALU.subtract), t)
                    release(r2[2], c)
                    yield
                    k, q2, f2 = temp()
                    s = act(do(nc.scalar.activation, q2[:, :], q[:, :], ACT.Square), c, f2)
                    yield
                    t = ones_sum(ones_ret, q2, r2, True, True, [s] + take(r2[2]))
                    x1, x2 = inv_root(q2[:, :], r2[0], eps6, [t])
                    release(r2[2], x1)
                    c = dve(do(nc.vector.scalar_tensor_tensor, q[:, :], q[:, :], par("retn", l), q2[:, :],
                                                                         ALU.mult, ALU.mult), x2, c)
                    tmp_free[k] = [c]
                    Gb = (G, G2)[n]
                    while len(gr) <= n:
                        yield
                    c = dve(do(nc.vector.tensor_tensor, q[:, :], q[:, :], Gb[:, :], ALU.mult), c, gr[n])
                    out_split(q[:, :], 4 + n, [c], i)
                    yield

            behind(retention())
            for n in range(2):
                r = region()
                t = product(units(1), XH, XL, xr, r)
                v = act(do(nc.scalar.activation, LY[n][:, :], r[0], ACT.Gelu_apprx_tanh), t, qb_free)
                release(r[2], v)
                ly_t.append(v)
            behind(lru())
            until(lambda: 3 in hg_done)
            ret_gate(1)
            x_read[:] = [pe_done[unit[0] - 1]]
            us = units(2)
            begin_tiles(us, GH, GL, g_ready, [two(0), two(1)], 4)
            drain()
            rstd_free[:] = lr_end
            residual(lambda m, r: end_tile(us[m], GH, GL, g_ready, r, 4) if m < 2 else
                     product(units(1), GH, GL, g_ready, r), 3)
            st["share"] = False
            ph.close()

        def conv_glu(l):
            ph = ExitStack()
            fence = phase_fence()
            HH = sb(f"GHH{l}", [128, NF, T], R, ph)
            HL = sb(f"GHL{l}", [128, NF, T], R, ph)
            hr = []

            def conv_tile(r, t, c):
                def w(j):
                    k = pc["fcw"] + 132 * l + 44 * j + c
                    return PP[:, k:k + 1]
                i, y, f_ = temp()
                p = r[0]
                a = act(do(nc.scalar.activation, y[:, :], p, ACT.Identity, bias=par("fcb", 44 * l + c), scale=w(2)), t, f_)
                b = dve(do(nc.vector.scalar_tensor_tensor, y[:, 1:T], p[:, 0:T - 1], w(1), y[:, 1:T], ALU.mult, ALU.add), a)
                b = dve(do(nc.vector.scalar_tensor_tensor, y[:, 2:T], p[:, 0:T - 2], w(0), y[:, 2:T], ALU.mult, ALU.add), b)
                release(r[2], b)
                return i, y, b

            early = products(units(3), XH, XL, xr, [two(0), two(1), two(2)])

            def tile(n):
                r = two(n % 4)
                return r, early[n] if n < 3 else product(units(1), XH, XL, xr, r)

            for m in range(NF):
                r, t = tile(2 * m)
                i, yg, tg = conv_tile(r, t, m)
                a = act(do(nc.scalar.activation, yg[:, :], yg[:, :], ACT.Silu), tg)
                r, t = tile(2 * m + 1)
                j, yv, tv = conv_tile(r, t, NF + m)
                b = dve(do(nc.vector.tensor_tensor, yg[:, :], yg[:, :], yv[:, :], ALU.mult), a, tv)
                tmp_free[j] = [b]
                th, tl = split(yg[:, :], HH[:, m, :], HL[:, m, :], [b], fence)
                tmp_free[i] = [th, tl]
                hr.append([th, tl])
            x_read[:] = [pe_done[unit[0] - 1]]
            residual(lambda m, r: product(units(3), HH, HL, hr, r), 3)
            ph.close()

        for l in range(2):
            rms(pc["nmix"] + 8 * l)
            mixer(l)
            rms(pc["nffn"] + 8 * l)
            conv_glu(l)
        rms(pc["nfin"], final=True)
        sp(None, outs)
        assert unit[0] == len(plan)

        for q in (pe, act, dve, pool):
            n = 0
            for _, _, t in q.items:
                if t.sem is None and t.used:
                    n += 1
                    t.sem, t.val = sems[q.name], n

        def emit(q, e):
            seen = {}
            mine = sems.get(q.name)
            for what, waits, t in q.items:
                need_ = {}
                for w in waits:
                    k = w.sem.num if hasattr(w.sem, "num") else id(w.sem)
                    if seen.get(k, 0) < w.val:
                        if k not in need_ or need_[k][1] < w.val:
                            need_[k] = (w.sem, w.val)
                for k, (s, v) in need_.items():
                    e.wait_ge(s, v)
                    seen[k] = v
                if what is None:
                    continue
                ins = what[0](*what[1], **what[2])
                if t.sem is not None:
                    ins.then_inc(t.sem, 1 if t.sem is mine else 16)

        block = ctx.enter_context(nc.Block())

        @block.sync
        def _(e):
            emit(sp, e)

        @block.gpsimd
        def _(e):
            emit(pool, e)

        @block.scalar
        def _(e):
            emit(act, e)

        @block.vector
        def _(e):
            emit(dve, e)

        @block.tensor
        def _(e):
            emit(pe, e)


def constants():
    f = np.float32
    c = np.zeros((128, CN), f)
    eye = np.eye(128, dtype=f)
    c[:, CI:CI + 128] = eye
    c[:, CM:CM + 128] = 1.0 / 1024
    c[:, CG:CG + 128] = 1.0 / 128
    c[0:64, CB:CB + 64] = 1.0 / 64
    c[64:128, CB + 64:CB + 128] = 1.0 / 64
    i = np.arange(128)
    c[i, CPA + (i ^ 32)] = 1.0
    c[i, CPR + (i ^ 16)] = 1.0
    c[:, CE] = 1e-5
    c[:, CE + 1] = 1e-6
    s, t = np.meshgrid(i, i, indexing="ij")
    m = np.zeros((128, 8, 128), np.uint8)
    m[:, 0] = s == t
    for lev in range(7):
        b = 1 << lev
        m[:, lev + 1] = (s < t) & (s // (2 * b) == t // (2 * b)) & (s // b != t // b)
    inv = (f(10000.0) ** (-np.arange(0, 64, 2, dtype=f) / f(64))).astype(f)
    ang = np.arange(512, dtype=f)[:, None] * inv[None, :]
    co, si = np.cos(ang).T, np.sin(ang).T
    ta = np.stack([np.concatenate([co] * 4), np.concatenate([-si, si, -si, si])], 1).astype(f)
    th = (f(10000.0) ** (-np.linspace(0.0, 1.0, 16, dtype=f))).astype(f)
    ang = np.arange(T, dtype=f)[:, None] * th[None, :]
    co, si = np.cos(ang).T, np.sin(ang).T
    tr = np.stack([np.concatenate([co] * 8), np.concatenate([-si, si] * 4)], 1).astype(f)
    h = np.arange(4, dtype=np.float64)
    lg = np.log1p(-np.exp2(-5.0 - h))
    rel = np.arange(T)[None, :] - i[:, None]
    d = np.where(rel >= 0, np.exp(lg[:, None, None] * np.maximum(rel, 0)), 0.0) * 32 ** -0.5
    return c, m.reshape(128, 1024).view(np.int32), ta, tr, d.astype(f)


def pack_weights(w):
    plan = unit_plan()
    out = np.zeros((len(plan) // 2, 128, 2048), np.float32)
    for c in range(len(plan) // 2):
        a = 0
        for name, k0, nk, c0, n in plan[2 * c:2 * c + 2]:
            blk = w[name][128 * k0:128 * (k0 + nk), c0:c0 + n].reshape(nk, 128, n).transpose(1, 0, 2)
            out[c, :, a:a + nk * n] = blk.reshape(128, nk * n)
            a += nk * n
    return out


def pack_params(p):
    at, n = param_columns()
    out = np.zeros((128, n), np.float32)

    def put(name, a):
        out[:, at[name]:at[name] + a.shape[1]] = a

    def tiles(a):
        return a.reshape(-1, 128).T

    put("ln_g", tiles(p["ln_g"]))
    put("ln_b", tiles(p["ln_b"]))
    put("subln", tiles(p["a_subln_g"]))
    put("lam", np.broadcast_to(p["a_lambda"].reshape(1, 256), (128, 256)))
    put("nmix", tiles(p["norm_mix_g_2"]))
    put("nffn", tiles(p["norm_ffn_g_2"]))
    put("nfin", tiles(p["final_norm_g_2"]))
    put("lb", tiles(p["hg_lb_logits_2"]))
    put("hgn", tiles(p["hg_norm_g_2"]))
    put("retn", np.concatenate([p["ret_norm_g_2"]] * 2, 1).T)
    put("lcw", tiles(p["lru_conv_w_2"]))
    put("lcb", tiles(p["lru_conv_b_2"]))
    put("gab", tiles(p["lru_gate_a_b_2"]))
    put("gib", tiles(p["lru_gate_i_b_2"]))
    put("lru", tiles(p["lru_lambda_2"]))
    put("fcw", tiles(p["ffn_conv_w_2"]))
    put("fcb", tiles(p["ffn_conv_b_2"]))
    return out


def kernel(**inputs):
    import concourse.bacc as _bacc
    from concourse.bass_utils import run_bass_kernel_spmd as _run

    p = {k: np.asarray(v) for k, v in inputs.items()}
    w = {"a_qkv": p["a_w_qkv"][0], "a_o": p["a_w_o"][0], "kv": p["kv_w"], "b_q": p["b_w_q"][0], "b_o": p["b_w_o"][0]}
    for l in range(2):
        w[f"f_in{l}"], w[f"f_out{l}"] = p["ffn_w_in"][l], p["ffn_w_out"][l]
        w[f"m_in{l}"], w[f"m_out{l}"] = p["w_in_2"][l], p["w_out_2"][l]
        w[f"g_in{l}"], w[f"g_out{l}"] = p["ffn_w_up_2"][l], p["ffn_w_down_2"][l]
    c, masks, ta, tr, dec = constants()
    idx = np.clip(np.arange(512)[None, :] - 384 - np.arange(128)[:, None], -256, 256) + 256
    gates = np.zeros((2, 128, 4, 128), np.float32)
    for l in range(2):
        for a, name in enumerate(("lru_gate_a_w_2", "lru_gate_i_w_2")):
            for b in range(4):
                o = 64 * (b % 2)
                gates[l, o:o + 64, 2 * a + b // 2, o:o + 64] = p[name][l, b]
    arrays = {
        "wts": pack_weights(w),
        "xT": np.ascontiguousarray(p["x"][0].T.reshape(8, 128, 512).transpose(1, 0, 2)),
        "mT": np.ascontiguousarray(p["meta_tokens_2"].T.reshape(8, 128, META).transpose(1, 0, 2)),
        "pp": pack_params(p),
        "cst": c, "cstm": masks, "tA": np.ascontiguousarray(ta), "tR": np.ascontiguousarray(tr), "dech": dec,
        "biasT": np.ascontiguousarray(p["b_rel_bias"][0][:, idx]),
        "gates": gates,
    }
    nc = _bacc.Bacc("TRN2", target_bir_lowering=False, num_devices=1)
    args = [nc.dram_tensor("in_" + k, a.shape, mybir.dt.from_np(a.dtype), kind="ExternalInput").ap()
            for k, a in arrays.items()]
    args.append(nc.dram_tensor("out_0", (128, 8, 512), mybir.dt.float32, kind="ExternalOutput").ap())
    build(nc, *args)
    r = _run(nc, [{"in_" + k: a for k, a in arrays.items()}], core_ids=[0])
    o = r.results[0]["out_0"]
    return np.ascontiguousarray(o.transpose(1, 0, 2).reshape(1024, 512).T)[None]
```
